# Optimizing a Trainium2 kernel written in Bass

```python
import jax, jax.numpy as jnp
from jax import lax
import numpy as np

D_MODEL = 2048
BATCH = 1
SEQ = 256
DEPTH = 1

CHUNK = 64
Q_BLOCK = 128
ROPE_THETA = 500000.0
ROPE_FRACTION = 4
NORM_EPS = 1e-6

ATTN_HEAD_DIM = 128
ATTN_WIDTH = D_MODEL // 2
ATTN_HEADS = ATTN_WIDTH // ATTN_HEAD_DIM
ATTN_KV_HEADS = max(1, ATTN_HEADS // 4)
KV_WIDTH = ATTN_KV_HEADS * ATTN_HEAD_DIM
IDX_HEADS = 8
IDX_HEAD_DIM = 64
TOPK_MAX = 256

RWKV_HEAD_DIM = 64
RWKV_WIDTH = D_MODEL - ATTN_WIDTH
RWKV_HEADS = RWKV_WIDTH // RWKV_HEAD_DIM
DECAY_LORA = 64
ICLR_LORA = 64
GATE_LORA = 64
GN_EPS = 64e-5

MIX_WIDTH = ATTN_WIDTH + RWKV_WIDTH
D_FF = 5632

PROJ_SPLITS = (ATTN_WIDTH, KV_WIDTH, KV_WIDTH,
               IDX_HEADS * IDX_HEAD_DIM, IDX_HEAD_DIM, IDX_HEADS,
               RWKV_WIDTH, RWKV_WIDTH, RWKV_WIDTH,
               DECAY_LORA, ICLR_LORA, GATE_LORA)
PROJ_WIDTH = sum(PROJ_SPLITS)

kernel_name = 'hymba_dsa_rwkv7_macaron_block'

def rms_norm(x, g):
    x32 = x.astype(jnp.float32)
    y = x32 * lax.rsqrt(jnp.mean(x32 * x32, axis=-1, keepdims=True) + NORM_EPS)
    return (y * g.astype(jnp.float32)).astype(x.dtype)

def swiglu(x, w_gate, w_up, w_down):
    return (jax.nn.silu(x @ w_gate) * (x @ w_up)) @ w_down

def rope_partial(x, pos):
    dh = x.shape[-1]
    rot = dh // ROPE_FRACTION
    half = rot // 2
    inv_freq = ROPE_THETA ** (-(jnp.arange(half, dtype=jnp.float32) * 2.0 / rot))
    ang = pos.astype(jnp.float32)[:, None] * inv_freq[None, :]
    cos = jnp.cos(ang)[None, :, None, :]
    sin = jnp.sin(ang)[None, :, None, :]
    x32 = x.astype(jnp.float32)
    x1, x2, rest = x32[..., :half], x32[..., half:rot], x32[..., rot:]
    out = jnp.concatenate([x1 * cos - x2 * sin, x2 * cos + x1 * sin, rest], axis=-1)
    return out.astype(x.dtype)

def split_columns(u):
    idx = [int(v) for v in np.cumsum(PROJ_SPLITS)[:-1]]
    return jnp.split(u, idx, axis=-1)

def dsa_attention(q, k, v, qi, ki, wi):
    B, S = q.shape[0], q.shape[1]
    G, R, Dh = ATTN_KV_HEADS, ATTN_HEADS // ATTN_KV_HEADS, ATTN_HEAD_DIM
    k_sel = min(TOPK_MAX, S // 4)
    nblk = S // Q_BLOCK
    key_chunk = jnp.arange(S) // CHUNK
    idx_scale = (IDX_HEADS ** -0.5) * (IDX_HEAD_DIM ** -0.5)
    att_scale = Dh ** -0.5
    ki32 = ki.astype(jnp.float32)

    def to_blocks(a):
        return jnp.moveaxis(a.reshape((B, nblk, Q_BLOCK) + a.shape[2:]), 1, 0)

    qb = to_blocks(q.reshape(B, S, G, R, Dh))
    qib = to_blocks(qi)
    wib = to_blocks(wi)
    tb = jnp.arange(S).reshape(nblk, Q_BLOCK)

    def block(args):
        q_blk, qi_blk, wi_blk, t_blk = args
        s_idx = jnp.einsum('bqhd,bsd->bqhs', qi_blk.astype(jnp.float32), ki32)
        score = jnp.einsum('bqh,bqhs->bqs', wi_blk.astype(jnp.float32) * idx_scale,
                           jax.nn.relu(s_idx))
        q_chunk = t_blk // CHUNK
        admissible = key_chunk[None, :] <= q_chunk[:, None]
        score = jnp.where(admissible[None], score, -jnp.inf)
        _, sel = lax.top_k(score, k_sel)
        valid = (sel // CHUNK) <= q_chunk[None, :, None]
        k_g = jax.vmap(lambda kb, ib: kb[ib])(k, sel)
        v_g = jax.vmap(lambda vb, ib: vb[ib])(v, sel)
        s = jnp.einsum('bqgrd,bqngd->bqgrn', q_blk.astype(jnp.float32),
                       k_g.astype(jnp.float32)) * att_scale
        s = jnp.where(valid[:, :, None, None, :], s, -jnp.inf)
        p = jax.nn.softmax(s, axis=-1)
        o = jnp.einsum('bqgrn,bqngd->bqgrd', p, v_g.astype(jnp.float32))
        return o.astype(q.dtype)

    out = lax.map(block, (qb, qib, wib, tb))
    return jnp.moveaxis(out, 0, 1).reshape(B, S, ATTN_WIDTH)

def token_shift_lerp(p, mu):
    prev = jnp.pad(p, ((0, 0), (1, 0), (0, 0)))[:, :-1]
    return p + (prev - p) * mu

def rwkv7_time_mix(r_p, k_p, v_p, wd_p, ad_p, gd_p, mu_r, mu_k, mu_v, mu_w, mu_a, mu_g,
                   w0, w2, a0, a2, g2, k_k, k_a, r_k, gn_gain, gn_bias):
    B, S = r_p.shape[0], r_p.shape[1]
    H, N = RWKV_HEADS, RWKV_HEAD_DIM
    dt = r_p.dtype
    r = token_shift_lerp(r_p, mu_r)
    k = token_shift_lerp(k_p, mu_k)
    v = token_shift_lerp(v_p, mu_v)
    xw = token_shift_lerp(wd_p, mu_w)
    xa = token_shift_lerp(ad_p, mu_a)
    xg = token_shift_lerp(gd_p, mu_g)

    w = -jax.nn.softplus(-(w0 + jnp.tanh(xw) @ w2)) - 0.5
    decay = jnp.exp(-jnp.exp(w.astype(jnp.float32)))
    a = jax.nn.sigmoid((a0 + xa @ a2).astype(jnp.float32))
    g = jax.nn.sigmoid(xg) @ g2

    hd = lambda t: t.reshape(B, S, H, N).astype(jnp.float32)
    r, k, v, a, decay = hd(r), hd(k), hd(v), hd(a), hd(decay)
    kk = k * k_k.reshape(H, N).astype(jnp.float32)
    kk = kk / jnp.maximum(jnp.sqrt(jnp.sum(kk * kk, axis=-1, keepdims=True)), 1e-12)
    k = k * (1.0 + (a - 1.0) * k_a.reshape(H, N).astype(jnp.float32))

    def step(state, xs):
        r_t, w_t, k_t, v_t, a_t, b_t = xs
        sa = jnp.einsum('bhvk,bhk->bhv', state, a_t)
        state = (state * w_t[:, :, None, :] + sa[..., None] * b_t[:, :, None, :]
                 + v_t[..., None] * k_t[:, :, None, :])
        y_t = jnp.einsum('bhvk,bhk->bhv', state, r_t)
        return state, y_t

    tf = lambda t: jnp.moveaxis(t, 1, 0)
    state0 = jnp.zeros((B, H, N, N), jnp.float32)
    _, y = lax.scan(step, state0, (tf(r), tf(decay), tf(k), tf(v), tf(-kk), tf(kk * a)))
    y = jnp.moveaxis(y, 0, 1)

    mean = jnp.mean(y, axis=-1, keepdims=True)
    var = jnp.mean(jnp.square(y - mean), axis=-1, keepdims=True)
    y = ((y - mean) * lax.rsqrt(var + GN_EPS)).reshape(B, S, RWKV_WIDTH)
    y = y * gn_gain.astype(jnp.float32) + gn_bias.astype(jnp.float32)
    bonus = jnp.sum(r * k * r_k.astype(jnp.float32), axis=-1, keepdims=True) * v
    y = y + bonus.reshape(B, S, RWKV_WIDTH)
    return (y * g.astype(jnp.float32)).astype(dt)

def setup_inputs(seed: int = 0) -> dict:
    key = jax.random.key(seed)
    ks = iter(jax.random.split(key, 40))
    L, D, F = DEPTH, D_MODEL, D_FF
    nrm = lambda shape, scale: jax.random.normal(next(ks), shape, jnp.float32) * scale
    gain = lambda shape: 1.0 + nrm(shape, 0.02)
    unif = lambda shape, lo, hi: jax.random.uniform(next(ks), shape, jnp.float32, lo, hi)
    return {
        'x': nrm((BATCH, SEQ, D), 1.0),
        'ffn1_norm': gain((L, D)),
        'ffn1_w_gate': nrm((L, D, F), D ** -0.5),
        'ffn1_w_up': nrm((L, D, F), D ** -0.5),
        'ffn1_w_down': nrm((L, F, D), F ** -0.5),
        'mix_norm': gain((L, D)),
        'w_in': nrm((L, D, PROJ_WIDTH), D ** -0.5),
        'w_out': nrm((L, MIX_WIDTH, D), MIX_WIDTH ** -0.5),
        'rwkv_mu_r': unif((L, RWKV_WIDTH), 0.0, 1.0),
        'rwkv_mu_k': unif((L, RWKV_WIDTH), 0.0, 1.0),
        'rwkv_mu_v': unif((L, RWKV_WIDTH), 0.0, 1.0),
        'rwkv_mu_w': unif((L, DECAY_LORA), 0.0, 1.0),
        'rwkv_mu_a': unif((L, ICLR_LORA), 0.0, 1.0),
        'rwkv_mu_g': unif((L, GATE_LORA), 0.0, 1.0),
        'rwkv_w0': unif((L, RWKV_WIDTH), -6.5, -1.5),
        'rwkv_w2': nrm((L, DECAY_LORA, RWKV_WIDTH), 0.1 * DECAY_LORA ** -0.5),
        'rwkv_a0': nrm((L, RWKV_WIDTH), 0.1),
        'rwkv_a2': nrm((L, ICLR_LORA, RWKV_WIDTH), 0.1 * ICLR_LORA ** -0.5),
        'rwkv_g2': nrm((L, GATE_LORA, RWKV_WIDTH), GATE_LORA ** -0.5),
        'rwkv_k_k': 0.85 + nrm((L, RWKV_WIDTH), 0.02),
        'rwkv_k_a': gain((L, RWKV_WIDTH)),
        'rwkv_r_k': nrm((L, RWKV_HEADS, RWKV_HEAD_DIM), 0.1),
        'rwkv_gn_gain': gain((L, RWKV_WIDTH)),
        'rwkv_gn_bias': nrm((L, RWKV_WIDTH), 0.02),
        'ffn2_norm': gain((L, D)),
        'ffn2_w_gate': nrm((L, D, F), D ** -0.5),
        'ffn2_w_up': nrm((L, D, F), D ** -0.5),
        'ffn2_w_down': nrm((L, F, D), F ** -0.5),
        'final_norm': gain((D,)),
    }

def reference(x, ffn1_norm, ffn1_w_gate, ffn1_w_up, ffn1_w_down, mix_norm, w_in, w_out,
              rwkv_mu_r, rwkv_mu_k, rwkv_mu_v, rwkv_mu_w, rwkv_mu_a, rwkv_mu_g,
              rwkv_w0, rwkv_w2, rwkv_a0, rwkv_a2, rwkv_g2, rwkv_k_k, rwkv_k_a, rwkv_r_k,
              rwkv_gn_gain, rwkv_gn_bias, ffn2_norm, ffn2_w_gate, ffn2_w_up, ffn2_w_down,
              final_norm):
    B, S, _ = x.shape
    pos = jnp.arange(S)
    h = x
    for l in range(DEPTH):
        h = h + 0.5 * swiglu(rms_norm(h, ffn1_norm[l]), ffn1_w_gate[l], ffn1_w_up[l], ffn1_w_down[l])

        u = rms_norm(h, mix_norm[l]) @ w_in[l]
        q, k, v, qi, ki, wi, rr, rk, rv, wd, ad, gd = split_columns(u)

        q = rope_partial(q.reshape(B, S, ATTN_HEADS, ATTN_HEAD_DIM), pos)
        k = rope_partial(k.reshape(B, S, ATTN_KV_HEADS, ATTN_HEAD_DIM), pos)
        v = v.reshape(B, S, ATTN_KV_HEADS, ATTN_HEAD_DIM)
        qi = rope_partial(qi.reshape(B, S, IDX_HEADS, IDX_HEAD_DIM), pos)
        ki = rope_partial(ki.reshape(B, S, 1, IDX_HEAD_DIM), pos)[:, :, 0]
        attn_out = dsa_attention(q, k, v, qi, ki, wi)

        rwkv_out = rwkv7_time_mix(rr, rk, rv, wd, ad, gd,
                                  rwkv_mu_r[l], rwkv_mu_k[l], rwkv_mu_v[l],
                                  rwkv_mu_w[l], rwkv_mu_a[l], rwkv_mu_g[l],
                                  rwkv_w0[l], rwkv_w2[l], rwkv_a0[l], rwkv_a2[l], rwkv_g2[l],
                                  rwkv_k_k[l], rwkv_k_a[l], rwkv_r_k[l],
                                  rwkv_gn_gain[l], rwkv_gn_bias[l])

        h = h + jnp.concatenate([attn_out, rwkv_out], axis=-1) @ w_out[l]

        h = h + 0.5 * swiglu(rms_norm(h, ffn2_norm[l]), ffn2_w_gate[l], ffn2_w_up[l], ffn2_w_down[l])
    return rms_norm(h, final_norm)


_drawn_inputs = setup_inputs


def setup_inputs(seed=0):
    import zlib

    import numpy as np

    out = dict(_drawn_inputs(seed))
    spreads = {}
    factors = {'ffn1_norm': 3.605,
     'rwkv_mu_w': 30.126,
     'rwkv_mu_a': 8.0,
     'rwkv_w2': 8.0,
     'rwkv_a0': 3.741,
     'rwkv_a2': 3.377,
     'rwkv_k_k': 35.358,
     'rwkv_k_a': 7.746,
     'rwkv_gn_gain': 30.077,
     'rwkv_gn_bias': 31.214,
     'ffn2_norm': 7.645,
     'final_norm': 7.469}
    for name, (base, spread) in spreads.items():
        noise = np.random.default_rng([zlib.crc32(name.encode()), seed]).standard_normal(out[name].shape)
        drawn = base * np.exp(spread * noise) if base else spread * noise
        out[name] = __import__('jax').numpy.asarray(drawn.astype(out[name].dtype))
    for name, factor in factors.items():
        out[name] = (out[name] * factor).astype(out[name].dtype)
    return out
```

```python
from contextlib import ExitStack

import numpy as np

import concourse.bass as bass
from concourse import mybir

F32 = mybir.dt.float32
F32R = mybir.dt.float32r
ALU = mybir.AluOpType
ACT = mybir.ActivationFunctionType
AX = mybir.AxisListType

P = 128
D = 2048
S = 256
TB = S // P
F = 5632
COLS = 512
KD = D // P
KF = F // P
NORM_EPS = 1e-6
AW = 1024
RW = 1024
NT = RW // P

SLOTS = 4
KT = 2
GD = KD // KT
GF = KF // KT
FC = F // COLS
DC = D // COLS

MIX_GROUPS = 11 * GD + DC * GD
AH = 8
KVW = 256
ATT_SCALE = float(P) ** -0.5
IDX_HEADS = 8
IDX_SCALE = (IDX_HEADS ** -0.5) * (64 ** -0.5)
TOPK = 64
TAKEN = -float(2.0 ** 127)
HIDDEN = -float(2.0 ** 126)
OFF = -1e30
RH = 16
C = 64
NCHUNK = S // C
GN_EPS = 64e-5
DECAY = float(np.exp(-0.5))


CONST_WIDTH = 2816


def constants():
    t = np.zeros((P, CONST_WIDTH), np.float32)
    p = np.arange(P)
    s = np.arange(S)
    t[:, 0:128] = np.eye(P)
    t[:, 128:256] = p[:, None] // 64 == p[None, :] // 64
    head = 2 * np.arange(NT)[:, None] + (p // 64)[None, :]
    t[:, 256:384] = (head.T[:, :, None] == np.arange(RH)).reshape(P, NT * RH)
    t[:, 384:448] = np.arange(C)[None, :] > (p % 64)[:, None]
    t[:, 448:512] = np.arange(C)[None, :] >= (p % 64)[:, None]
    t[:, 512:768] = s[None, :] % C != 0

    def rotary(width, rows_, at):
        rot = width // 4
        half = rot // 2
        freq = np.float32(500000.0) ** (-(np.arange(half, dtype=np.float32) * np.float32(2.0) / np.float32(rot)))
        ang = s.astype(np.float32)[:, None] * freq[None, :].astype(np.float32)
        cos, sin = np.cos(ang).astype(np.float32).T, np.sin(ang).astype(np.float32).T
        for q in range(rows_):
            j = q % width
            t[q, at:at + S] = cos[j % half] if j < rot else 1.0
            if j < rot:
                t[q, at + S:at + 2 * S] = -sin[j] if j < half else sin[j - half]

    rotary(64, P, 768)
    rotary(P, 32, 1280)
    t[0:RH, 1792:2816] = (head[None, :, :] == np.arange(RH)[:, None, None]).reshape(RH, NT * P)
    return t


def build(nc, a, out):
    with ExitStack() as ctx:
        address = {}

        def sb(name, shape, dt=F32):
            handle = ctx.enter_context(nc.sbuf_tensor(name, shape, dt))
            address[name] = nc.sbuf_base - 4 * int(np.prod(shape[1:]))
            return handle

        def pb(name, shape):
            return ctx.enter_context(nc.psum_tensor(name, shape, F32))

        def sem(name):
            return ctx.enter_context(nc.semaphore(name))

        x = sb("x", [P, TB, D])
        raw = sb("raw", [P, SLOTS, KT, COLS])
        whi = sb("whi", [P, SLOTS, KT, COLS], F32R)
        wlo = sb("wlo", [P, SLOTS, KT, COLS], F32R)
        xh = sb("xh", [P, KD, S], F32R)
        xl = sb("xl", [P, KD, S], F32R)
        consts = sb("consts", [P, CONST_WIDTH])
        ident = consts[:, 0:128]
        same_head = consts[:, 128:256]
        to_heads = consts[:, 256:384].rearrange("p (t h) -> p t h", h=RH)
        mask2 = consts[:, 384:512]
        keep = consts[:, 512:768]
        cos_i, sin_i = consts[:, 768:1024], consts[:, 1024:1280]
        cos_q, sin_q = consts[0:32, 1280:1536], consts[0:32, 1536:1792]
        to_channels = consts[:, 1792:2816].rearrange("p (t c) -> p t c", c=P)
        prow = sb("prow", [P, P])
        pcol = sb("pcol", [P, P])
        prow2 = sb("prow2", [2, P])
        pcol2 = sb("pcol2", [P, 2])
        ss = sb("ss", [P, 8])
        stage = sb("stage", [P, 2, TB, COLS])
        silu, act = stage[:, 0], stage[:, 1]
        fgain = stage[:, :, :, :].rearrange("p a b c -> p (a b c)")
        UNIT = NT * S * 4
        arena = sb("arena", [P, 11 * UNIT // 4])

        def at(name, shape, where, unit=0, plus=0, dt=F32):
            return nc.alloc_sbuf_tensor_at(name, shape, dt, offset=address[where.name] + unit * UNIT + plus)

        KB = 1024
        xs = at("xs", [P, TB, D], arena)
        hh = at("hh", [P, KF, S], arena, dt=F32R)
        hl = at("hl", [P, KF, S], arena, plus=KF * S * 4, dt=F32R)
        rkv = at("rkv", [P, 3 * NT, S], arena, 0)
        qk = at("qk", [P, 10, S], arena, plus=61 * KB)
        vals = at("vals", [P, TB, S], arena, plus=71 * KB)
        qi = at("qi", [P, 5, S], arena, plus=73 * KB)
        lora_in = at("lora_in", [P, 2, S], arena, plus=78 * KB)
        lora_w = at("lora_w", [P, RW], arena, plus=80 * KB)
        lora_g = at("lora_g", [P, RW], arena, plus=84 * KB)
        widx = sb("widx", [P, TB, IDX_HEADS])
        swap = at("swap", [P, 10, S], wlo)
        relu = at("relu", [P, IDX_HEADS, S], whi, 0)
        att = at("att", [P, AH, S], whi, 1)
        prob_t = at("prob_t", [P, TB, AH, P], wlo, 0)
        score = at("score", [P, TB, S], stage)
        top8 = at("top8", [P, 8], stage, plus=2 * KB)
        top = at("top", [P, 3 * AH], stage, plus=2 * KB + 64)
        r, k, v = (at(n, [P, NT, S], arena, 3 + i) for i, n in enumerate(("r", "k", "v")))
        ksq = at("ksq", [P, NT, S], arena, 6)
        sw = at("sw", [P, NT, S], arena, 0)
        lsum = at("lsum", [P, NT, S], arena, 1)
        pdec = at("pdec", [P, NT, S], arena, 2)
        pinv = at("pinv", [P, NT, S], arena, 0)
        iclr = at("iclr", [P, NT, S], wlo, 0)
        kk = at("kk", [P, NT, S], wlo, 1)
        ar = at("ar", [P, 2, NT, S], whi)
        gate = at("gate", [P, NT, S], xh, 1)
        bonus = at("bonus", [P, NT, S], xl, 1)
        lora = at("lora", [P, 2, S], stage)
        hstat = at("hstat", [P, 3, S], stage, plus=4 * KB)
        ka1 = sb("ka1", [P, NT])
        pend = sb("pend", [P, NT * NCHUNK, 1])
        v_tok = at("v_tok", [P, TB, RW], arena, 7)
        a_tok = at("a_tok", [P, TB, RW], wlo, 1)
        b_tok = at("b_tok", [P, TB, RW], arena, 5)
        k_tok = at("k_tok", [P, TB, RW], arena, 6)
        bx = at("bx", [P, 2 * RH, 2, C], arena, 0)
        kx = at("kx", [P, 2 * RH, 2, C], arena, 2)
        tt_all = at("tt_all", [P, 2 * RH, C], arena, 10)
        nsys = at("nsys", [P, 1024], arena, 8)
        tinv = at("tinv", [P, 1024], arena, 8, 4 * KB)
        subst = at("subst", [P, 1024], arena, 9)
        t_plain = at("t_plain", [P, 2 * RH, 32], arena, 9, 4 * KB)
        xm = at("xm", [P, 2 * RH, 32], arena, 4)
        sa = at("sa", [P, RW], arena, 4, 4 * KB)
        akv = at("akv", [P, TB, RW], wlo, 0)
        sa0 = at("sa0", [P, TB, RW], stage)
        gt = at("gt", [P, TB, RW], arena, 8)
        state = at("state", [P, NT, C], arena, 9)
        sdec = at("sdec", [P, NT, C], arena, 9, 2 * KB)
        y = at("y", [P, NT, S], wlo, 1)
        ysq = at("ysq", [P, NT, S], arena, 0)
        n_dram = nc.dram_tensor("n_dram", [4, 2 * RH, 32, 32], F32, kind="Internal").ap()
        t_dram = nc.dram_tensor("t_dram", [2, 4, 2 * RH, 32, 32], F32, kind="Internal").ap()

        psA = pb("psA", [P, TB, COLS])
        psB = pb("psB", [P, TB, COLS])
        psT = pb("psT", [P, 2 * COLS])
        psM = pb("psM", [P, 2 * COLS])
        pA, pB = (ps[:, :, :].rearrange("p b c -> p (b c)") for ps in (psA, psB))
        pT, pM = psT[:, :], psM[:, :]

        PER = 2 * GD
        m0 = FC * PER + DC * GF
        raw_landed = [sem(f"raw_landed{i}") for i in range(SLOTS)]
        hi_ready = sem("hi_ready")
        lo_ready = sem("lo_ready")
        group_used = sem("group_used")
        const_landed = sem("const_landed")
        params_turned = sem("params_turned")
        params_ready = sem("params_ready")
        x_landed = sem("x_landed")
        square_ready = sem("square_ready")
        norm_step = sem("norm_step")
        root_ready = sem("root_ready")
        xs_ready = sem("xs_ready")
        xs_turned = sem("xs_turned")
        xh_ready = sem("xh_ready")
        xl_ready = sem("xl_ready")
        silu_ready = sem("silu_ready")
        act_ready = sem("act_ready")
        act_turned = sem("act_turned")
        hh_ready = sem("hh_ready")
        hl_ready = sem("hl_ready")
        x_added = sem("x_added")
        gain_landed = sem("gain_landed")
        out_ready = sem("out_ready")
        out_stored = sem("out_stored")
        in_read = sem("in_read")
        lora_landed = sem("lora_landed")
        round_full = sem("round_full")
        round_read = [sem(f"round_read{i}") for i in range(4)]
        sys_stored = sem("sys_stored")
        sys_landed = sem("sys_landed")
        inv_stored = sem("inv_stored")
        inv_landed = sem("inv_landed")
        multiplied = sem("multiplied")
        substituted = sem("substituted")

        def load_group(sp, src, base, n, per, j, ncol=COLS):
            g = base + j
            slot = g % SLOTS
            if not (isinstance(n, int) and g + n * per < SLOTS):
                sp.wait_ge(hi_ready, n * per + g - SLOTS + 1)
                sp.wait_ge(lo_ready, n * per + g - SLOTS + 1)
            sp.dma_start(raw[:, slot, :, 0:ncol], src).then_inc(raw_landed[slot], 16)

        def split_hi(base, n, per, j, ncol=COLS):
            g = base + j
            slot = g % SLOTS
            extra = 48 * min(max(g // SLOTS + 1 - m0 // SLOTS, 0), GD // SLOTS)
            nc.scalar.wait_ge(raw_landed[slot], n * (16 * per // SLOTS) + 16 * (g // SLOTS + 1) + extra)
            if not (isinstance(n, int) and g + n * per < SLOTS):
                nc.scalar.wait_ge(group_used, n * per + g - SLOTS + 1)
            nc.scalar.copy(whi[:, slot, :, 0:ncol], raw[:, slot, :, 0:ncol]).then_inc(hi_ready, 1)

        def split_lo(base, n, per, j, ncol=COLS):
            g = base + j
            slot = g % SLOTS
            nc.vector.wait_ge(hi_ready, n * per + g + 1)
            if not (isinstance(n, int) and g + n * per < SLOTS):
                nc.vector.wait_ge(group_used, n * per + g - SLOTS + 1)
            nc.vector.tensor_tensor(wlo[:, slot, :, 0:ncol], raw[:, slot, :, 0:ncol],
                                    whi[:, slot, :, 0:ncol].bitcast(F32), ALU.subtract).then_inc(lo_ready, 1)

        def wait_group(base, n, per, j):
            nc.tensor.wait_ge(lo_ready, n * per + base + j + 1)

        def project_tokens(ps, h, l, base, n, per, j, k0, first, last, ncol=COLS):
            wait_group(base, n, per, j)
            slot = (base + j) % SLOTS
            for t in range(KT):
                for tb in range(TB):
                    tok = slice(tb * P, tb * P + P)
                    for p, (lhs, rhs) in enumerate(((h, whi), (h, wlo), (l, whi))):
                        mm = nc.tensor.matmul(ps[:, tb, 0:ncol], lhs[:, k0 + t, tok], rhs[:, slot, t, 0:ncol],
                                              start=(first and t == 0 and p == 0),
                                              stop=(last and t == KT - 1 and p == 2))
            mm.then_inc(group_used, 1)

        def rows(w, k0):
            return w[k0 * P:(k0 + KT) * P, :].rearrange("(t p) n -> p t n", p=P)

        def norm_act(f):
            if f == 0:
                nc.scalar.wait_ge(x_landed, 16)
            else:
                nc.scalar.wait_ge(x_added, DC * f)
            nc.scalar.activation(xs[:, 0, :], x[:, 0, :], ACT.Square, accum_out=ss[:, 0:1]).then_inc(square_ready, 1)
            nc.scalar.wait_ge(norm_step, 2 * f + 1)
            nc.scalar.activation(ss[:, 4:6], ss[:, 2:4], ACT.Sqrt).then_inc(root_ready, 1)

        def norm_dve(f):
            if f == 0:
                nc.vector.wait_ge(x_landed, 16)
            else:
                nc.vector.wait_ge(x_added, DC * f)
            nc.vector.tensor_tensor_reduce(xs[:, 1, :], x[:, 1, :], x[:, 1, :], 1.0, 0.0, ALU.mult, ALU.add,
                                           ss[:, 1:2]).then_inc(square_ready, 1)
            nc.vector.wait_ge(square_ready, 2 * (f + 1))
            nc.vector.tensor_scalar(ss[:, 2:4], ss[:, 0:2], 1.0 / D, NORM_EPS, ALU.mult, ALU.add)\
                .then_inc(norm_step, 1)
            nc.vector.wait_ge(root_ready, f + 1)
            nc.vector.reciprocal(ss[:, 6:8], ss[:, 4:6]).then_inc(norm_step, 1)
            nc.vector.wait_ge(norm_step, 2 * f + 2)
            for tb in range(TB):
                nc.vector.tensor_scalar(xs[:, tb, :], x[:, tb, :], ss[:, 6 + tb:7 + tb], None, ALU.mult)\
                    .then_inc(xs_ready, 1)

        QK = 4

        def turn_norm(f):
            for q in range(KD // QK):
                nc.tensor.wait_ge(xs_ready, TB * (f + 1))
                if q >= 2 or f:
                    nc.tensor.wait_ge(xl_ready, (KD // QK) * f + max(q - 1, 0))
                ps = (psT, psM)[q % 2]
                for t in range(QK):
                    for tb in range(TB):
                        k = q * QK + t
                        mm = nc.tensor.transpose(ps[:, t * S + tb * P:t * S + tb * P + P],
                                                 xs[:, tb, k * P:k * P + P], ident)
                mm.then_inc(xs_turned, 1)

        def norm_hi(f):
            for q in range(KD // QK):
                nc.scalar.wait_ge(xs_turned, (KD // QK) * f + q + 1)
                if q == 0:
                    nc.scalar.wait_ge(params_ready, 1)
                ps = (psT, psM)[q % 2]
                for t in range(QK):
                    k = q * QK + t
                    g = f * KD + k
                    mm = nc.scalar.activation(xh[:, k, :], ps[:, t * S:t * S + S], ACT.Copy, scale=pcol[:, g:g + 1])
                mm.then_inc(xh_ready, 1)

        def norm_lo(f):
            for q in range(KD // QK):
                nc.vector.wait_ge(xh_ready, (KD // QK) * f + q + 1)
                ps = (psT, psM)[q % 2]
                for t in range(QK):
                    k = q * QK + t
                    g = f * KD + k
                    mm = nc.vector.scalar_tensor_tensor(xl[:, k, :], ps[:, t * S:t * S + S], pcol[:, g:g + 1],
                                                        xh[:, k, :].bitcast(F32), ALU.mult, ALU.subtract)
                mm.then_inc(xl_ready, 1)

        PER = 2 * GD

        def ffn_load(sp, f, base, w_gate, w_up, w_down):
            def chunk(n):
                col = n * COLS
                for j in range(GD):
                    load_group(sp, rows(w_gate, j * KT)[:, :, bass.ds(col, COLS)], base, n, PER, j)
                for j in range(GD):
                    load_group(sp, rows(w_up, j * KT)[:, :, bass.ds(col, COLS)], base, n, PER, GD + j)
            chunk(0)
            with sp.Fori(1, FC) as n:
                chunk(n)
            down = base + FC * PER
            with sp.Fori(0, DC // 2) as m:
                for j in range(2 * GF):
                    col = (2 * m + j // GF) * COLS
                    load_group(sp, rows(w_down, (j % GF) * KT)[:, :, bass.ds(col, COLS)], down, m, 2 * GF, j)

        def ffn_act(f, base):
            def silu_gate(n):
                nc.scalar.wait_ge(group_used, n * PER + (base + GD))
                if not (isinstance(n, int) and n == 0 and f == 0):
                    nc.scalar.wait_ge(act_ready, n + f * FC)
                nc.scalar.activation(silu[:, :, :], psA[:, :, :], ACT.Silu).then_inc(silu_ready, 1)

            def turned_hi(n):
                nc.scalar.wait_ge(act_turned, n + (f * FC + 1))
                nc.scalar.copy(hh[:, bass.ds(n * 4, 4), :], psT[:, :].rearrange("p (t s) -> p t s", t=4))\
                    .then_inc(hh_ready, 1)

            def chunk(n, first):
                for j in range(PER):
                    if not (first and j < SLOTS):
                        split_hi(base, n, PER, j)
                    if j == GD + SLOTS - 1:
                        if not first:
                            turned_hi(n - 1)
                        silu_gate(n)
            chunk(0, True)
            chunk(1, False)
            with nc.scalar.Fori(2, FC) as n:
                chunk(n, False)
            down = base + FC * PER
            for j in range(SLOTS):
                split_hi(down, 0, 2 * GF, j)
            turned_hi(FC - 1)
            for j in range(SLOTS, 2 * GF):
                split_hi(down, 0, 2 * GF, j)
            for j in range(2 * GF):
                split_hi(down, 1, 2 * GF, j)

        def ffn_dve(f, base):
            def gate_up(n):
                nc.vector.wait_ge(silu_ready, n + (f * FC + 1))
                nc.vector.wait_ge(group_used, n * PER + (base + PER))
                if not (isinstance(n, int) and n == 0 and f == 0):
                    nc.vector.wait_ge(act_turned, n + f * FC)
                nc.vector.tensor_tensor(act[:, :, :], psB[:, :, :], silu[:, :, :], ALU.mult).then_inc(act_ready, 1)

            def turned_lo(n):
                nc.vector.wait_ge(hh_ready, n + (f * FC + 1))
                nc.vector.tensor_tensor(hl[:, bass.ds(n * 4, 4), :], psT[:, :].rearrange("p (t s) -> p t s", t=4),
                                        hh[:, bass.ds(n * 4, 4), :].bitcast(F32), ALU.subtract)\
                    .then_inc(hl_ready, 1)

            def chunk(n, first):
                for j in range(PER):
                    if not (first and j < SLOTS):
                        split_lo(base, n, PER, j)
                    if j == SLOTS - 1 and not first:
                        gate_up(n - 1)
                    if j == GD + SLOTS - 1 and not first:
                        turned_lo(n - 1)
            chunk(0, True)
            chunk(1, False)
            with nc.vector.Fori(2, FC) as n:
                chunk(n, False)
            down = base + FC * PER
            for j in range(SLOTS):
                split_lo(down, 0, 2 * GF, j)
            gate_up(FC - 1)
            turned_lo(FC - 1)
            for c in range(DC):
                for j in range(GF):
                    if c or j >= SLOTS:
                        split_lo(down, 0, 0, c * GF + j)
                    if c and j == SLOTS - 1:
                        add_down(f, down, c - 1)
            add_down(f, down, DC - 1)

        def add_down(f, down, c):
            nc.vector.wait_ge(group_used, down + (c + 1) * GF)
            ps = (psA, psB)[c % 2]
            nc.vector.scalar_tensor_tensor(x[:, :, c * COLS:(c + 1) * COLS], ps[:, :, :], 0.5,
                                           x[:, :, c * COLS:(c + 1) * COLS], ALU.mult, ALU.add)\
                .then_inc(x_added, 1)

        def ffn_pe(f, base):
            def turn(n):
                nc.tensor.wait_ge(act_ready, n + (f * FC + 1))
                if not (isinstance(n, int) and n == 0 and f == 0):
                    nc.tensor.wait_ge(hl_ready, n + f * FC)
                for t in range(4):
                    for tb in range(TB):
                        mm = nc.tensor.transpose(psT[:, t * S + tb * P:t * S + tb * P + P],
                                                 act[:, tb, t * P:t * P + P], ident)
                mm.then_inc(act_turned, 1)

            def chunk(n, first):
                if not first:
                    nc.tensor.wait_ge(silu_ready, n + f * FC)
                for j in range(GD):
                    if first and j % 2 == 0:
                        nc.tensor.wait_ge(xl_ready, 4 * (2 * f) + j // 2 + 1)
                    project_tokens(psA, xh, xl, base, n, PER, j, j * KT, j == 0, j == GD - 1)
                if not first:
                    turn(n - 1)
                for j in range(GD):
                    project_tokens(psB, xh, xl, base, n, PER, GD + j, j * KT, j == 0, j == GD - 1)
            chunk(0, True)
            chunk(1, False)
            with nc.tensor.Fori(2, FC) as n:
                chunk(n, False)
            turn(FC - 1)
            down = base + FC * PER
            for c in range(DC):
                if c == 0:
                    nc.tensor.wait_ge(hl_ready, (f + 1) * FC)
                if c >= 2:
                    nc.tensor.wait_ge(x_added, added_before_down[f] + c - 1)
                for j in range(GF):
                    project_tokens((psA, psB)[c % 2], hh, hl, down, 0, 0, c * GF + j, j * KT,
                                   j == 0, j == GF - 1)

        FFN_GROUPS = FC * PER + DC * GF
        ki_col, wi_col, rkv_col = 2048, 2112, 2120
        lora_col = rkv_col + 3 * RW
        KI2, LORA, WI = 0, P, P + 192
        SMALL = WI + IDX_HEADS
        NCH = 11
        in_col = [None] + [rkv_col + i * COLS for i in range(6)] + [AW, AW + 2 * KVW, 0, COLS]
        m0 = FFN_GROUPS
        w0_out = m0 + NCH * GD

        def in_rows(k0, lo, hi):
            return rows(a["w_in"], k0)[:, :, lo:hi]

        def mix_load(sp):
            for j in range(GD):
                g = m0 + j
                slot = g % SLOTS
                sp.wait_ge(hi_ready, g - SLOTS + 1)
                sp.wait_ge(lo_ready, g - SLOTS + 1)
                for at, lo, hi in ((KI2, ki_col, wi_col), (KI2 + 64, ki_col, wi_col),
                                   (LORA, lora_col, lora_col + 192), (WI, wi_col, rkv_col)):
                    sp.dma_start(raw[:, slot, :, at:at + hi - lo], in_rows(j * KT, lo, hi))\
                        .then_inc(raw_landed[slot], 16)
            for c in range(1, NCH):
                for j in range(GD):
                    load_group(sp, in_rows(j * KT, in_col[c], in_col[c] + COLS), m0 + c * GD, 0, 0, j)
            sp.wait_ge(x_added, DC)
            sp.dma_start(lora_w[0:64, :], a["rwkv_w2"]).then_inc(lora_landed, 16)
            sp.dma_start(lora_w[64:P, :], a["rwkv_a2"]).then_inc(lora_landed, 16)
            sp.dma_start(lora_g[0:64, :], a["rwkv_g2"]).then_inc(lora_landed, 16)

        def out_load(sp, g0, g1):
            for g in range(g0, g1):
                c, j = g // GD, g % GD
                load_group(sp, rows(a["w_out"], j * KT)[:, :, c * COLS:(c + 1) * COLS], w0_out, 0, 0, g)

        def project_channels(ps, cts, base, n, per, j, k0, first, last):
            slot = (base + j) % SLOTS
            for i, ct in enumerate(cts):
                for t in range(KT):
                    for p, (w, h) in enumerate(((whi, xh), (wlo, xh), (whi, xl))):
                        mm = nc.tensor.matmul(ps[:, i * S:(i + 1) * S], w[:, slot, t, ct * P:(ct + 1) * P],
                                              h[:, k0 + t, :], start=(first and t == 0 and p == 0 and i % 2 == 0),
                                              stop=(last and t == KT - 1 and p == 2), skip_group_check=True)
            return mm

        def project_small_tokens(ps, at, step, col, width, base, j, k0, first, last):
            slot = (base + j) % SLOTS
            for t in range(KT):
                for tb in range(TB):
                    tok = slice(tb * P, tb * P + P)
                    for p, (h, w) in enumerate(((xh, whi), (xh, wlo), (xl, whi))):
                        mm = nc.tensor.matmul(ps[:, at + tb * step:at + tb * step + width], h[:, k0 + t, tok],
                                              w[:, slot, t, col:col + width],
                                              start=(first and t == 0 and p == 0 and tb == 0),
                                              stop=(last and t == KT - 1 and p == 2), skip_group_check=True)
            return mm

        def win_pe():
            for j in range(GD):
                if j % 2 == 0:
                    nc.tensor.wait_ge(xl_ready, 4 + j // 2 + 1)
                wait_group(m0, 0, 0, j)
                project_small_tokens(pA, 2 * S, IDX_HEADS, WI, IDX_HEADS, m0, j, j * KT, j == 0, j == GD - 1)
                slot = (m0 + j) % SLOTS
                for t in range(KT):
                    for p, (w, h) in enumerate(((whi, xh), (wlo, xh), (whi, xl))):
                        nc.tensor.matmul(pA[0:64, 3 * S:4 * S], w[:, slot, t, LORA + P:LORA + 192],
                                         h[:, j * KT + t, :], start=False,
                                         stop=(j == GD - 1 and t == KT - 1 and p == 2), skip_group_check=True)
                project_channels(pA, (0, 1), m0, 0, 0, j, j * KT, j == 0, j == GD - 1).then_inc(group_used, 1)
            for c in range(1, NCH):
                if c >= 2:
                    nc.tensor.wait_ge(in_read, c - 1)
                base = m0 + c * GD
                for j in range(GD):
                    wait_group(base, 0, 0, j)
                    if c == 7:
                        project_small_tokens(pB, 2 * S, S, 2 * P, 2 * P, base, j, j * KT, j == 0, j == GD - 1)
                        mm = project_channels(pB, (0, 1), base, 0, 0, j, j * KT, j == 0, j == GD - 1)
                    else:
                        mm = project_channels((pA, pB)[c % 2], range(4), base, 0, 0, j, j * KT,
                                              j == 0, j == GD - 1)
                    mm.then_inc(group_used, 1)

        def tiles(ps):
            return ps[:, :].rearrange("p (t s) -> p t s", s=S)

        def in_done(c):
            nc.scalar.wait_ge(group_used, m0 + (c + 1) * GD)

        def in_out(c):
            nc.scalar.wait_ge(group_used, m0 + (c + 1) * GD)
            ps = (pA, pB)[c % 2]
            if c == 0:
                nc.scalar.copy(qi[:, 4, :], pA[:, 0:S])
                nc.scalar.copy(lora_in[:, 0, :], pA[:, S:2 * S])
                nc.scalar.copy(lora_in[0:64, 1, :], pA[0:64, 3 * S:4 * S])
                last = nc.scalar.activation(widx[:, :, :], pA[:, 2 * S:2 * S + TB * IDX_HEADS]
                                            .rearrange("p (b h) -> p b h", b=TB), ACT.Copy, scale=IDX_SCALE)
            elif c < 7:
                last = nc.scalar.copy(rkv[:, 4 * (c - 1):4 * c, :], tiles(ps))
            elif c == 7:
                nc.scalar.copy(qk[:, 8:10, :], tiles(pB)[:, 0:2, :])
                last = nc.scalar.copy(vals[:, :, :], tiles(pB)[:, 2:4, :])
            elif c == 8:
                last = nc.scalar.copy(qi[:, 0:4, :], tiles(ps))
            else:
                last = nc.scalar.copy(qk[:, 4 * (c - 9):4 * (c - 8), :], tiles(ps))
            last.then_inc(in_read, 1)

        def win_act():
            for c in range(NCH):
                for j in range(GD):
                    if c or j >= SLOTS:
                        split_hi(m0, 0, 0, c * GD + j, SMALL if c == 0 else COLS)
                    if c and j == SLOTS - 1:
                        in_out(c - 1)
            in_out(NCH - 1)

        def win_dve():
            for c in range(NCH):
                for j in range(GD):
                    if c or j >= SLOTS:
                        split_lo(m0, 0, 0, c * GD + j, SMALL if c == 0 else COLS)

        PAIRS = (pA, pB, pT, pM)
        names = [("idx", 0), ("idx", 1), ("idx", 2), ("idx", 3), ("qk", 0), ("pt", 0), ("pv", 0),
                 ("qk", 1), ("qk", 2), ("pt", 1), ("pt", 2), ("pv", 1)]
        names += [("z", 0), ("z", 1), ("za", 0), ("za", 1), ("g", 0), ("g", 1), ("kn", 0), ("kb", 0), ("kb", 1),
                  ("bonus", 0), ("bonus", 1), ("vt", 0), ("vt", 1), ("at", 0), ("at", 1)]
        names += [("bx", i) for i in range(4)] + [("kx", i) for i in range(4)]
        names += [("bt", 0), ("bt", 1), ("kt", 0), ("kt", 1), ("akv", 0), ("akv", 1), ("m1", 0), ("m1", 1),
                  ("m2", 0), ("m2", 1), ("sa0", 0), ("sa0", 1), ("gt", 0), ("gt", 1)]
        for c in range(NCHUNK):
            names += [("sa", c)] * (c > 0) + [("ys", c)] + [("st", c)] * (c < NCHUNK - 1)
        names += [("mean", 0), ("mean", 1), ("var", 0), ("vb", 0), ("vb", 1)]
        number = {name: r for r, name in enumerate(names)}

        def fill(name, i):
            r = number[name, i]
            if r >= 4:
                nc.tensor.wait_ge(round_read[r % 4], r // 4)
            return PAIRS[r % 4]

        def filled(mm):
            mm.then_inc(round_full, 1)

        def full(eng, name, i):
            r = number[name, i]
            eng.wait_ge(round_full, r + 1)
            return PAIRS[r % 4]

        def read(ins, name, i):
            ins.then_inc(round_read[number[name, i] % 4], 1)

        def stored(eng, name, i):
            r = number[name, i]
            eng.wait_ge(round_read[r % 4], r // 4 + 1)

        steps = {name: sem("done_" + name) for name in (
            "qi_roped", "qk_roped", "score0_7", "max0", "max1", "exp0", "exp1", "prob0", "prob1",
            "att_hi0", "att_hi1", "lora_wa", "lora_g", "tanh", "gsig", "r", "v", "kk_sq", "kk_root", "kk_inv",
            "lsum", "p", "pinv", "rk", "a_rest", "a_first", "r_dec", "b_dec", "k_dec", "b_end", "k_end",
            "t_turned", "tt_zero", "sa_first", "y_intra1", "y_intra2", "y_intra3", "y_sq", "gn_root", "gn_inv",
            "y_gated", "mix_hi", "mix_lo")}
        vector_step = sem("vector_step")
        count = {}

        def done(ins, name):
            if name in steps:
                ins.then_inc(steps[name], 1)
            else:
                count[name] = len(count) + 1
                ins.then_inc(vector_step, 1)

        def need(eng, name):
            eng.wait_ge(steps[name], 1)

        def after(name):
            if name in steps:
                nc.vector.wait_ge(steps[name], 1)
            else:
                nc.vector.wait_ge(vector_step, count[name])

        V, A, T = nc.vector, nc.scalar, nc.tensor

        def tt(out, a0, a1, op):
            return V.tensor_tensor(out, a0, a1, op)

        def vdone(ins, name):
            done(ins, name)
            after(name)

        def vread(ins, name, i):
            read(ins, name, i)
            stored(nc.vector, name, i)

        def adone(ins, name):
            done(ins, name)
            nc.scalar.wait_ge(steps[name], 1)

        def aread(ins, name, i):
            read(ins, name, i)
            stored(nc.scalar, name, i)

        def head_rows(h):
            return slice(64 * (h % 2), 64 * (h % 2) + 64)

        def rope(arr, swap_buf, cosv, sinv, rows_, nt, mask, tag):
            vdone(V.stream_shuffle(swap_buf, arr, mask), tag + "_swapped")
            cb = cosv.unsqueeze(1).to_broadcast([rows_, nt, S])
            sb_ = sinv.unsqueeze(1).to_broadcast([rows_, nt, S])
            vdone(tt(swap_buf, swap_buf, sb_, ALU.mult), tag + "_sin")
            vdone(tt(arr, arr, cb, ALU.mult), tag + "_cos")
            vdone(tt(arr, arr, swap_buf, ALU.add), tag + "_roped")

        def attention_dve():
            V.wait_ge(in_read, NCH)
            rope(qi[:, :, :], swap[:, 0:5, :], cos_i, sin_i, P, 5, [8 + i for i in range(8)] + list(range(8))
                 + list(range(16, 32)), "qi")
            rope(qk[0:32, :, :], swap[0:32, :, :], cos_q, sin_q, 32, 10, [16 + i for i in range(16)]
                 + list(range(16)), "qk")
            for tb in range(TB):
                nk = (tb + 1) * P
                sc = score[:, tb, 0:nk]
                for i in range(2):
                    stored(V, "idx", 2 * tb + i)
                for h in range(IDX_HEADS):
                    src = relu[:, 4 * (h // 4) + 2 * (h % 2) + (h % 4) // 2, 0:nk]
                    if h == 0:
                        step = V.tensor_scalar(sc, src, widx[:, tb, 0:1], None, ALU.mult)
                    else:
                        step = V.scalar_tensor_tensor(sc, src, widx[:, tb, h:h + 1], sc, ALU.mult, ALU.add)
                    vdone(step, f"score{tb}_{h}")
                vdone(V.memset(score[0:64, tb, nk - 64:nk], HIDDEN), f"hidden{tb}")
                for i in range(TOPK // 8):
                    vdone(V.max(top8[:, :], sc), f"top{tb}_{i}")
                    vdone(V.match_replace(sc, top8[:, :], sc, TAKEN), f"taken{tb}_{i}")
                vdone(V.tensor_scalar(sc, sc, TAKEN, OFF, ALU.not_equal, ALU.mult), f"bias{tb}")
                for i in range(1 + tb):
                    hs = AH // (1 + tb)
                    ps = full(V, "qk", tb + i)
                    vread(V.scalar_tensor_tensor(att[:, i * hs:(i + 1) * hs, 0:nk],
                                                ps[:, 0:hs * nk].rearrange("p (h k) -> p h k", k=nk), ATT_SCALE,
                                                sc.unsqueeze(1).to_broadcast([P, hs, nk]), ALU.mult, ALU.add),
                         "qk", tb + i)
                    stored(V, "qk", tb + i)
                vdone(V.tensor_reduce(top[:, 0:AH], att[:, :, 0:nk], AX.X, ALU.max, negate=True), f"max{tb}")
                need(V, f"exp{tb}")
                vdone(V.reciprocal(top[:, 2 * AH:3 * AH], top[:, AH:2 * AH]), f"recip{tb}")
                vdone(tt(att[:, :, 0:nk], att[:, :, 0:nk],
                        top[:, 2 * AH:3 * AH].unsqueeze(2).to_broadcast([P, AH, nk]), ALU.mult), f"prob{tb}")
                need(V, f"att_hi{tb}")
                ps = PAIRS[number["pv", tb] % 4]
                vread(tt(xl[:, 0:AH, tb * P:tb * P + P], ps[:, :].rearrange("p (h q) -> p h q", q=P),
                        xh[:, 0:AH, tb * P:tb * P + P].bitcast(F32), ALU.subtract), "pv", tb)

        def attention_act():
            for tb in range(TB):
                nk = (tb + 1) * P
                for i in range(2):
                    ps = full(A, "idx", 2 * tb + i)
                    if tb:
                        need(A, f"score{tb - 1}_{IDX_HEADS - 1}")
                    aread(A.activation(relu[:, 4 * i:4 * i + 4, 0:nk], tiles(ps)[:, :, 0:nk], ACT.Relu),
                         "idx", 2 * tb + i)
            for tb in range(TB):
                nk = (tb + 1) * P
                need(A, f"max{tb}")
                for h in range(AH):
                    last = A.activation(att[:, h, 0:nk], att[:, h, 0:nk], ACT.Exp, bias=top[:, h:h + 1],
                                        accum_out=top[:, AH + h:AH + h + 1])
                adone(last, f"exp{tb}")
                for i in range(1 + tb):
                    ps = full(A, "pt", tb + i)
                    if tb and i == 0:
                        stored(A, "pv", 0)
                    aread(A.copy(prob_t[:, i, :, :], ps[:, :].rearrange("p (h q) -> p h q", q=P)), "pt", tb + i)
                ps = full(A, "pv", tb)
                adone(A.copy(xh[:, 0:AH, tb * P:tb * P + P], ps[:, :].rearrange("p (h q) -> p h q", q=P)),
                     f"att_hi{tb}")

        def attention_pe():
            need(T, "qi_roped")
            for tb in range(TB):
                nk = (tb + 1) * P
                tok = slice(tb * P, tb * P + P)
                for i in range(2):
                    ps = fill("idx", 2 * tb + i)
                    for k in range(4):
                        h = 4 * i + k
                        at = (2 * (h % 2) + (h % 4) // 2) * S
                        mm = T.matmul(ps[:, at:at + nk], qi[head_rows(h), h // 2, tok], qi[head_rows(h), 4, 0:nk],
                                      start=True, stop=True)
                    filled(mm)
            need(T, "qk_roped")
            for tb in range(TB):
                nk = (tb + 1) * P
                tok = slice(tb * P, tb * P + P)
                hs = AH // (1 + tb)
                for i in range(1 + tb):
                    ps = fill("qk", tb + i)
                    for k in range(hs):
                        h = i * hs + k
                        mm = T.matmul(ps[:, k * nk:(k + 1) * nk], qk[:, h, tok], qk[:, 8 + h // 4, 0:nk],
                                      start=True, stop=True)
                    filled(mm)
                need(T, f"prob{tb}")
                for i in range(1 + tb):
                    ps = fill("pt", tb + i)
                    for h in range(AH):
                        mm = T.transpose(ps[:, h * P:(h + 1) * P], att[:, h, i * P:(i + 1) * P], ident)
                    filled(mm)
                ps = fill("pv", tb)
                for i in range(1 + tb):
                    stored(T, "pt", tb + i)
                for gr in range(2):
                    for i in range(1 + tb):
                        mm = T.matmul(ps[:, gr * COLS:(gr + 1) * COLS], vals[:, i, gr * P:(gr + 1) * P],
                                      prob_t[:, i, 4 * gr:4 * gr + 4, :].rearrange("p h q -> p (h q)"),
                                      start=(i == 0), stop=(i == tb))
                filled(mm)

        def col(name, t):
            c = 3 * KD + NT * _CHANNELS.index("rwkv_" + name) + t
            return pcol[:, c:c + 1]

        def cols(name):
            c = 3 * KD + NT * _CHANNELS.index("rwkv_" + name)
            return pcol[:, c:c + NT]

        def chunks(arr):
            return arr[:, :, :].rearrange("p t (c s) -> p (t c) s", s=C)

        def lerp(dst, src, n, tag, mus, rows_=P):
            vdone(tt(dst[0:rows_, :, 1:S], src[0:rows_, :, 0:S - 1], src[0:rows_, :, 1:S], ALU.subtract), tag + "_d")
            vdone(V.tensor_scalar(dst[0:rows_, :, 0:1], src[0:rows_, :, 0:1], -1.0, None, ALU.mult), tag + "_d0")
            for t in range(n):
                last = V.scalar_tensor_tensor(dst[0:rows_, t, :], dst[0:rows_, t, :], mus(t), src[0:rows_, t, :],
                                              ALU.mult, ALU.add)
            vdone(last, tag)

        def rwkv_dve():
            lerp(lora[:, 0:1, :], lora_in[:, 0:1, :], 1, "lora_wa", lambda t: pcol2[:, 0:1])
            lerp(lora[:, 1:2, :], lora_in[:, 1:2, :], 1, "lora_g", lambda t: pcol2[0:64, 1:2], 64)
            lerp(k, rkv[:, 8:16, :], NT, "k", lambda t: col("mu_k", t))
            for t in range(NT):
                last = V.tensor_scalar(kk[:, t, :], k[:, t, :], col("k_k", t), None, ALU.mult)
            vdone(last, "kk_raw")
            vdone(tt(ksq[:, :, :], kk[:, :, :], kk[:, :, :], ALU.mult), "kk_sq")
            lerp(r, rkv[:, 0:8, :], NT, "r", lambda t: col("mu_r", t))
            lerp(v, rkv[:, 16:24, :], NT, "v", lambda t: col("mu_v", t))
            ps = full(V, "kn", 0)
            vread(V.tensor_scalar(hstat[0:RH, 0, :], ps[0:RH, 0:S], 1e-24, None, ALU.max), "kn", 0)
            need(V, "kk_root")
            vdone(V.reciprocal(hstat[0:RH, 2, :], hstat[0:RH, 1, :]), "kk_inv")
            for i in range(2):
                ps = full(V, "kb", i)
                vread(tt(kk[:, 4 * i:4 * i + 4, :], kk[:, 4 * i:4 * i + 4, :], tiles(ps), ALU.mult), "kb", i)
            for i in range(2):
                stored(V, "z", i)
            stored(V, "kb", 1)
            for t in range(NT):
                last = V.tensor_tensor_scan(lsum[:, t, :], keep, sw[:, t, :], 0.0, ALU.mult, ALU.add)
            vdone(last, "lsum")
            vdone(V.tensor_scalar(ka1[:, :], cols("k_a"), -1.0, 1.0, ALU.mult, ALU.add), "ka1")
            for i in range(2):
                stored(V, "za", i)
            for t in range(NT):
                last = V.tensor_scalar(ksq[:, t, :], iclr[:, t, :], col("k_a", t), ka1[:, t:t + 1],
                                       ALU.mult, ALU.add)
            vdone(last, "kmul")
            vdone(tt(k[:, :, :], k[:, :, :], ksq[:, :, :], ALU.mult), "k_mod")
            stored(V, "kb", 0)
            vdone(tt(iclr[:, :, :], iclr[:, :, :], kk[:, :, :], ALU.mult), "b")
            for t in range(NT):
                last = V.scalar_tensor_tensor(ksq[:, t, :], r[:, t, :], col("r_k", t), k[:, t, :],
                                              ALU.mult, ALU.mult)
            vdone(last, "rk")
            need(V, "p")
            a_dec, r_dec = chunks(ar[:, 0, :, :]), chunks(ar[:, 1, :, :])
            vdone(V.scalar_tensor_tensor(a_dec[:, :, 1:C], chunks(kk)[:, :, 1:C], -1.0,
                                        chunks(pdec)[:, :, 0:C - 1], ALU.mult, ALU.mult), "a_rest")
            vdone(V.tensor_scalar(a_dec[:, :, 0:1], chunks(kk)[:, :, 0:1], -1.0, None, ALU.mult), "a_first")
            vdone(tt(r_dec, chunks(r), chunks(pdec), ALU.mult), "r_dec")
            vdone(V.tensor_copy(pend[:, :, :], chunks(pdec)[:, :, C - 1:C]), "pend")
            need(V, "pinv")
            vdone(tt(iclr[:, :, :], iclr[:, :, :], pinv[:, :, :], ALU.mult), "b_dec")
            need(V, "rk")
            vdone(tt(k[:, :, :], k[:, :, :], pinv[:, :, :], ALU.mult), "k_dec")
            for i in range(2):
                ps = full(V, "bonus", i)
                vread(tt(bonus[:, 4 * i:4 * i + 4, :], v[:, 4 * i:4 * i + 4, :], tiles(ps), ALU.mult), "bonus", i)
            for name, dst in (("bx", bx), ("kx", kx)):
                for i in range(4):
                    ps = full(V, name, i)
                    vread(tt(dst[:, 8 * i:8 * i + 8, :, :].rearrange("p j a t -> p j (a t)"),
                            ps[:, :].rearrange("p (j a) -> p j a", j=8),
                            mask2.unsqueeze(1).to_broadcast([P, 8, 2 * C]), ALU.mult), name, i)
            pe_ = pend[:, :, :].to_broadcast([P, NT * NCHUNK, C])
            need(V, "b_dec")
            need(V, "k_dec")
            vdone(tt(chunks(iclr), chunks(iclr), pe_, ALU.mult), "b_end")
            vdone(tt(chunks(k), chunks(k), pe_, ALU.mult), "k_end")
            vdone(V.memset(tinv[:, :], 0.0), "t_zero")
            vdone(V.memset(tinv[:, 0:1024:33], 1.0), "t_one")
            vdone(V.memset(tt_all[:, :, :], 0.0), "tt_zero")
            V.wait_ge(sys_landed, 16)
            tv = tinv[:, :].rearrange("p (t s) -> p t s", s=32)
            nv = nsys[:, :].rearrange("p (s t) -> p s t", t=32)
            for q in range(31):
                if q:
                    V.wait_ge(substituted, q)
                shape = [P, 31 - q, q + 1]
                tmp = subst[:, 0:(31 - q) * (q + 1)].rearrange("p (t s) -> p t s", s=q + 1)
                tt(tmp, nv[:, q, q + 1:32].unsqueeze(2).to_broadcast(shape),
                   tv[:, q, 0:q + 1].unsqueeze(1).to_broadcast(shape), ALU.mult).then_inc(multiplied, 1)
                V.wait_ge(multiplied, q + 1)
                tt(tv[:, q + 1:32, 0:q + 1], tv[:, q + 1:32, 0:q + 1], tmp, ALU.add).then_inc(substituted, 1)
            V.wait_ge(substituted, 31)
            vdone(V.tensor_copy(subst[:, :].rearrange("p (s t) -> p s t", t=32),
                               tv.rearrange("p t s -> p s t")), "t_turned")
            for i in range(2):
                ps = full(V, "m1", i)
                vread(V.tensor_copy(xm[64 * i + 32:64 * i + 64, :, :],
                                   ps[64 * i + 32:64 * i + 64, :].rearrange("p (j s) -> p j s", s=32)), "m1", i)
            for i in range(2):
                ps = full(V, "m2", i)
                vread(V.tensor_copy(tt_all[64 * i:64 * i + 32, :, 32:64],
                                   ps[64 * i:64 * i + 32, :].rearrange("p (j s) -> p j s", s=32)), "m2", i)
            for i in range(2):
                ps = full(V, "sa0", i)
                vread(V.tensor_copy(sa0[:, i, :], ps[:, :]), "sa0", i)
            for i in range(2):
                stored(V, "sa0", i)
            for c in range(NCHUNK):
                half, blk = c % 2, c // 2
                hp = slice(64 * half, 64 * half + 64)
                if c:
                    ps = full(V, "sa", c)
                    vread(tt(sa[hp, :], sa0[hp, blk, :], ps[hp, :], ALU.add), "sa", c)
                else:
                    vdone(V.tensor_copy(sa[hp, :], sa0[hp, 0, :]), "sa_first")
                if c < NCHUNK - 1:
                    if c:
                        stored(V, "st", c - 1)
                        vdone(tt(sdec[:, :, :], state[:, :, :], pend[:, c:32:4, :].to_broadcast([P, NT, C]),
                                ALU.mult), f"sdec{c}")
                    ps = full(V, "st", c)
                    s3 = ps[:, 0:COLS].rearrange("p (t v) -> p t v", v=C)
                    if c:
                        step = tt(state[:, :, :], sdec[:, :, :], s3, ALU.add)
                    else:
                        step = V.tensor_copy(state[:, :, :], s3)
                    vread(step, "st", c)
                if c:
                    need(V, f"y_intra{c}")
                    ps = PAIRS[number["ys", c] % 4]
                    yc = y[:, :, c * C:(c + 1) * C]
                    vread(tt(yc, yc, ps[:, 0:COLS].rearrange("p (t s) -> p t s", s=C), ALU.add), "ys", c)
            for i in range(2):
                ps = full(V, "mean", i)
                yi = y[:, 4 * i:4 * i + 4, :]
                vread(V.scalar_tensor_tensor(yi, tiles(ps), -1.0 / C, yi, ALU.mult, ALU.add), "mean", i)
            for i in range(2):
                stored(V, "mean", i)
            vdone(tt(ysq[:, :, :], y[:, :, :], y[:, :, :], ALU.mult), "y_sq")
            ps = full(V, "var", 0)
            vread(V.tensor_scalar(hstat[0:RH, 0, :], ps[0:RH, 0:S], 1.0 / C, GN_EPS, ALU.mult, ALU.add), "var", 0)
            need(V, "gn_root")
            vdone(V.reciprocal(hstat[0:RH, 2, :], hstat[0:RH, 1, :]), "gn_inv")
            for i in range(2):
                ps = full(V, "vb", i)
                vread(tt(y[:, 4 * i:4 * i + 4, :], y[:, 4 * i:4 * i + 4, :], tiles(ps), ALU.mult), "vb", i)
            for i in range(2):
                stored(V, "vb", i)
            for t in range(NT):
                last = V.tensor_scalar(y[:, t, :], y[:, t, :], col("gn_gain", t), col("gn_bias", t),
                                       ALU.mult, ALU.add)
            vdone(last, "y_affine")
            for i in range(2):
                stored(V, "bonus", i)
            vdone(tt(y[:, :, :], y[:, :, :], bonus[:, :, :], ALU.add), "y_bonus")
            for i in range(2):
                stored(V, "g", i)
            vdone(tt(y[:, :, :], y[:, :, :], gate[:, :, :], ALU.mult), "y_gated")
            need(V, "mix_hi")
            vdone(tt(xl[:, NT:2 * NT, :], y[:, :, :], xh[:, NT:2 * NT, :].bitcast(F32), ALU.subtract), "mix_lo")

        def rwkv_act():
            A.wait_ge(lora_landed, 48)
            need(A, "lora_wa")
            adone(A.activation(lora[0:64, 0, :], lora[0:64, 0, :], ACT.Tanh), "tanh")
            need(A, "lora_g")
            adone(A.activation(lora[0:64, 1, :], lora[0:64, 1, :], ACT.Sigmoid), "gsig")
            for name, dst, bias in (("z", sw, "w0"), ("za", iclr, "a0")):
                for i in range(2):
                    ps = full(A, name, i)
                    if name == "z" and i == 0:
                        need(A, "r")
                    for t in range(4):
                        last = A.activation(dst[:, 4 * i + t, :], tiles(ps)[:, t, :], ACT.Sigmoid,
                                            bias=col(bias, 4 * i + t))
                    aread(last, name, i)
            for i in range(2):
                ps = full(A, "g", i)
                aread(A.copy(gate[:, 4 * i:4 * i + 4, :], tiles(ps)), "g", i)
            stored(A, "kn", 0)
            adone(A.activation(hstat[0:RH, 1, :], hstat[0:RH, 0, :], ACT.Sqrt), "kk_root")
            need(A, "lsum")
            need(A, "v")
            adone(A.activation(pdec[:, :, :], lsum[:, :, :], ACT.Exp, scale=-DECAY), "p")
            adone(A.activation(pinv[:, :, :], lsum[:, :, :], ACT.Exp, scale=DECAY), "pinv")
            for name, dst in (("vt", v_tok), ("at", a_tok)):
                for i in range(2):
                    ps = full(A, name, i)
                    aread(A.copy(dst[:, i, :], ps[:, :]), name, i)
            for name, dst in (("bt", b_tok), ("kt", k_tok)):
                for i in range(2):
                    ps = full(A, name, i)
                    aread(A.copy(dst[:, i, :], ps[:, :]), name, i)
            for i in range(2):
                ps = full(A, "akv", i)
                aread(A.copy(akv[:, i, :], ps[:, :]), "akv", i)
            for i in range(2):
                ps = full(A, "gt", i)
                aread(A.copy(gt[:, i, :], ps[:, :]), "gt", i)
            for c in range(NCHUNK):
                ps = full(A, "ys", c)
                step = A.copy(y[:, :, c * C:(c + 1) * C],
                              ps[:, COLS:2 * COLS].rearrange("p (t s) -> p t s", s=C))
                if c:
                    adone(step, f"y_intra{c}")
                else:
                    aread(step, "ys", 0)
            stored(A, "var", 0)
            adone(A.activation(hstat[0:RH, 1, :], hstat[0:RH, 0, :], ACT.Sqrt), "gn_root")
            need(A, "y_gated")
            adone(A.copy(xh[:, NT:2 * NT, :], y[:, :, :]), "mix_hi")

        def rwkv_pe():
            def channel_rounds(name, lhs, rhs, width=S):
                for i in range(2):
                    ps = fill(name, i)
                    for t in range(4):
                        mm = T.matmul(ps[:, t * S:(t + 1) * S], lhs(4 * i + t), rhs, start=True, stop=True)
                    filled(mm)

            def spread(name):
                for i in range(2):
                    ps = fill(name, i)
                    for t in range(4):
                        mm = T.matmul(ps[:, t * S:(t + 1) * S], to_channels[0:RH, 4 * i + t, :], hstat[0:RH, 2, :],
                                      start=True, stop=True)
                    filled(mm)

            def head_sums(name, src):
                ps = fill(name, 0)
                for t in range(NT):
                    mm = T.matmul(ps[0:RH, 0:S], to_heads[:, t, :], src[:, t, :], start=(t == 0), stop=(t == NT - 1))
                filled(mm)

            def within_heads(name, src):
                for i in range(2):
                    ps = fill(name, i)
                    for b in range(2):
                        t = 4 * i + 2 * b
                        mm = T.matmul(ps[:, b * COLS:(b + 1) * COLS], same_head,
                                      src[:, t:t + 2, :].rearrange("p t s -> p (t s)"), start=True, stop=True)
                    filled(mm)

            def turn_tokens(name, tile_of):
                for i in range(TB):
                    ps = fill(name, i)
                    for t in range(NT):
                        mm = T.transpose(ps[:, t * P:(t + 1) * P], tile_of(t, i), ident)
                    filled(mm)

            T.wait_ge(lora_landed, 48)
            need(T, "tanh")
            channel_rounds("z", lambda t: lora_w[0:64, t * P:(t + 1) * P], lora[0:64, 0, :])
            channel_rounds("za", lambda t: lora_w[64:P, t * P:(t + 1) * P], lora[64:P, 0, :])
            need(T, "gsig")
            channel_rounds("g", lambda t: lora_g[0:64, t * P:(t + 1) * P], lora[0:64, 1, :])
            need(T, "kk_sq")
            head_sums("kn", ksq)
            need(T, "kk_inv")
            spread("kb")
            need(T, "rk")
            within_heads("bonus", ksq)
            need(T, "v")
            turn_tokens("vt", lambda t, i: v[:, t, i * P:(i + 1) * P])
            need(T, "a_rest")
            need(T, "a_first")
            turn_tokens("at", lambda t, i: ar[:, 0, t, i * P:(i + 1) * P])
            need(T, "r_dec")
            for name, arr, step in (("bx", iclr, "b_dec"), ("kx", k, "k_dec")):
                need(T, step)
                for i in range(4):
                    blk, par = i // 2, i % 2
                    hs = slice(64 * par, 64 * par + 64)
                    ps = fill(name, i)
                    for t in range(NT):
                        for half in range(2):
                            c = 2 * blk + half
                            mm = T.matmul(ps[64 * half:64 * half + 64, t * 2 * C:(t + 1) * 2 * C].rearrange(
                                              "p (a s) -> p a s", a=2),
                                          arr[hs, t, c * C:(c + 1) * C],
                                          ar[hs, :, t, c * C:(c + 1) * C],
                                          start=True, stop=True)
                    filled(mm)
            need(T, "b_end")
            turn_tokens("bt", lambda t, i: iclr[:, t, i * P:(i + 1) * P])
            need(T, "k_end")
            turn_tokens("kt", lambda t, i: k[:, t, i * P:(i + 1) * P])
            for i in range(2):
                stored(T, "vt", i)
            for i in range(4):
                stored(T, "kx", i)

            def by_chunk(name, lhs, rhs, extra=None):
                for blk in range(2):
                    ps = fill(name, blk)
                    for jj in range(RH):
                        for half in range(2):
                            hs = slice(64 * half, 64 * half + 64)
                            mm = T.matmul(ps[hs, jj * C:(jj + 1) * C], lhs(hs, blk, jj), rhs(hs, blk, jj),
                                          start=True, stop=True)
                    filled(mm)

            def hcol(jj):
                h = 2 * (jj % NT) + jj // NT
                return slice(h * C, h * C + C)
            by_chunk("akv", lambda hs, b, jj: kx[hs, b * RH + jj, 0, :], lambda hs, b, jj: v_tok[hs, b, hcol(jj)])
            T.wait_ge(inv_landed, 16 * 6)
            for i in range(2):
                ps = fill("m1", i)
                lo, hi = slice(64 * i, 64 * i + 32), slice(64 * i + 32, 64 * i + 64)
                for j in range(2 * RH):
                    mm = T.matmul(ps[hi, j * 32:(j + 1) * 32], bx[lo, j, 0, 32:64], t_plain[lo, j, :],
                                  start=True, stop=True)
                filled(mm)
            for i in range(2):
                stored(T, "m1", i)
                ps = fill("m2", i)
                lo, hi = slice(64 * i, 64 * i + 32), slice(64 * i + 32, 64 * i + 64)
                for j in range(2 * RH):
                    mm = T.matmul(ps[lo, j * 32:(j + 1) * 32], xm[hi, j, :], tt_all[hi, j, 32:64],
                                  start=True, stop=True)
                filled(mm)
            for i in range(2):
                stored(T, "m2", i)
                stored(T, "akv", i)
                stored(T, "at", i)
            by_chunk("sa0", lambda hs, b, jj: tt_all[hs, b * RH + jj, :], lambda hs, b, jj: akv[hs, b, jj * C:(jj + 1) * C])
            for blk in range(2):
                ps = fill("gt", blk)
                for half in range(2):
                    hs = slice(64 * half, 64 * half + 64)
                    for jj in range(RH):
                        par, t = jj // NT, jj % NT
                        mm = T.matmul(ps[64 * par:64 * par + 64, half * COLS + t * C:half * COLS + (t + 1) * C],
                                      a_tok[hs, blk, hcol(jj)], tt_all[hs, blk * RH + jj, :], start=True, stop=True)
                filled(mm)
            for i in range(2):
                stored(T, "gt", i)
                stored(T, "bt", i)
                stored(T, "kt", i)
                stored(T, "sa0", i)
            for c in range(NCHUNK):
                half, blk = c % 2, c // 2
                hs = slice(64 * half, 64 * half + 64)
                if c:
                    stored(T, "st", c - 1)
                    ps = fill("sa", c)
                    for jj in range(RH):
                        par, t = jj // NT, jj % NT
                        ch = slice(64 * par, 64 * par + 64)
                        mm = T.matmul(ps[hs, jj * C:(jj + 1) * C],
                                      gt[ch, blk, half * COLS + t * C:half * COLS + (t + 1) * C], state[ch, t, :],
                                      start=True, stop=True)
                    filled(mm)
                ps = fill("ys", c)
                if c:
                    for jj in range(RH):
                        par, t = jj // NT, jj % NT
                        ch = slice(64 * par, 64 * par + 64)
                        T.matmul(ps[ch, t * C:(t + 1) * C], state[ch, t, :], ar[ch, 1, t, c * C:(c + 1) * C],
                                 start=True, stop=True)
                    stored(T, "sa", c)
                else:
                    need(T, "sa_first")
                for jj in range(RH):
                    par, t = jj // NT, jj % NT
                    ch = slice(64 * par, 64 * par + 64)
                    out_ = ps[ch, COLS + t * C:COLS + (t + 1) * C]
                    j = blk * RH + jj
                    T.matmul(out_, sa[hs, jj * C:(jj + 1) * C], bx[hs, j, 1, :], start=True, stop=False)
                    mm = T.matmul(out_, v_tok[hs, blk, hcol(jj)], kx[hs, j, 1, :], start=False, stop=True)
                filled(mm)
                if c < NCHUNK - 1:
                    ps = fill("st", c)
                    for jj in range(RH):
                        par, t = jj // NT, jj % NT
                        ch = slice(64 * par, 64 * par + 64)
                        out_ = ps[ch, t * C:(t + 1) * C]
                        T.matmul(out_, b_tok[hs, blk, hcol(jj)], sa[hs, jj * C:(jj + 1) * C], start=True, stop=False)
                        mm = T.matmul(out_, k_tok[hs, blk, hcol(jj)], v_tok[hs, blk, hcol(jj)], start=False, stop=True)
                    filled(mm)
            for c in range(NCHUNK):
                stored(T, "ys", c)
            within_heads("mean", y)
            need(T, "y_sq")
            head_sums("var", ysq)
            need(T, "gn_inv")
            spread("vb")

        def mix_sp_dmas(eng):
            for i in range(4):
                stored(eng, "bx", i)
            for q in range(4):
                half = q % 2
                eng.dma_start(n_dram[q].rearrange("j s t -> s j t"),
                              bx[32 * q:32 * q + 32, :, 0, 32 * half:32 * half + 32]).then_inc(sys_stored, 16)
            eng.wait_ge(sys_stored, 64)
            eng.dma_start(nsys[:, :], n_dram.rearrange("q j s t -> (q j) (s t)")).then_inc(sys_landed, 16)
            need(eng, "t_turned")
            need(eng, "tt_zero")
            eng.dma_start(t_dram[0].rearrange("q j s t -> (q j) (s t)"), subst[:, :]).then_inc(inv_stored, 16)
            eng.dma_start(t_dram[1].rearrange("q j s t -> (q j) (s t)"), tinv[:, :]).then_inc(inv_stored, 16)
            eng.wait_ge(inv_stored, 32)
            for q in range(4):
                half = q % 2
                eng.dma_start(tt_all[32 * q:32 * q + 32, :, 32 * half:32 * half + 32],
                              t_dram[0, q].rearrange("j s t -> s j t")).then_inc(inv_landed, 16)
                if half == 0:
                    eng.dma_start(t_plain[32 * q:32 * q + 32, :, :],
                                  t_dram[1, q].rearrange("j t s -> t j s")).then_inc(inv_landed, 16)

        def out_pe():
            need(T, "mix_lo")
            for i in range(TB):
                stored(T, "pv", i)
            for c in range(DC):
                if c >= 2:
                    T.wait_ge(x_added, DC + c - 1)
                for j in range(GD):
                    project_tokens((psA, psB)[c % 2], xh, xl, w0_out, 0, 0, c * GD + j, j * KT,
                                   j == 0, j == GD - 1)

        def out_act():
            for g in range(DC * GD):
                split_hi(w0_out, 0, 0, g)

        def out_dve():
            def add(c):
                V.wait_ge(group_used, w0_out + (c + 1) * GD)
                xc = x[:, :, c * COLS:(c + 1) * COLS]
                tt(xc, (psA, psB)[c % 2][:, :, :], xc, ALU.add).then_inc(x_added, 1)
            for g in range(DC * GD):
                split_lo(w0_out, 0, 0, g)
                if g > GD and g % GD == SLOTS - 1:
                    add(g // GD - 1)
            add(DC - 1)

        def mix_load_all(sp):
            mix_load(sp)
            out_load(sp, 0, SLOTS)
            mix_sp_dmas(sp)
            out_load(sp, SLOTS, DC * GD)

        def mix_act():
            for j in range(SLOTS):
                split_hi(m0, 0, 0, j, SMALL)
            norm_act(1)
            norm_hi(1)
            win_act()
            attention_act()
            rwkv_act()
            out_act()

        def mix_dve():
            for j in range(SLOTS):
                split_lo(m0, 0, 0, j, SMALL)
            norm_dve(1)
            norm_lo(1)
            win_dve()
            attention_dve()
            rwkv_dve()
            out_dve()

        def mix_pe():
            turn_norm(1)
            win_pe()
            attention_pe()
            rwkv_pe()
            out_pe()

        added_before_down = [0, 2 * DC]

        ffn1, ffn2 = a["ffn1"], a["ffn2"]
        base2 = FFN_GROUPS + MIX_GROUPS

        block = ctx.enter_context(nc.Block())

        @block.sync
        def _(sp):
            xv = a["x"].rearrange("(b p) d -> p b d", p=P)
            sp.dma_start(x[:, :, :], xv).then_inc(x_landed, 16)
            sp.dma_start(consts[:, :], a["consts"]).then_inc(const_landed, 16)
            n = 0
            for name in ("ffn1_norm", "mix_norm", "ffn2_norm"):
                sp.dma_start(prow[n:n + KD, :], a[name].rearrange("(k p) -> k p", p=P)).then_inc(const_landed, 16)
                n += KD
            for name in _CHANNELS:
                sp.dma_start(prow[n:n + NT, :], a[name].rearrange("(k p) -> k p", p=P)).then_inc(const_landed, 16)
                n += NT
            for row, col_, name in ((0, 0, "rwkv_mu_w"), (0, 64, "rwkv_mu_a"), (1, 0, "rwkv_mu_g"), (1, 64, "rwkv_mu_g")):
                sp.dma_start(prow2[row:row + 1, col_:col_ + 64], a[name].rearrange("(o n) -> o n", o=1))\
                    .then_inc(const_landed, 16)
            ffn_load(sp, 0, 0, *ffn1)
            mix_load_all(sp)
            ffn_load(sp, 1, base2, *ffn2)
            sp.wait_ge(x_added, (3) * DC)
            sp.dma_start(fgain[:, :], a["final_norm"].rearrange("(o d) -> o d", o=1).to_broadcast([P, D]))\
                .then_inc(gain_landed, 16)
            sp.wait_ge(out_ready, TB)
            sp.dma_start(out.rearrange("(b p) d -> p b d", p=P), xs[:, :, :]).then_inc(out_stored, 16)
            sp.wait_ge(out_stored, 16)

        @block.scalar
        def _(act_engine):
            for j in range(SLOTS):
                split_hi(0, 0, PER, j)
            norm_act(0)
            norm_hi(0)
            ffn_act(0, 0)
            mix_act()
            for j in range(SLOTS):
                split_hi(base2, 0, PER, j)
            norm_act(2)
            norm_hi(2)
            ffn_act(1, base2)
            norm_act(3)

        @block.vector
        def _(dve):
            dve.wait_ge(params_turned, 1)
            nc.vector.tensor_copy(pcol2[:, :], psM[:, P:P + 2])
            nc.vector.tensor_copy(pcol[:, :], psM[:, 0:P]).then_inc(params_ready, 1)
            for j in range(SLOTS):
                split_lo(0, 0, PER, j)
            norm_dve(0)
            norm_lo(0)
            ffn_dve(0, 0)
            mix_dve()
            for j in range(SLOTS):
                split_lo(base2, 0, PER, j)
            norm_dve(2)
            norm_lo(2)
            ffn_dve(1, base2)
            norm_dve(3)
            dve.wait_ge(gain_landed, 16)
            dve.wait_ge(xs_ready, TB * (4))
            for tb in range(TB):
                nc.vector.tensor_tensor(xs[:, tb, :], xs[:, tb, :], fgain[:, :], ALU.mult).then_inc(out_ready, 1)

        @block.tensor
        def _(pe):
            pe.wait_ge(const_landed, 16 * (8 + len(_CHANNELS)))
            nc.tensor.transpose(psM[:, 0:P], prow[:, :], ident)
            nc.tensor.transpose(psM[:, P:P + 2], prow2[:, :], ident[0:2, 0:2]).then_inc(params_turned, 1)
            turn_norm(0)
            ffn_pe(0, 0)
            mix_pe()
            turn_norm(2)
            ffn_pe(1, base2)


_CHANNELS = ["rwkv_mu_r", "rwkv_mu_k", "rwkv_mu_v", "rwkv_w0", "rwkv_a0", "rwkv_k_k", "rwkv_k_a", "rwkv_r_k",
             "rwkv_gn_gain", "rwkv_gn_bias"]


def launch(nc, args, out):
    a = {}
    for name, v in args.items():
        a[name] = v if name == "final_norm" else v[0]
    a["rwkv_r_k"] = a["rwkv_r_k"].rearrange("h n -> (h n)")
    for f in ("ffn1", "ffn2"):
        a[f] = (a[f + "_w_gate"], a[f + "_w_up"], a[f + "_w_down"])
    a["consts"] = nc.inline_tensor(constants(), "constants").ap()
    build(nc, a, out[0])


def kernel(**inputs):
    import numpy as _np
    import concourse.bacc as _bacc
    from concourse import mybir as _mybir
    from concourse.bass_utils import run_bass_kernel_spmd as _run

    nc = _bacc.Bacc("TRN2", target_bir_lowering=False, num_devices=1)
    arrays, args = {}, {}
    for name, v in inputs.items():
        v = _np.ascontiguousarray(v)
        arrays[f"in_{name}"] = v
        args[name] = nc.dram_tensor(f"in_{name}", v.shape, _mybir.dt.from_np(v.dtype), kind="ExternalInput").ap()
    out = nc.dram_tensor("out", (1, S, D), F32, kind="ExternalOutput").ap()
    launch(nc, args, out)
    r = _run(nc, [arrays], core_ids=[0])
    return r.results[0]["out"]
```

```python
from contextlib import ExitStack

import numpy as np

import concourse.bass as bass
from concourse import mybir

F32 = mybir.dt.float32
F32R = mybir.dt.float32r
ALU = mybir.AluOpType
ACT = mybir.ActivationFunctionType
AX = mybir.AxisListType

P = 128
D = 2048
S = 256
TB = S // P
F = 5632
COLS = 512
KD = D // P
KF = F // P
NORM_EPS = 1e-6
AW = 1024
RW = 1024
NT = RW // P

SLOTS = 4
KT = 2
GD = KD // KT
GF = KF // KT
FC = F // COLS
DC = D // COLS

MIX_GROUPS = 11 * GD + DC * GD
AH = 8
KVW = 256
ATT_SCALE = float(P) ** -0.5
IDX_HEADS = 8
IDX_SCALE = (IDX_HEADS ** -0.5) * (64 ** -0.5)
TOPK = 64
TAKEN = -float(2.0 ** 127)
HIDDEN = -float(2.0 ** 126)
OFF = -1e30
RH = 16
C = 64
NCHUNK = S // C
GN_EPS = 64e-5
DECAY = float(np.exp(-0.5))


CONST_WIDTH = 2816


def constants():
    t = np.zeros((P, CONST_WIDTH), np.float32)
    p = np.arange(P)
    s = np.arange(S)
    t[:, 0:128] = np.eye(P)
    t[:, 128:256] = p[:, None] // 64 == p[None, :] // 64
    head = 2 * np.arange(NT)[:, None] + (p // 64)[None, :]
    t[:, 256:384] = (head.T[:, :, None] == np.arange(RH)).reshape(P, NT * RH)
    t[:, 384:448] = np.arange(C)[None, :] > (p % 64)[:, None]
    t[:, 448:512] = np.arange(C)[None, :] >= (p % 64)[:, None]
    t[:, 512:768] = s[None, :] % C != 0

    def rotary(width, rows_, at):
        rot = width // 4
        half = rot // 2
        freq = np.float32(500000.0) ** (-(np.arange(half, dtype=np.float32) * np.float32(2.0) / np.float32(rot)))
        ang = s.astype(np.float32)[:, None] * freq[None, :].astype(np.float32)
        cos, sin = np.cos(ang).astype(np.float32).T, np.sin(ang).astype(np.float32).T
        for q in range(rows_):
            j = q % width
            t[q, at:at + S] = cos[j % half] if j < rot else 1.0
            if j < rot:
                t[q, at + S:at + 2 * S] = -sin[j] if j < half else sin[j - half]

    rotary(64, P, 768)
    rotary(P, 32, 1280)
    t[0:RH, 1792:2816] = (head[None, :, :] == np.arange(RH)[:, None, None]).reshape(RH, NT * P)
    return t


def build(nc, a, out):
    with ExitStack() as ctx:
        address = {}

        def sb(name, shape, dt=F32):
            handle = ctx.enter_context(nc.sbuf_tensor(name, shape, dt))
            address[name] = nc.sbuf_base - 4 * int(np.prod(shape[1:]))
            return handle

        def pb(name, shape):
            return ctx.enter_context(nc.psum_tensor(name, shape, F32))

        def sem(name):
            return ctx.enter_context(nc.semaphore(name))

        x = sb("x", [P, TB, D])
        raw = sb("raw", [P, SLOTS, KT, COLS])
        whi = sb("whi", [P, SLOTS, KT, COLS], F32R)
        wlo = sb("wlo", [P, SLOTS, KT, COLS], F32R)
        xh = sb("xh", [P, KD, S], F32R)
        xl = sb("xl", [P, KD, S], F32R)
        consts = sb("consts", [P, CONST_WIDTH])
        ident = consts[:, 0:128]
        same_head = consts[:, 128:256]
        to_heads = consts[:, 256:384].rearrange("p (t h) -> p t h", h=RH)
        mask2 = consts[:, 384:512]
        keep = consts[:, 512:768]
        cos_i, sin_i = consts[:, 768:1024], consts[:, 1024:1280]
        cos_q, sin_q = consts[0:32, 1280:1536], consts[0:32, 1536:1792]
        to_channels = consts[:, 1792:2816].rearrange("p (t c) -> p t c", c=P)
        prow = sb("prow", [P, P])
        pcol = sb("pcol", [P, P])
        prow2 = sb("prow2", [2, P])
        pcol2 = sb("pcol2", [P, 2])
        ss = sb("ss", [P, 8])
        stage = sb("stage", [P, 2, TB, COLS])
        silu, act = stage[:, 0], stage[:, 1]
        fgain = stage[:, :, :, :].rearrange("p a b c -> p (a b c)")
        UNIT = NT * S * 4
        arena = sb("arena", [P, 11 * UNIT // 4])

        def at(name, shape, where, unit=0, plus=0, dt=F32):
            return nc.alloc_sbuf_tensor_at(name, shape, dt, offset=address[where.name] + unit * UNIT + plus)

        KB = 1024
        xs = at("xs", [P, TB, D], arena)
        hh = at("hh", [P, KF, S], arena, dt=F32R)
        hl = at("hl", [P, KF, S], arena, plus=KF * S * 4, dt=F32R)
        ar = at("ar", [P, 2, NT, S], arena, 0)
        kk, r = ar[:, 0, :, :], ar[:, 1, :, :]
        k, v = at("k", [P, NT, S], arena, 2), at("v", [P, NT, S], arena, 3)
        temp = at("temp", [P, 5, S], arena, 7)
        qk = at("qk", [P, 10, S], arena, plus=61 * KB)
        vals = at("vals", [P, TB, S], arena, plus=71 * KB)
        qi = at("qi", [P, 5, S], arena, plus=73 * KB)
        lora = at("lora", [P, 2, S], arena, plus=78 * KB)
        lora_w = at("lora_w", [P, RW], arena, plus=80 * KB)
        lora_g = at("lora_g", [P, RW], arena, plus=84 * KB)
        widx = sb("widx", [P, TB, IDX_HEADS])
        att = at("att", [P, AH, S], raw, 0)
        relu = at("relu", [P, IDX_HEADS, S], raw, 1)
        prob_t = at("prob_t", [P, TB, AH, P], xl, 1)
        score = at("score", [P, TB, S], arena, 7)
        top8 = at("top8", [P, 8], arena, 7, 2 * KB)
        top = at("top", [P, 3 * AH], arena, 7, 2 * KB + 64)
        ksq = at("ksq", [P, NT, S], arena, 3)
        sw = at("sw", [P, NT, S], arena, 4)
        pdec = at("pdec", [P, NT, S], arena, 4)
        lsum = at("lsum", [P, NT, S], arena, 5)
        pinv = at("pinv", [P, NT, S], arena, 5)
        bonus = at("bonus", [P, NT, S], arena, 5)
        iclr = at("iclr", [P, NT, S], arena, 6)
        gate = at("gate", [P, NT, S], xh, 1)
        hstat = at("hstat", [P, 3, S], stage, plus=4 * KB)
        ka1 = sb("ka1", [P, NT])
        pend = sb("pend", [P, NT * NCHUNK, 1])
        a_tok = at("a_tok", [P, TB, RW], arena, 3)
        v_tok = at("v_tok", [P, TB, RW], arena, 4)
        b_tok = at("b_tok", [P, TB, RW], arena, 0)
        k_tok = at("k_tok", [P, TB, RW], arena, 6)
        bx = at("bx", [P, 2 * RH, 2, C], whi)
        kx = at("kx", [P, 2 * RH, 2, C], wlo)
        tt_all = at("tt_all", [P, 2 * RH, C], arena, 2)
        nsys = at("nsys", [P, 1024], arena, 10)
        tinv = at("tinv", [P, 1024], arena, 10, 4 * KB)
        subst = at("subst", [P, 1024], arena, 8)
        t_plain = at("t_plain", [P, 2 * RH, 32], arena, 8, 4 * KB)
        xm = at("xm", [P, 2 * RH, 32], arena, 9)
        sa = at("sa", [P, RW], arena, 9, 4 * KB)
        akv = at("akv", [P, TB, RW], arena, 7)
        sa0 = at("sa0", [P, TB, RW], xl, 1)
        gt = at("gt", [P, TB, RW], stage)
        state = at("state", [P, NT, C], arena, 10)
        sdec = at("sdec", [P, NT, C], arena, 10, 2 * KB)
        y = at("y", [P, NT, S], arena, 7)
        ysq = at("ysq", [P, NT, S], arena, 8)
        n_dram = nc.dram_tensor("n_dram", [4, 2 * RH, 32, 32], F32, kind="Internal").ap()
        t_dram = nc.dram_tensor("t_dram", [2, 4, 2 * RH, 32, 32], F32, kind="Internal").ap()

        psA = pb("psA", [P, TB, COLS])
        psB = pb("psB", [P, TB, COLS])
        psT = pb("psT", [P, 2 * COLS])
        psM = pb("psM", [P, 2 * COLS])
        pA, pB = (ps[:, :, :].rearrange("p b c -> p (b c)") for ps in (psA, psB))
        pT, pM = psT[:, :], psM[:, :]

        PER = 2 * GD
        m0 = FC * PER + DC * GF
        raw_landed = [sem(f"raw_landed{i}") for i in range(SLOTS)]
        hi_ready = sem("hi_ready")
        lo_ready = sem("lo_ready")
        group_used = sem("group_used")
        const_landed = sem("const_landed")
        params_turned = sem("params_turned")
        params_ready = sem("params_ready")
        x_landed = sem("x_landed")
        square_ready = sem("square_ready")
        norm_step = sem("norm_step")
        root_ready = sem("root_ready")
        xs_ready = sem("xs_ready")
        xs_turned = sem("xs_turned")
        xh_ready = sem("xh_ready")
        xl_ready = sem("xl_ready")
        silu_ready = sem("silu_ready")
        act_ready = sem("act_ready")
        act_turned = sem("act_turned")
        hh_ready = sem("hh_ready")
        hl_ready = sem("hl_ready")
        x_added = sem("x_added")
        gain_landed = sem("gain_landed")
        out_ready = sem("out_ready")
        out_stored = sem("out_stored")
        in_read = sem("in_read")
        a_rest = sem("a_rest")
        lora_landed = sem("lora_landed")
        round_full = sem("round_full")
        round_read = [sem(f"round_read{i}") for i in range(4)]
        sys_stored = sem("sys_stored")
        sys_landed = sem("sys_landed")
        inv_stored = sem("inv_stored")
        inv_landed = sem("inv_landed")
        multiplied = sem("multiplied")
        substituted = sem("substituted")

        def load_group(sp, src, base, n, per, j, ncol=COLS):
            g = base + j
            slot = g % SLOTS
            if not (isinstance(n, int) and g + n * per < SLOTS):
                sp.wait_ge(hi_ready, n * per + g - SLOTS + 1)
                sp.wait_ge(lo_ready, n * per + g - SLOTS + 1)
            sp.dma_start(raw[:, slot, :, 0:ncol], src).then_inc(raw_landed[slot], 16)

        def split_hi(base, n, per, j, ncol=COLS):
            g = base + j
            slot = g % SLOTS
            extra = 48 * min(max(g // SLOTS + 1 - m0 // SLOTS, 0), GD // SLOTS)
            nc.scalar.wait_ge(raw_landed[slot], n * (16 * per // SLOTS) + 16 * (g // SLOTS + 1) + extra)
            if not (isinstance(n, int) and g + n * per < SLOTS):
                nc.scalar.wait_ge(group_used, n * per + g - SLOTS + 1)
            nc.scalar.copy(whi[:, slot, :, 0:ncol], raw[:, slot, :, 0:ncol]).then_inc(hi_ready, 1)

        def split_lo(base, n, per, j, ncol=COLS):
            g = base + j
            slot = g % SLOTS
            nc.vector.wait_ge(hi_ready, n * per + g + 1)
            if not (isinstance(n, int) and g + n * per < SLOTS):
                nc.vector.wait_ge(group_used, n * per + g - SLOTS + 1)
            nc.vector.tensor_tensor(wlo[:, slot, :, 0:ncol], raw[:, slot, :, 0:ncol],
                                    whi[:, slot, :, 0:ncol].bitcast(F32), ALU.subtract).then_inc(lo_ready, 1)

        def wait_group(base, n, per, j):
            nc.tensor.wait_ge(lo_ready, n * per + base + j + 1)

        def project_tokens(ps, h, l, base, n, per, j, k0, first, last, ncol=COLS):
            wait_group(base, n, per, j)
            slot = (base + j) % SLOTS
            for t in range(KT):
                for tb in range(TB):
                    tok = slice(tb * P, tb * P + P)
                    for p, (lhs, rhs) in enumerate(((h, whi), (h, wlo), (l, whi))):
                        mm = nc.tensor.matmul(ps[:, tb, 0:ncol], lhs[:, k0 + t, tok], rhs[:, slot, t, 0:ncol],
                                              start=(first and t == 0 and p == 0),
                                              stop=(last and t == KT - 1 and p == 2))
            mm.then_inc(group_used, 1)

        def rows(w, k0):
            return w[k0 * P:(k0 + KT) * P, :].rearrange("(t p) n -> p t n", p=P)

        def norm_act(f):
            if f == 0:
                nc.scalar.wait_ge(x_landed, 16)
            else:
                nc.scalar.wait_ge(x_added, DC * f)
            nc.scalar.activation(xs[:, 0, :], x[:, 0, :], ACT.Square, accum_out=ss[:, 0:1]).then_inc(square_ready, 1)
            nc.scalar.wait_ge(norm_step, 2 * f + 1)
            nc.scalar.activation(ss[:, 4:6], ss[:, 2:4], ACT.Sqrt).then_inc(root_ready, 1)

        def norm_dve(f):
            if f == 0:
                nc.vector.wait_ge(x_landed, 16)
            else:
                nc.vector.wait_ge(x_added, DC * f)
            nc.vector.tensor_tensor_reduce(xs[:, 1, :], x[:, 1, :], x[:, 1, :], 1.0, 0.0, ALU.mult, ALU.add,
                                           ss[:, 1:2]).then_inc(square_ready, 1)
            nc.vector.wait_ge(square_ready, 2 * (f + 1))
            nc.vector.tensor_scalar(ss[:, 2:4], ss[:, 0:2], 1.0 / D, NORM_EPS, ALU.mult, ALU.add)\
                .then_inc(norm_step, 1)
            nc.vector.wait_ge(root_ready, f + 1)
            nc.vector.reciprocal(ss[:, 6:8], ss[:, 4:6]).then_inc(norm_step, 1)
            nc.vector.wait_ge(norm_step, 2 * f + 2)
            for tb in range(TB):
                nc.vector.tensor_scalar(xs[:, tb, :], x[:, tb, :], ss[:, 6 + tb:7 + tb], None, ALU.mult)\
                    .then_inc(xs_ready, 1)

        QK = 4

        def turn_norm(f):
            for q in range(KD // QK):
                nc.tensor.wait_ge(xs_ready, TB * (f + 1))
                if q >= 2 or f:
                    nc.tensor.wait_ge(xl_ready, (KD // QK) * f + max(q - 1, 0))
                ps = (psT, psM)[q % 2]
                for t in range(QK):
                    for tb in range(TB):
                        k = q * QK + t
                        mm = nc.tensor.transpose(ps[:, t * S + tb * P:t * S + tb * P + P],
                                                 xs[:, tb, k * P:k * P + P], ident)
                mm.then_inc(xs_turned, 1)

        def norm_hi(f):
            for q in range(KD // QK):
                nc.scalar.wait_ge(xs_turned, (KD // QK) * f + q + 1)
                if q == 0:
                    nc.scalar.wait_ge(params_ready, 1)
                ps = (psT, psM)[q % 2]
                for t in range(QK):
                    k = q * QK + t
                    g = f * KD + k
                    mm = nc.scalar.activation(xh[:, k, :], ps[:, t * S:t * S + S], ACT.Copy, scale=pcol[:, g:g + 1])
                mm.then_inc(xh_ready, 1)

        def norm_lo(f):
            for q in range(KD // QK):
                nc.vector.wait_ge(xh_ready, (KD // QK) * f + q + 1)
                ps = (psT, psM)[q % 2]
                for t in range(QK):
                    k = q * QK + t
                    g = f * KD + k
                    mm = nc.vector.scalar_tensor_tensor(xl[:, k, :], ps[:, t * S:t * S + S], pcol[:, g:g + 1],
                                                        xh[:, k, :].bitcast(F32), ALU.mult, ALU.subtract)
                mm.then_inc(xl_ready, 1)

        PER = 2 * GD

        def ffn_load(sp, f, base, w_gate, w_up, w_down):
            def chunk(n):
                col = n * COLS
                for j in range(GD):
                    load_group(sp, rows(w_gate, j * KT)[:, :, bass.ds(col, COLS)], base, n, PER, j)
                for j in range(GD):
                    load_group(sp, rows(w_up, j * KT)[:, :, bass.ds(col, COLS)], base, n, PER, GD + j)
            chunk(0)
            with sp.Fori(1, FC) as n:
                chunk(n)
            down = base + FC * PER
            with sp.Fori(0, DC // 2) as m:
                for j in range(2 * GF):
                    col = (2 * m + j // GF) * COLS
                    load_group(sp, rows(w_down, (j % GF) * KT)[:, :, bass.ds(col, COLS)], down, m, 2 * GF, j)

        def ffn_act(f, base):
            def silu_gate(n):
                nc.scalar.wait_ge(group_used, n * PER + (base + GD))
                if not (isinstance(n, int) and n == 0 and f == 0):
                    nc.scalar.wait_ge(act_ready, n + f * FC)
                nc.scalar.activation(silu[:, :, :], psA[:, :, :], ACT.Silu).then_inc(silu_ready, 1)

            def turned_hi(n):
                nc.scalar.wait_ge(act_turned, n + (f * FC + 1))
                nc.scalar.copy(hh[:, bass.ds(n * 4, 4), :], psT[:, :].rearrange("p (t s) -> p t s", t=4))\
                    .then_inc(hh_ready, 1)

            def chunk(n, first):
                for j in range(PER):
                    if not (first and j < SLOTS):
                        split_hi(base, n, PER, j)
                    if j == GD + SLOTS - 1:
                        if not first:
                            turned_hi(n - 1)
                        silu_gate(n)
            chunk(0, True)
            chunk(1, False)
            with nc.scalar.Fori(2, FC) as n:
                chunk(n, False)
            down = base + FC * PER
            for j in range(SLOTS):
                split_hi(down, 0, 2 * GF, j)
            turned_hi(FC - 1)
            for j in range(SLOTS, 2 * GF):
                split_hi(down, 0, 2 * GF, j)
            for j in range(2 * GF):
                split_hi(down, 1, 2 * GF, j)

        def ffn_dve(f, base):
            def gate_up(n):
                nc.vector.wait_ge(silu_ready, n + (f * FC + 1))
                nc.vector.wait_ge(group_used, n * PER + (base + PER))
                if not (isinstance(n, int) and n == 0 and f == 0):
                    nc.vector.wait_ge(act_turned, n + f * FC)
                nc.vector.tensor_tensor(act[:, :, :], psB[:, :, :], silu[:, :, :], ALU.mult).then_inc(act_ready, 1)

            def turned_lo(n):
                nc.vector.wait_ge(hh_ready, n + (f * FC + 1))
                nc.vector.tensor_tensor(hl[:, bass.ds(n * 4, 4), :], psT[:, :].rearrange("p (t s) -> p t s", t=4),
                                        hh[:, bass.ds(n * 4, 4), :].bitcast(F32), ALU.subtract)\
                    .then_inc(hl_ready, 1)

            def chunk(n, first):
                for j in range(PER):
                    if not (first and j < SLOTS):
                        split_lo(base, n, PER, j)
                    if j == SLOTS - 1 and not first:
                        gate_up(n - 1)
                    if j == GD + SLOTS - 1 and not first:
                        turned_lo(n - 1)
            chunk(0, True)
            chunk(1, False)
            with nc.vector.Fori(2, FC) as n:
                chunk(n, False)
            down = base + FC * PER
            for j in range(SLOTS):
                split_lo(down, 0, 2 * GF, j)
            gate_up(FC - 1)
            turned_lo(FC - 1)
            for c in range(DC):
                for j in range(GF):
                    if c or j >= SLOTS:
                        split_lo(down, 0, 0, c * GF + j)
                    if c and j == SLOTS - 1:
                        add_down(f, down, c - 1)
            add_down(f, down, DC - 1)

        def add_down(f, down, c):
            nc.vector.wait_ge(group_used, down + (c + 1) * GF)
            ps = (psA, psB)[c % 2]
            nc.vector.scalar_tensor_tensor(x[:, :, c * COLS:(c + 1) * COLS], ps[:, :, :], 0.5,
                                           x[:, :, c * COLS:(c + 1) * COLS], ALU.mult, ALU.add)\
                .then_inc(x_added, 1)

        def ffn_pe(f, base):
            def turn(n):
                nc.tensor.wait_ge(act_ready, n + (f * FC + 1))
                if not (isinstance(n, int) and n == 0 and f == 0):
                    nc.tensor.wait_ge(hl_ready, n + f * FC)
                for t in range(4):
                    for tb in range(TB):
                        mm = nc.tensor.transpose(psT[:, t * S + tb * P:t * S + tb * P + P],
                                                 act[:, tb, t * P:t * P + P], ident)
                mm.then_inc(act_turned, 1)

            def chunk(n, first):
                if not first:
                    nc.tensor.wait_ge(silu_ready, n + f * FC)
                for j in range(GD):
                    if first and j % 2 == 0:
                        nc.tensor.wait_ge(xl_ready, 4 * (2 * f) + j // 2 + 1)
                    project_tokens(psA, xh, xl, base, n, PER, j, j * KT, j == 0, j == GD - 1)
                if not first:
                    turn(n - 1)
                for j in range(GD):
                    project_tokens(psB, xh, xl, base, n, PER, GD + j, j * KT, j == 0, j == GD - 1)
            chunk(0, True)
            chunk(1, False)
            with nc.tensor.Fori(2, FC) as n:
                chunk(n, False)
            turn(FC - 1)
            down = base + FC * PER
            for c in range(DC):
                if c == 0:
                    nc.tensor.wait_ge(hl_ready, (f + 1) * FC)
                if c >= 2:
                    nc.tensor.wait_ge(x_added, added_before_down[f] + c - 1)
                for j in range(GF):
                    project_tokens((psA, psB)[c % 2], hh, hl, down, 0, 0, c * GF + j, j * KT,
                                   j == 0, j == GF - 1)

        FFN_GROUPS = FC * PER + DC * GF
        ki_col, wi_col, rkv_col = 2048, 2112, 2120
        lora_col = rkv_col + 3 * RW
        KI2, LORA, WI = 0, P, P + 192
        SMALL = WI + IDX_HEADS
        NCH = 11
        in_col = [None] + [rkv_col + i * COLS for i in (2, 3, 0, 1, 4, 5)] + [AW, AW + 2 * KVW, 0, COLS]
        m0 = FFN_GROUPS
        w0_out = m0 + NCH * GD

        def in_rows(k0, lo, hi):
            return rows(a["w_in"], k0)[:, :, lo:hi]

        def mix_load(sp):
            for j in range(GD):
                g = m0 + j
                slot = g % SLOTS
                sp.wait_ge(hi_ready, g - SLOTS + 1)
                sp.wait_ge(lo_ready, g - SLOTS + 1)
                for at, lo, hi in ((KI2, ki_col, wi_col), (KI2 + 64, ki_col, wi_col),
                                   (LORA, lora_col, lora_col + 192), (WI, wi_col, rkv_col)):
                    sp.dma_start(raw[:, slot, :, at:at + hi - lo], in_rows(j * KT, lo, hi))\
                        .then_inc(raw_landed[slot], 16)
            sp.wait_ge(x_added, DC)
            sp.dma_start(lora_w[0:64, :], a["rwkv_w2"]).then_inc(lora_landed, 16)
            sp.dma_start(lora_w[64:P, :], a["rwkv_a2"]).then_inc(lora_landed, 16)
            sp.dma_start(lora_g[0:64, :], a["rwkv_g2"]).then_inc(lora_landed, 16)
            for c in range(1, NCH):
                for j in range(GD):
                    load_group(sp, in_rows(j * KT, in_col[c], in_col[c] + COLS), m0 + c * GD, 0, 0, j)

        def out_load(sp, g0, g1):
            for g in range(g0, g1):
                c, j = g // GD, g % GD
                load_group(sp, rows(a["w_out"], j * KT)[:, :, c * COLS:(c + 1) * COLS], w0_out, 0, 0, g)

        def project_channels(ps, cts, base, n, per, j, k0, first, last):
            slot = (base + j) % SLOTS
            for i, ct in enumerate(cts):
                for t in range(KT):
                    for p, (w, h) in enumerate(((whi, xh), (wlo, xh), (whi, xl))):
                        mm = nc.tensor.matmul(ps[:, i * S:(i + 1) * S], w[:, slot, t, ct * P:(ct + 1) * P],
                                              h[:, k0 + t, :], start=(first and t == 0 and p == 0 and i % 2 == 0),
                                              stop=(last and t == KT - 1 and p == 2), skip_group_check=True)
            return mm

        def project_small_tokens(ps, at, step, col, width, base, j, k0, first, last):
            slot = (base + j) % SLOTS
            for t in range(KT):
                for tb in range(TB):
                    tok = slice(tb * P, tb * P + P)
                    for p, (h, w) in enumerate(((xh, whi), (xh, wlo), (xl, whi))):
                        mm = nc.tensor.matmul(ps[:, at + tb * step:at + tb * step + width], h[:, k0 + t, tok],
                                              w[:, slot, t, col:col + width],
                                              start=(first and t == 0 and p == 0 and tb == 0),
                                              stop=(last and t == KT - 1 and p == 2), skip_group_check=True)
            return mm

        def win_small():
            for j in range(GD):
                if j % 2 == 0:
                    nc.tensor.wait_ge(xl_ready, 4 + j // 2 + 1)
                wait_group(m0, 0, 0, j)
                project_small_tokens(pA, 2 * S, IDX_HEADS, WI, IDX_HEADS, m0, j, j * KT, j == 0, j == GD - 1)
                slot = (m0 + j) % SLOTS
                for t in range(KT):
                    for p, (w, h) in enumerate(((whi, xh), (wlo, xh), (whi, xl))):
                        nc.tensor.matmul(pA[0:64, 3 * S:4 * S], w[:, slot, t, LORA + P:LORA + 192],
                                         h[:, j * KT + t, :], start=False,
                                         stop=(j == GD - 1 and t == KT - 1 and p == 2), skip_group_check=True)
                project_channels(pA, (0, 1), m0, 0, 0, j, j * KT, j == 0, j == GD - 1).then_inc(group_used, 1)

        def win_groups(g0, g1):
            for g in range(g0, g1):
                c, j = g // GD, g % GD
                base = m0 + c * GD
                if c >= 2 and j == 0:
                    nc.tensor.wait_ge(in_read, c - 1)
                wait_group(base, 0, 0, j)
                if c == 7:
                    project_small_tokens(pB, 2 * S, S, 2 * P, 2 * P, base, j, j * KT, j == 0, j == GD - 1)
                    mm = project_channels(pB, (0, 1), base, 0, 0, j, j * KT, j == 0, j == GD - 1)
                else:
                    mm = project_channels((pA, pB)[c % 2], range(4), base, 0, 0, j, j * KT,
                                          j == 0, j == GD - 1)
                mm.then_inc(group_used, 1)

        def tiles(ps):
            return ps[:, :].rearrange("p (t s) -> p t s", s=S)

        def in_out(c):
            nc.scalar.wait_ge(group_used, m0 + (c + 1) * GD)
            ps = (pA, pB)[c % 2]
            if c == 0:
                nc.scalar.copy(qi[:, 4, :], pA[:, 0:S])
                nc.scalar.copy(lora[:, 0, :], pA[:, S:2 * S])
                nc.scalar.copy(lora[0:64, 1, :], pA[0:64, 3 * S:4 * S])
                last = nc.scalar.activation(widx[:, :, :], pA[:, 2 * S:2 * S + TB * IDX_HEADS]
                                            .rearrange("p (b h) -> p b h", b=TB), ACT.Copy, scale=IDX_SCALE)
            elif c < 7:
                half = 4 * ((c - 1) % 2)
                if c == 5:
                    full(nc.scalar, "bonus", 1)
                last = nc.scalar.copy((k, r, v)[(c - 1) // 2][:, half:half + 4, :], tiles(ps))
            elif c == 7:
                nc.scalar.copy(qk[:, 8:10, :], tiles(pB)[:, 0:2, :])
                last = nc.scalar.copy(vals[:, :, :], tiles(pB)[:, 2:4, :])
            elif c == 8:
                last = nc.scalar.copy(qi[:, 0:4, :], tiles(ps))
            else:
                last = nc.scalar.copy(qk[:, 4 * (c - 9):4 * (c - 8), :], tiles(ps))
            last.then_inc(in_read, 1)

        PAIRS = (pA, pB, pT, pM)
        early = [("z", 0), ("z", 1), ("za", 0), ("za", 1), ("kn", 0), ("kb", 0), ("kb", 1), ("bonus", 0), ("bonus", 1),
                 ("vt", 0), ("vt", 1), ("at", 0), ("at", 1)]
        names = [("bx", i) for i in range(4)] + [("kx", i) for i in range(4)]
        names += [("idx", 0), ("idx", 1), ("bt", 0), ("bt", 1), ("kt", 0), ("kt", 1), ("g", 0), ("g", 1),
                  ("idx", 2), ("idx", 3), ("qk", 0), ("pt", 0), ("pv", 0),
                  ("qk", 1), ("qk", 2), ("pt", 1), ("pt", 2), ("pv", 1)]
        names += [("akv", 0), ("akv", 1), ("m1", 0), ("m1", 1), ("m2", 0), ("m2", 1), ("sa0", 0), ("sa0", 1),
                  ("gt", 0), ("gt", 1)]
        for c in range(NCHUNK):
            names += [("sa", c)] * (c > 0) + [("ys", c)] + [("st", c)] * (c < NCHUNK - 1)
        names += [("mean", 0), ("mean", 1), ("var", 0), ("vb", 0), ("vb", 1)]
        number = {name: n for n, name in enumerate(early + names)}
        pair = {name: 2 + n % 2 for n, name in enumerate(early)}
        pair.update({name: n % 4 for n, name in enumerate(names)})
        before = {name: sum(pair[other] == pair[name] and number[other] < number[name] for other in number)
                  for name in number}

        def fill(name, i):
            if before[name, i]:
                nc.tensor.wait_ge(round_read[pair[name, i]], before[name, i])
            return PAIRS[pair[name, i]]

        def filled(mm):
            mm.then_inc(round_full, 1)

        def full(eng, name, i):
            eng.wait_ge(round_full, number[name, i] + 1)
            return PAIRS[pair[name, i]]

        def read(ins, name, i):
            ins.then_inc(round_read[pair[name, i]], 1)

        def stored(eng, name, i):
            eng.wait_ge(round_read[pair[name, i]], before[name, i] + 1)

        steps = {name: sem("done_" + name) for name in (
            "qi_roped", "q_roped", "score0_7", "max0", "max1", "exp0", "exp1", "prob0", "prob1",
            "att_hi0", "att_hi1", "lora_wa", "lora_g", "tanh", "gsig", "v1", "kk_sq", "kk_root", "kk_inv",
            "lsum", "p", "pinv", "rk", "b_dec", "r_dec", "k_dec", "b_end", "k_end",
            "t_turned", "tt_zero", "sa_first", "y_intra1", "y_intra2", "y_intra3", "y_sq", "gn_root", "gn_inv",
            "y_gated", "mix_hi", "mix_lo")}
        vector_step = sem("vector_step")
        count = {}

        def done(ins, name):
            if name in steps:
                ins.then_inc(steps[name], 1)
            else:
                count[name] = len(count) + 1
                ins.then_inc(vector_step, 1)

        def need(eng, name):
            eng.wait_ge(steps[name], 1)

        def after(name):
            if name in steps:
                nc.vector.wait_ge(steps[name], 1)
            else:
                nc.vector.wait_ge(vector_step, count[name])

        V, A, T = nc.vector, nc.scalar, nc.tensor

        def tt(out, a0, a1, op):
            return V.tensor_tensor(out, a0, a1, op)

        def vdone(ins, name):
            done(ins, name)
            after(name)

        def vread(ins, name, i):
            read(ins, name, i)
            stored(nc.vector, name, i)

        def adone(ins, name):
            done(ins, name)
            nc.scalar.wait_ge(steps[name], 1)

        def aread(ins, name, i):
            read(ins, name, i)
            stored(nc.scalar, name, i)

        def head_rows(h):
            return slice(64 * (h % 2), 64 * (h % 2) + 64)

        def rope(arr, swap_buf, cosv, sinv, rows_, nt, mask, tag):
            vdone(V.stream_shuffle(swap_buf, arr, mask), tag + "_swapped")
            cb = cosv.unsqueeze(1).to_broadcast([rows_, nt, S])
            sb_ = sinv.unsqueeze(1).to_broadcast([rows_, nt, S])
            vdone(tt(swap_buf, swap_buf, sb_, ALU.mult), tag + "_sin")
            vdone(tt(arr, arr, cb, ALU.mult), tag + "_cos")
            vdone(tt(arr, arr, swap_buf, ALU.add), tag + "_roped")

        def attention_dve():
            for tb in range(TB):
                nk = (tb + 1) * P
                sc = score[:, tb, 0:nk]
                for i in range(2):
                    stored(V, "idx", 2 * tb + i)
                for h in range(IDX_HEADS):
                    src = relu[:, 4 * (h // 4) + 2 * (h % 2) + (h % 4) // 2, 0:nk]
                    if h == 0:
                        step = V.tensor_scalar(sc, src, widx[:, tb, 0:1], None, ALU.mult)
                    else:
                        step = V.scalar_tensor_tensor(sc, src, widx[:, tb, h:h + 1], sc, ALU.mult, ALU.add)
                    vdone(step, f"score{tb}_{h}")
                vdone(V.memset(score[0:64, tb, nk - 64:nk], HIDDEN), f"hidden{tb}")
                for i in range(TOPK // 8):
                    vdone(V.max(top8[:, :], sc), f"top{tb}_{i}")
                    vdone(V.match_replace(sc, top8[:, :], sc, TAKEN), f"taken{tb}_{i}")
                vdone(V.tensor_scalar(sc, sc, TAKEN, OFF, ALU.not_equal, ALU.mult), f"bias{tb}")
                for i in range(1 + tb):
                    hs = AH // (1 + tb)
                    ps = full(V, "qk", tb + i)
                    vread(V.scalar_tensor_tensor(att[:, i * hs:(i + 1) * hs, 0:nk],
                                                ps[:, 0:hs * nk].rearrange("p (h k) -> p h k", k=nk), ATT_SCALE,
                                                sc.unsqueeze(1).to_broadcast([P, hs, nk]), ALU.mult, ALU.add),
                         "qk", tb + i)
                vdone(V.tensor_reduce(top[:, 0:AH], att[:, :, 0:nk], AX.X, ALU.max, negate=True), f"max{tb}")
                need(V, f"exp{tb}")
                vdone(V.reciprocal(top[:, 2 * AH:3 * AH], top[:, AH:2 * AH]), f"recip{tb}")
                vdone(tt(att[:, :, 0:nk], att[:, :, 0:nk],
                        top[:, 2 * AH:3 * AH].unsqueeze(2).to_broadcast([P, AH, nk]), ALU.mult), f"prob{tb}")
                need(V, f"att_hi{tb}")
                ps = PAIRS[pair["pv", tb]]
                vread(tt(xl[:, 0:AH, tb * P:tb * P + P], ps[:, :].rearrange("p (h q) -> p h q", q=P),
                        xh[:, 0:AH, tb * P:tb * P + P].bitcast(F32), ALU.subtract), "pv", tb)

        def index_act(tb):
            nk = (tb + 1) * P
            for i in range(2):
                ps = full(A, "idx", 2 * tb + i)
                if tb:
                    need(A, f"score{tb - 1}_{IDX_HEADS - 1}")
                aread(A.activation(relu[:, 4 * i:4 * i + 4, 0:nk], tiles(ps)[:, :, 0:nk], ACT.Relu),
                      "idx", 2 * tb + i)

        def attention_act():
            for tb in range(TB):
                nk = (tb + 1) * P
                need(A, f"max{tb}")
                for h in range(AH):
                    last = A.activation(att[:, h, 0:nk], att[:, h, 0:nk], ACT.Exp, bias=top[:, h:h + 1],
                                        accum_out=top[:, AH + h:AH + h + 1])
                adone(last, f"exp{tb}")
                for i in range(1 + tb):
                    ps = full(A, "pt", tb + i)
                    if tb and i == 0:
                        stored(A, "pv", 0)
                    aread(A.copy(prob_t[:, i, :, :], ps[:, :].rearrange("p (h q) -> p h q", q=P)), "pt", tb + i)
                ps = full(A, "pv", tb)
                adone(A.copy(xh[:, 0:AH, tb * P:tb * P + P], ps[:, :].rearrange("p (h q) -> p h q", q=P)),
                     f"att_hi{tb}")

        def index_pe(tb):
            nk = (tb + 1) * P
            tok = slice(tb * P, tb * P + P)
            for i in range(2):
                ps = fill("idx", 2 * tb + i)
                for m in range(4):
                    h = 4 * i + m
                    at = (2 * (h % 2) + (h % 4) // 2) * S
                    mm = T.matmul(ps[:, at:at + nk], qi[head_rows(h), h // 2, tok], qi[head_rows(h), 4, 0:nk],
                                  start=True, stop=True)
                filled(mm)

        def attention_pe():
            need(T, "q_roped")
            for tb in range(TB):
                nk = (tb + 1) * P
                tok = slice(tb * P, tb * P + P)
                hs = AH // (1 + tb)
                for i in range(1 + tb):
                    ps = fill("qk", tb + i)
                    for k in range(hs):
                        h = i * hs + k
                        mm = T.matmul(ps[:, k * nk:(k + 1) * nk], qk[:, h, tok], qk[:, 8 + h // 4, 0:nk],
                                      start=True, stop=True)
                    filled(mm)
                need(T, f"prob{tb}")
                for i in range(1 + tb):
                    ps = fill("pt", tb + i)
                    for h in range(AH):
                        mm = T.transpose(ps[:, h * P:(h + 1) * P], att[:, h, i * P:(i + 1) * P], ident)
                    filled(mm)
                ps = fill("pv", tb)
                for i in range(1 + tb):
                    stored(T, "pt", tb + i)
                for gr in range(2):
                    for i in range(1 + tb):
                        mm = T.matmul(ps[:, gr * COLS:(gr + 1) * COLS], vals[:, i, gr * P:(gr + 1) * P],
                                      prob_t[:, i, 4 * gr:4 * gr + 4, :].rearrange("p h q -> p (h q)"),
                                      start=(i == 0), stop=(i == tb))
                filled(mm)

        def col(name, t):
            c = 3 * KD + NT * _CHANNELS.index("rwkv_" + name) + t
            return pcol[:, c:c + 1]

        def cols(name):
            c = 3 * KD + NT * _CHANNELS.index("rwkv_" + name)
            return pcol[:, c:c + NT]

        def chunks(arr):
            return arr[:, :, :].rearrange("p t (c s) -> p (t c) s", s=C)

        def lerp(arr, t0, n, tag, mus, rows_=P):
            part = arr[0:rows_, t0:t0 + n, :]
            diff = temp[0:rows_, 0:n, :]
            tt(diff[:, :, 1:S], part[:, :, 0:S - 1], part[:, :, 1:S], ALU.subtract)
            vdone(V.tensor_scalar(diff[:, :, 0:1], part[:, :, 0:1], -1.0, None, ALU.mult), tag + "_d")
            for t in range(n):
                last = V.scalar_tensor_tensor(part[:, t, :], diff[:, t, :], mus(t0 + t), part[:, t, :],
                                              ALU.mult, ALU.add)
            vdone(last, tag)

        def win_dve():
            def splits(g0, g1):
                for g in range(g0, g1):
                    split_lo(m0, 0, 0, g, SMALL if g < GD else COLS)

            splits(SLOTS, 13)
            V.wait_ge(in_read, 1)
            lerp(lora, 0, 1, "lora_wa", lambda t: pcol2[:, 0:1])
            lerp(lora, 1, 1, "lora_g", lambda t: pcol2[0:64, 1:2], 64)
            splits(13, 21)
            V.wait_ge(in_read, 2)
            lerp(k, 0, 4, "k0", lambda t: col("mu_k", t))
            splits(21, 25)
            for i in range(2):
                stored(V, "z", i)
            for t in range(NT):
                last = V.tensor_tensor_scan(lsum[:, t, :], keep, sw[:, t, :], 0.0, ALU.mult, ALU.add)
            vdone(last, "lsum")
            splits(25, 29)
            V.wait_ge(in_read, 3)
            lerp(k, 4, 4, "k1", lambda t: col("mu_k", t))
            splits(29, 31)
            for t in range(NT):
                last = V.tensor_scalar(kk[:, t, :], k[:, t, :], col("k_k", t), None, ALU.mult)
            vdone(last, "kk_raw")
            splits(31, 32)
            vdone(tt(ksq[:, :, :], kk[:, :, :], kk[:, :, :], ALU.mult), "kk_sq")
            splits(32, 37)
            V.wait_ge(in_read, 4)
            lerp(r, 0, 4, "r0", lambda t: col("mu_r", t))
            splits(37, 39)
            ps = full(V, "kn", 0)
            vread(V.tensor_scalar(hstat[0:RH, 0, :], ps[0:RH, 0:S], 1e-24, None, ALU.max), "kn", 0)
            splits(39, 40)
            vdone(V.tensor_scalar(ka1[:, :], cols("k_a"), -1.0, 1.0, ALU.mult, ALU.add), "ka1")
            for i in range(2):
                stored(V, "za", i)
            for t in range(NT):
                last = V.tensor_scalar(ksq[:, t, :], iclr[:, t, :], col("k_a", t), ka1[:, t:t + 1],
                                       ALU.mult, ALU.add)
            vdone(last, "kmul")
            splits(40, 42)
            need(V, "kk_root")
            vdone(V.reciprocal(hstat[0:RH, 2, :], hstat[0:RH, 1, :]), "kk_inv")
            vdone(tt(k[:, :, :], k[:, :, :], ksq[:, :, :], ALU.mult), "k_mod")
            splits(42, 45)
            V.wait_ge(in_read, 5)
            lerp(r, 4, 4, "r1", lambda t: col("mu_r", t))
            splits(45, 47)
            for t in range(NT):
                last = V.scalar_tensor_tensor(ksq[:, t, :], r[:, t, :], col("r_k", t), k[:, t, :],
                                              ALU.mult, ALU.mult)
            vdone(last, "rk")
            splits(47, 49)
            for i in range(2):
                ps = full(V, "kb", i)
                vread(tt(kk[:, 4 * i:4 * i + 4, :], kk[:, 4 * i:4 * i + 4, :], tiles(ps), ALU.mult), "kb", i)
            splits(49, 50)
            vdone(tt(iclr[:, :, :], iclr[:, :, :], kk[:, :, :], ALU.mult), "b")
            splits(50, 51)
            need(V, "p")
            a_dec, r_dec = chunks(kk), chunks(r)
            tt(a_dec[:, :, 1:C], a_dec[:, :, 1:C], chunks(pdec)[:, :, 0:C - 1], ALU.mult).then_inc(a_rest, 1)
            V.wait_ge(a_rest, 1)
            vdone(V.tensor_scalar(kk[:, :, :], kk[:, :, :], -1.0, None, ALU.mult), "a_dec")
            splits(51, 53)
            V.wait_ge(in_read, 6)
            lerp(v, 0, 4, "v0", lambda t: col("mu_v", t))
            splits(53, 55)
            vdone(tt(r_dec, r_dec, chunks(pdec), ALU.mult), "r_dec")
            splits(55, 57)
            vdone(V.tensor_copy(pend[:, :, :], chunks(pdec)[:, :, C - 1:C]), "pend")
            need(V, "pinv")
            vdone(tt(iclr[:, :, :], iclr[:, :, :], pinv[:, :, :], ALU.mult), "b_dec")
            splits(57, 59)
            vdone(tt(k[:, :, :], k[:, :, :], pinv[:, :, :], ALU.mult), "k_dec")
            splits(59, 61)
            V.wait_ge(in_read, 7)
            lerp(v, 4, 4, "v1", lambda t: col("mu_v", t))
            splits(61, 64)
            for i in range(2):
                ps = full(V, "bonus", i)
                vread(tt(bonus[:, 4 * i:4 * i + 4, :], v[:, 4 * i:4 * i + 4, :], tiles(ps), ALU.mult), "bonus", i)
            splits(64, 69)
            V.wait_ge(in_read, 8)
            rope_heads(qk[0:32, 8:10, :], temp[0:32, 0:2, :], "k")
            splits(69, 77)
            V.wait_ge(in_read, 9)
            rope(qi[:, :, :], temp[:, 0:5, :], cos_i, sin_i, P, 5, [8 + i for i in range(8)] + list(range(8))
                 + list(range(16, 32)), "qi")
            splits(77, NCH * GD)

        def rope_heads(arr, swap_buf, tag):
            rope(arr, swap_buf, cos_q, sin_q, 32, arr.shape[1], [16 + i for i in range(16)] + list(range(16)), tag)

        def win_act():
            def splits(g0, g1):
                for g in range(g0, g1):
                    split_hi(m0, 0, 0, g, SMALL if g < GD else COLS)
                    if g > GD and g % GD == SLOTS - 1:
                        in_out(g // GD - 1)

            def sigmoids(name, dst, bias, i):
                ps = full(A, name, i)
                for t in range(4):
                    last = A.activation(dst[:, 4 * i + t, :], tiles(ps)[:, t, :], ACT.Sigmoid,
                                        bias=col(bias, 4 * i + t))
                aread(last, name, i)

            splits(SLOTS, 15)
            need(A, "lora_wa")
            adone(A.activation(lora[0:64, 0, :], lora[0:64, 0, :], ACT.Tanh), "tanh")
            need(A, "lora_g")
            adone(A.activation(lora[0:64, 1, :], lora[0:64, 1, :], ACT.Sigmoid), "gsig")
            splits(15, 22)
            sigmoids("z", sw, "w0", 0)
            splits(22, 23)
            sigmoids("z", sw, "w0", 1)
            splits(23, 30)
            sigmoids("za", iclr, "a0", 0)
            splits(30, 31)
            sigmoids("za", iclr, "a0", 1)
            splits(31, 33)
            need(A, "lsum")
            adone(A.activation(pdec[:, :, :], lsum[:, :, :], ACT.Exp, scale=-DECAY), "p")
            splits(33, 35)
            adone(A.activation(pinv[:, :, :], lsum[:, :, :], ACT.Exp, scale=DECAY), "pinv")
            splits(35, 40)
            stored(A, "kn", 0)
            adone(A.activation(hstat[0:RH, 1, :], hstat[0:RH, 0, :], ACT.Sqrt), "kk_root")
            splits(40, 70)
            for i in range(2):
                copy_tokens("vt", v_tok, i)
            splits(70, 78)
            for i in range(2):
                copy_tokens("at", a_tok, i)
            splits(78, NCH * GD)
            in_out(NCH - 1)

        def copy_tokens(name, dst, i):
            ps = full(A, name, i)
            aread(A.copy(dst[:, i, :], ps[:, :]), name, i)

        def rwkv_systems():
            for name, dst in (("bx", bx), ("kx", kx)):
                for i in range(4):
                    ps = full(V, name, i)
                    vread(tt(dst[:, 8 * i:8 * i + 8, :, :].rearrange("p j a t -> p j (a t)"),
                            ps[:, :].rearrange("p (j a) -> p j a", j=8),
                            mask2.unsqueeze(1).to_broadcast([P, 8, 2 * C]), ALU.mult), name, i)
            pe_ = pend[:, :, :].to_broadcast([P, NT * NCHUNK, C])
            vdone(tt(chunks(iclr), chunks(iclr), pe_, ALU.mult), "b_end")
            vdone(tt(chunks(k), chunks(k), pe_, ALU.mult), "k_end")
            rope_heads(qk[0:32, 0:8, :], att[0:32, :, :], "q")

        def rwkv_dve():
            stored(V, "g", 1)
            vdone(V.memset(tinv[:, :], 0.0), "t_zero")
            vdone(V.memset(tinv[:, 0:1024:33], 1.0), "t_one")
            stored(V, "kt", 1)
            vdone(V.memset(tt_all[:, :, :], 0.0), "tt_zero")
            V.wait_ge(sys_landed, 16)
            tv = tinv[:, :].rearrange("p (t s) -> p t s", s=32)
            nv = nsys[:, :].rearrange("p (s t) -> p s t", t=32)
            for q in range(31):
                if q:
                    V.wait_ge(substituted, q)
                shape = [P, 31 - q, q + 1]
                tmp = subst[:, 0:(31 - q) * (q + 1)].rearrange("p (t s) -> p t s", s=q + 1)
                tt(tmp, nv[:, q, q + 1:32].unsqueeze(2).to_broadcast(shape),
                   tv[:, q, 0:q + 1].unsqueeze(1).to_broadcast(shape), ALU.mult).then_inc(multiplied, 1)
                V.wait_ge(multiplied, q + 1)
                tt(tv[:, q + 1:32, 0:q + 1], tv[:, q + 1:32, 0:q + 1], tmp, ALU.add).then_inc(substituted, 1)
            V.wait_ge(substituted, 31)
            vdone(V.tensor_copy(subst[:, :].rearrange("p (s t) -> p s t", t=32),
                               tv.rearrange("p t s -> p s t")), "t_turned")
            for i in range(2):
                ps = full(V, "m1", i)
                vread(V.tensor_copy(xm[64 * i + 32:64 * i + 64, :, :],
                                   ps[64 * i + 32:64 * i + 64, :].rearrange("p (j s) -> p j s", s=32)), "m1", i)
            for i in range(2):
                ps = full(V, "m2", i)
                vread(V.tensor_copy(tt_all[64 * i:64 * i + 32, :, 32:64],
                                   ps[64 * i:64 * i + 32, :].rearrange("p (j s) -> p j s", s=32)), "m2", i)
            for i in range(2):
                ps = full(V, "sa0", i)
                vread(V.tensor_copy(sa0[:, i, :], ps[:, :]), "sa0", i)
            for i in range(2):
                stored(V, "sa0", i)
            for c in range(NCHUNK):
                half, blk = c % 2, c // 2
                hp = slice(64 * half, 64 * half + 64)
                if c:
                    ps = full(V, "sa", c)
                    vread(tt(sa[hp, :], sa0[hp, blk, :], ps[hp, :], ALU.add), "sa", c)
                else:
                    vdone(V.tensor_copy(sa[hp, :], sa0[hp, 0, :]), "sa_first")
                if c < NCHUNK - 1:
                    if c:
                        stored(V, "st", c - 1)
                        vdone(tt(sdec[:, :, :], state[:, :, :], pend[:, c:32:4, :].to_broadcast([P, NT, C]),
                                ALU.mult), f"sdec{c}")
                    ps = full(V, "st", c)
                    s3 = ps[:, 0:COLS].rearrange("p (t v) -> p t v", v=C)
                    if c:
                        step = tt(state[:, :, :], sdec[:, :, :], s3, ALU.add)
                    else:
                        step = V.tensor_copy(state[:, :, :], s3)
                    vread(step, "st", c)
                if c:
                    need(V, f"y_intra{c}")
                    ps = PAIRS[pair["ys", c]]
                    yc = y[:, :, c * C:(c + 1) * C]
                    vread(tt(yc, yc, ps[:, 0:COLS].rearrange("p (t s) -> p t s", s=C), ALU.add), "ys", c)
            for i in range(2):
                ps = full(V, "mean", i)
                yi = y[:, 4 * i:4 * i + 4, :]
                vread(V.scalar_tensor_tensor(yi, tiles(ps), -1.0 / C, yi, ALU.mult, ALU.add), "mean", i)
            for i in range(2):
                stored(V, "mean", i)
            vdone(tt(ysq[:, :, :], y[:, :, :], y[:, :, :], ALU.mult), "y_sq")
            ps = full(V, "var", 0)
            vread(V.tensor_scalar(hstat[0:RH, 0, :], ps[0:RH, 0:S], 1.0 / C, GN_EPS, ALU.mult, ALU.add), "var", 0)
            need(V, "gn_root")
            vdone(V.reciprocal(hstat[0:RH, 2, :], hstat[0:RH, 1, :]), "gn_inv")
            for i in range(2):
                ps = full(V, "vb", i)
                vread(tt(y[:, 4 * i:4 * i + 4, :], y[:, 4 * i:4 * i + 4, :], tiles(ps), ALU.mult), "vb", i)
            for i in range(2):
                stored(V, "vb", i)
            for t in range(NT):
                last = V.tensor_scalar(y[:, t, :], y[:, t, :], col("gn_gain", t), col("gn_bias", t),
                                       ALU.mult, ALU.add)
            vdone(last, "y_affine")
            for i in range(2):
                stored(V, "bonus", i)
            vdone(tt(y[:, :, :], y[:, :, :], bonus[:, :, :], ALU.add), "y_bonus")
            for i in range(2):
                stored(V, "g", i)
            vdone(tt(y[:, :, :], y[:, :, :], gate[:, :, :], ALU.mult), "y_gated")
            need(V, "mix_hi")
            vdone(tt(xl[:, NT:2 * NT, :], y[:, :, :], xh[:, NT:2 * NT, :].bitcast(F32), ALU.subtract), "mix_lo")

        def systems_act():
            index_act(0)
            for i in range(2):
                copy_tokens("bt", b_tok, i)
            for i in range(2):
                copy_tokens("kt", k_tok, i)
            for i in range(2):
                ps = full(A, "g", i)
                aread(A.copy(gate[:, 4 * i:4 * i + 4, :], tiles(ps)), "g", i)
            index_act(1)

        def rwkv_act():
            for i in range(2):
                ps = full(A, "akv", i)
                aread(A.copy(akv[:, i, :], ps[:, :]), "akv", i)
            for i in range(2):
                ps = full(A, "gt", i)
                aread(A.copy(gt[:, i, :], ps[:, :]), "gt", i)
            for c in range(NCHUNK):
                ps = full(A, "ys", c)
                step = A.copy(y[:, :, c * C:(c + 1) * C],
                              ps[:, COLS:2 * COLS].rearrange("p (t s) -> p t s", s=C))
                if c:
                    adone(step, f"y_intra{c}")
                else:
                    aread(step, "ys", 0)
            stored(A, "var", 0)
            adone(A.activation(hstat[0:RH, 1, :], hstat[0:RH, 0, :], ACT.Sqrt), "gn_root")
            need(A, "y_gated")
            adone(A.copy(xh[:, NT:2 * NT, :], y[:, :, :]), "mix_hi")

        def channel_rounds(name, lhs, rhs, width=S):
            for i in range(2):
                ps = fill(name, i)
                for t in range(4):
                    mm = T.matmul(ps[:, t * S:(t + 1) * S], lhs(4 * i + t), rhs, start=True, stop=True)
                filled(mm)

        def spread(name):
            for i in range(2):
                ps = fill(name, i)
                for t in range(4):
                    mm = T.matmul(ps[:, t * S:(t + 1) * S], to_channels[0:RH, 4 * i + t, :], hstat[0:RH, 2, :],
                                  start=True, stop=True)
                filled(mm)

        def head_sums(name, src):
            ps = fill(name, 0)
            for t in range(NT):
                mm = T.matmul(ps[0:RH, 0:S], to_heads[:, t, :], src[:, t, :], start=(t == 0), stop=(t == NT - 1))
            filled(mm)

        def within_heads(name, src):
            for i in range(2):
                ps = fill(name, i)
                for b in range(2):
                    t = 4 * i + 2 * b
                    mm = T.matmul(ps[:, b * COLS:(b + 1) * COLS], same_head,
                                  src[:, t:t + 2, :].rearrange("p t s -> p (t s)"), start=True, stop=True)
                filled(mm)

        def turn_tokens(name, tile_of):
            for i in range(TB):
                ps = fill(name, i)
                for t in range(NT):
                    mm = T.transpose(ps[:, t * P:(t + 1) * P], tile_of(t, i), ident)
                filled(mm)

        def win_pe():
            win_small()
            win_groups(GD, 17)
            T.wait_ge(lora_landed, 48)
            need(T, "tanh")
            channel_rounds("z", lambda t: lora_w[0:64, t * P:(t + 1) * P], lora[0:64, 0, :])
            win_groups(17, 25)
            channel_rounds("za", lambda t: lora_w[64:P, t * P:(t + 1) * P], lora[64:P, 0, :])
            win_groups(25, 33)
            need(T, "kk_sq")
            head_sums("kn", ksq)
            win_groups(33, 43)
            need(T, "kk_inv")
            spread("kb")
            win_groups(43, 49)
            need(T, "rk")
            within_heads("bonus", ksq)
            win_groups(49, 65)
            need(T, "v1")
            turn_tokens("vt", lambda t, i: v[:, t, i * P:(i + 1) * P])
            win_groups(65, 73)
            turn_tokens("at", lambda t, i: kk[:, t, i * P:(i + 1) * P])
            win_groups(73, NCH * GD)

        def systems_pe():
            T.wait_ge(in_read, NCH)
            for name, arr in (("bx", iclr), ("kx", k)):
                for i in range(4):
                    blk, par = i // 2, i % 2
                    hs = slice(64 * par, 64 * par + 64)
                    ps = fill(name, i)
                    for t in range(NT):
                        for half in range(2):
                            c = 2 * blk + half
                            mm = T.matmul(ps[64 * half:64 * half + 64, t * 2 * C:(t + 1) * 2 * C].rearrange(
                                              "p (a s) -> p a s", a=2),
                                          arr[hs, t, c * C:(c + 1) * C],
                                          ar[hs, :, t, c * C:(c + 1) * C],
                                          start=True, stop=True)
                    filled(mm)
            index_pe(0)
            need(T, "b_end")
            turn_tokens("bt", lambda t, i: iclr[:, t, i * P:(i + 1) * P])
            need(T, "k_end")
            turn_tokens("kt", lambda t, i: k[:, t, i * P:(i + 1) * P])
            channel_rounds("g", lambda t: lora_g[0:64, t * P:(t + 1) * P], lora[0:64, 1, :])
            index_pe(1)

        def rwkv_pe():
            for i in range(2):
                stored(T, "vt", i)
            for i in range(4):
                stored(T, "kx", i)

            def by_chunk(name, lhs, rhs, extra=None):
                for blk in range(2):
                    ps = fill(name, blk)
                    for jj in range(RH):
                        for half in range(2):
                            hs = slice(64 * half, 64 * half + 64)
                            mm = T.matmul(ps[hs, jj * C:(jj + 1) * C], lhs(hs, blk, jj), rhs(hs, blk, jj),
                                          start=True, stop=True)
                    filled(mm)

            def hcol(jj):
                h = 2 * (jj % NT) + jj // NT
                return slice(h * C, h * C + C)
            by_chunk("akv", lambda hs, b, jj: kx[hs, b * RH + jj, 0, :], lambda hs, b, jj: v_tok[hs, b, hcol(jj)])
            T.wait_ge(inv_landed, 16 * 6)
            for i in range(2):
                ps = fill("m1", i)
                lo, hi = slice(64 * i, 64 * i + 32), slice(64 * i + 32, 64 * i + 64)
                for j in range(2 * RH):
                    mm = T.matmul(ps[hi, j * 32:(j + 1) * 32], bx[lo, j, 0, 32:64], t_plain[lo, j, :],
                                  start=True, stop=True)
                filled(mm)
            for i in range(2):
                stored(T, "m1", i)
                ps = fill("m2", i)
                lo, hi = slice(64 * i, 64 * i + 32), slice(64 * i + 32, 64 * i + 64)
                for j in range(2 * RH):
                    mm = T.matmul(ps[lo, j * 32:(j + 1) * 32], xm[hi, j, :], tt_all[hi, j, 32:64],
                                  start=True, stop=True)
                filled(mm)
            for i in range(2):
                stored(T, "m2", i)
                stored(T, "akv", i)
                stored(T, "at", i)
            by_chunk("sa0", lambda hs, b, jj: tt_all[hs, b * RH + jj, :], lambda hs, b, jj: akv[hs, b, jj * C:(jj + 1) * C])
            for blk in range(2):
                ps = fill("gt", blk)
                for half in range(2):
                    hs = slice(64 * half, 64 * half + 64)
                    for jj in range(RH):
                        par, t = jj // NT, jj % NT
                        mm = T.matmul(ps[64 * par:64 * par + 64, half * COLS + t * C:half * COLS + (t + 1) * C],
                                      a_tok[hs, blk, hcol(jj)], tt_all[hs, blk * RH + jj, :], start=True, stop=True)
                filled(mm)
            for i in range(2):
                stored(T, "gt", i)
                stored(T, "bt", i)
                stored(T, "kt", i)
                stored(T, "sa0", i)
            for c in range(NCHUNK):
                half, blk = c % 2, c // 2
                hs = slice(64 * half, 64 * half + 64)
                if c:
                    stored(T, "st", c - 1)
                    ps = fill("sa", c)
                    for jj in range(RH):
                        par, t = jj // NT, jj % NT
                        ch = slice(64 * par, 64 * par + 64)
                        mm = T.matmul(ps[hs, jj * C:(jj + 1) * C],
                                      gt[ch, blk, half * COLS + t * C:half * COLS + (t + 1) * C], state[ch, t, :],
                                      start=True, stop=True)
                    filled(mm)
                ps = fill("ys", c)
                if c:
                    for jj in range(RH):
                        par, t = jj // NT, jj % NT
                        ch = slice(64 * par, 64 * par + 64)
                        T.matmul(ps[ch, t * C:(t + 1) * C], state[ch, t, :], ar[ch, 1, t, c * C:(c + 1) * C],
                                 start=True, stop=True)
                    stored(T, "sa", c)
                else:
                    need(T, "sa_first")
                for jj in range(RH):
                    par, t = jj // NT, jj % NT
                    ch = slice(64 * par, 64 * par + 64)
                    out_ = ps[ch, COLS + t * C:COLS + (t + 1) * C]
                    j = blk * RH + jj
                    T.matmul(out_, sa[hs, jj * C:(jj + 1) * C], bx[hs, j, 1, :], start=True, stop=False)
                    mm = T.matmul(out_, v_tok[hs, blk, hcol(jj)], kx[hs, j, 1, :], start=False, stop=True)
                filled(mm)
                if c < NCHUNK - 1:
                    ps = fill("st", c)
                    for jj in range(RH):
                        par, t = jj // NT, jj % NT
                        ch = slice(64 * par, 64 * par + 64)
                        out_ = ps[ch, t * C:(t + 1) * C]
                        T.matmul(out_, b_tok[hs, blk, hcol(jj)], sa[hs, jj * C:(jj + 1) * C], start=True, stop=False)
                        mm = T.matmul(out_, k_tok[hs, blk, hcol(jj)], v_tok[hs, blk, hcol(jj)], start=False, stop=True)
                    filled(mm)
            for c in range(NCHUNK):
                stored(T, "ys", c)
            within_heads("mean", y)
            need(T, "y_sq")
            head_sums("var", ysq)
            need(T, "gn_inv")
            spread("vb")

        def mix_sp_dmas(eng):
            for i in range(4):
                stored(eng, "bx", i)
            for q in range(4):
                half = q % 2
                eng.dma_start(n_dram[q].rearrange("j s t -> s j t"),
                              bx[32 * q:32 * q + 32, :, 0, 32 * half:32 * half + 32]).then_inc(sys_stored, 16)
            eng.wait_ge(sys_stored, 64)
            eng.dma_start(nsys[:, :], n_dram.rearrange("q j s t -> (q j) (s t)")).then_inc(sys_landed, 16)
            full(eng, "pt", 2)
            out_load(eng, 0, SLOTS)
            need(eng, "t_turned")
            need(eng, "tt_zero")
            eng.dma_start(t_dram[0].rearrange("q j s t -> (q j) (s t)"), subst[:, :]).then_inc(inv_stored, 16)
            eng.dma_start(t_dram[1].rearrange("q j s t -> (q j) (s t)"), tinv[:, :]).then_inc(inv_stored, 16)
            eng.wait_ge(inv_stored, 32)
            for q in range(4):
                half = q % 2
                eng.dma_start(tt_all[32 * q:32 * q + 32, :, 32 * half:32 * half + 32],
                              t_dram[0, q].rearrange("j s t -> s j t")).then_inc(inv_landed, 16)
                if half == 0:
                    eng.dma_start(t_plain[32 * q:32 * q + 32, :, :],
                                  t_dram[1, q].rearrange("j t s -> t j s")).then_inc(inv_landed, 16)

        def out_pe():
            need(T, "mix_lo")
            for i in range(TB):
                stored(T, "pv", i)
            for c in range(DC):
                if c >= 2:
                    T.wait_ge(x_added, DC + c - 1)
                for j in range(GD):
                    project_tokens((psA, psB)[c % 2], xh, xl, w0_out, 0, 0, c * GD + j, j * KT,
                                   j == 0, j == GD - 1)

        def out_act():
            for g in range(DC * GD):
                split_hi(w0_out, 0, 0, g)

        def out_dve():
            def add(c):
                V.wait_ge(group_used, w0_out + (c + 1) * GD)
                xc = x[:, :, c * COLS:(c + 1) * COLS]
                tt(xc, (psA, psB)[c % 2][:, :, :], xc, ALU.add).then_inc(x_added, 1)
            for g in range(DC * GD):
                split_lo(w0_out, 0, 0, g)
                if g > GD and g % GD == SLOTS - 1:
                    add(g // GD - 1)
            add(DC - 1)

        def mix_load_all(sp):
            mix_load(sp)
            mix_sp_dmas(sp)
            out_load(sp, SLOTS, DC * GD)

        def mix_act():
            for j in range(SLOTS):
                split_hi(m0, 0, 0, j, SMALL)
            norm_act(1)
            norm_hi(1)
            win_act()
            systems_act()
            attention_act()
            rwkv_act()
            out_act()

        def mix_dve():
            for j in range(SLOTS):
                split_lo(m0, 0, 0, j, SMALL)
            norm_dve(1)
            norm_lo(1)
            win_dve()
            rwkv_systems()
            attention_dve()
            rwkv_dve()
            out_dve()

        def mix_pe():
            turn_norm(1)
            win_pe()
            systems_pe()
            attention_pe()
            rwkv_pe()
            out_pe()

        added_before_down = [0, 2 * DC]

        ffn1, ffn2 = a["ffn1"], a["ffn2"]
        base2 = FFN_GROUPS + MIX_GROUPS

        block = ctx.enter_context(nc.Block())

        @block.sync
        def _(sp):
            xv = a["x"].rearrange("(b p) d -> p b d", p=P)
            sp.dma_start(x[:, :, :], xv).then_inc(x_landed, 16)
            sp.dma_start(consts[:, :], a["consts"]).then_inc(const_landed, 16)
            n = 0
            for name in ("ffn1_norm", "mix_norm", "ffn2_norm"):
                sp.dma_start(prow[n:n + KD, :], a[name].rearrange("(k p) -> k p", p=P)).then_inc(const_landed, 16)
                n += KD
            for name in _CHANNELS:
                sp.dma_start(prow[n:n + NT, :], a[name].rearrange("(k p) -> k p", p=P)).then_inc(const_landed, 16)
                n += NT
            for row, col_, name in ((0, 0, "rwkv_mu_w"), (0, 64, "rwkv_mu_a"), (1, 0, "rwkv_mu_g"), (1, 64, "rwkv_mu_g")):
                sp.dma_start(prow2[row:row + 1, col_:col_ + 64], a[name].rearrange("(o n) -> o n", o=1))\
                    .then_inc(const_landed, 16)
            ffn_load(sp, 0, 0, *ffn1)
            mix_load_all(sp)
            ffn_load(sp, 1, base2, *ffn2)
            sp.wait_ge(x_added, (3) * DC)
            sp.dma_start(fgain[:, :], a["final_norm"].rearrange("(o d) -> o d", o=1).to_broadcast([P, D]))\
                .then_inc(gain_landed, 16)
            sp.wait_ge(out_ready, TB)
            sp.dma_start(out.rearrange("(b p) d -> p b d", p=P), xs[:, :, :]).then_inc(out_stored, 16)
            sp.wait_ge(out_stored, 16)

        @block.scalar
        def _(act_engine):
            for j in range(SLOTS):
                split_hi(0, 0, PER, j)
            norm_act(0)
            norm_hi(0)
            ffn_act(0, 0)
            mix_act()
            for j in range(SLOTS):
                split_hi(base2, 0, PER, j)
            norm_act(2)
            norm_hi(2)
            ffn_act(1, base2)
            norm_act(3)

        @block.vector
        def _(dve):
            dve.wait_ge(params_turned, 1)
            nc.vector.tensor_copy(pcol2[:, :], psM[:, P:P + 2])
            nc.vector.tensor_copy(pcol[:, :], psM[:, 0:P]).then_inc(params_ready, 1)
            for j in range(SLOTS):
                split_lo(0, 0, PER, j)
            norm_dve(0)
            norm_lo(0)
            ffn_dve(0, 0)
            mix_dve()
            for j in range(SLOTS):
                split_lo(base2, 0, PER, j)
            norm_dve(2)
            norm_lo(2)
            ffn_dve(1, base2)
            norm_dve(3)
            dve.wait_ge(gain_landed, 16)
            dve.wait_ge(xs_ready, TB * (4))
            for tb in range(TB):
                nc.vector.tensor_tensor(xs[:, tb, :], xs[:, tb, :], fgain[:, :], ALU.mult).then_inc(out_ready, 1)

        @block.tensor
        def _(pe):
            pe.wait_ge(const_landed, 16 * (8 + len(_CHANNELS)))
            nc.tensor.transpose(psM[:, 0:P], prow[:, :], ident)
            nc.tensor.transpose(psM[:, P:P + 2], prow2[:, :], ident[0:2, 0:2]).then_inc(params_turned, 1)
            turn_norm(0)
            ffn_pe(0, 0)
            mix_pe()
            turn_norm(2)
            ffn_pe(1, base2)


_CHANNELS = ["rwkv_mu_r", "rwkv_mu_k", "rwkv_mu_v", "rwkv_w0", "rwkv_a0", "rwkv_k_k", "rwkv_k_a", "rwkv_r_k",
             "rwkv_gn_gain", "rwkv_gn_bias"]


def launch(nc, args, out):
    a = {}
    for name, v in args.items():
        a[name] = v if name == "final_norm" else v[0]
    a["rwkv_r_k"] = a["rwkv_r_k"].rearrange("h n -> (h n)")
    for f in ("ffn1", "ffn2"):
        a[f] = (a[f + "_w_gate"], a[f + "_w_up"], a[f + "_w_down"])
    a["consts"] = nc.inline_tensor(constants(), "constants").ap()
    build(nc, a, out[0])


def kernel(**inputs):
    import numpy as _np
    import concourse.bacc as _bacc
    from concourse import mybir as _mybir
    from concourse.bass_utils import run_bass_kernel_spmd as _run

    nc = _bacc.Bacc("TRN2", target_bir_lowering=False, num_devices=1)
    arrays, args = {}, {}
    for name, v in inputs.items():
        v = _np.ascontiguousarray(v)
        arrays[f"in_{name}"] = v
        args[name] = nc.dram_tensor(f"in_{name}", v.shape, _mybir.dt.from_np(v.dtype), kind="ExternalInput").ap()
    out = nc.dram_tensor("out", (1, S, D), F32, kind="ExternalOutput").ap()
    launch(nc, args, out)
    r = _run(nc, [arrays], core_ids=[0])
    return r.results[0]["out"]
```

```python
from contextlib import ExitStack

import numpy as np

import concourse.bass as bass
from concourse import mybir

F32 = mybir.dt.float32
F32R = mybir.dt.float32r
ALU = mybir.AluOpType
ACT = mybir.ActivationFunctionType
AX = mybir.AxisListType

P = 128
D = 2048
S = 256
TB = S // P
F = 5632
COLS = 512
KD = D // P
KF = F // P
NORM_EPS = 1e-6
AW = 1024
RW = 1024
NT = RW // P

SLOTS = 4
KT = 2
GD = KD // KT
GF = KF // KT
FC = F // COLS
DC = D // COLS

MIX_GROUPS = 11 * GD + DC * GD
AH = 8
KVW = 256
ATT_SCALE = float(P) ** -0.5
IDX_HEADS = 8
IDX_SCALE = (IDX_HEADS ** -0.5) * (64 ** -0.5)
TOPK = 64
TAKEN = -float(2.0 ** 127)
HIDDEN = -float(2.0 ** 126)
OFF = -1e30
RH = 16
C = 64
NCHUNK = S // C
GN_EPS = 64e-5
DECAY = float(np.exp(-0.5))


CONST_WIDTH = 2816


def constants():
    t = np.zeros((P, CONST_WIDTH), np.float32)
    p = np.arange(P)
    s = np.arange(S)
    t[:, 0:128] = np.eye(P)
    t[:, 128:256] = p[:, None] // 64 == p[None, :] // 64
    head = 2 * np.arange(NT)[:, None] + (p // 64)[None, :]
    t[:, 256:384] = (head.T[:, :, None] == np.arange(RH)).reshape(P, NT * RH)
    t[:, 384:448] = np.arange(C)[None, :] > (p % 64)[:, None]
    t[:, 448:512] = np.arange(C)[None, :] >= (p % 64)[:, None]
    t[:, 512:768] = s[None, :] % C != 0

    def rotary(width, rows_, at):
        rot = width // 4
        half = rot // 2
        freq = np.float32(500000.0) ** (-(np.arange(half, dtype=np.float32) * np.float32(2.0) / np.float32(rot)))
        ang = s.astype(np.float32)[:, None] * freq[None, :].astype(np.float32)
        cos, sin = np.cos(ang).astype(np.float32).T, np.sin(ang).astype(np.float32).T
        for q in range(rows_):
            j = q % width
            t[q, at:at + S] = cos[j % half] if j < rot else 1.0
            if j < rot:
                t[q, at + S:at + 2 * S] = -sin[j] if j < half else sin[j - half]

    rotary(64, P, 768)
    rotary(P, 32, 1280)
    t[0:RH, 1792:2816] = (head[None, :, :] == np.arange(RH)[:, None, None]).reshape(RH, NT * P)
    return t


def build(nc, a, out):
    with ExitStack() as ctx:
        address = {}

        def sb(name, shape, dt=F32):
            handle = ctx.enter_context(nc.sbuf_tensor(name, shape, dt))
            address[name] = nc.sbuf_base - 4 * int(np.prod(shape[1:]))
            return handle

        def pb(name, shape):
            return ctx.enter_context(nc.psum_tensor(name, shape, F32))

        def sem(name):
            return ctx.enter_context(nc.semaphore(name))

        x = sb("x", [P, TB, D])
        raw = sb("raw", [P, SLOTS, KT, COLS])
        whi = sb("whi", [P, SLOTS, KT, COLS], F32R)
        wlo = sb("wlo", [P, SLOTS, KT, COLS], F32R)
        xh = sb("xh", [P, KD, S], F32R)
        xl = sb("xl", [P, KD, S], F32R)
        consts = sb("consts", [P, CONST_WIDTH])
        ident = consts[:, 0:128]
        same_head = consts[:, 128:256]
        to_heads = consts[:, 256:384].rearrange("p (t h) -> p t h", h=RH)
        mask2 = consts[:, 384:512]
        keep = consts[:, 512:768]
        cos_i, sin_i = consts[:, 768:1024], consts[:, 1024:1280]
        cos_q, sin_q = consts[0:32, 1280:1536], consts[0:32, 1536:1792]
        to_channels = consts[:, 1792:2816].rearrange("p (t c) -> p t c", c=P)
        prow = sb("prow", [P, P])
        pcol = sb("pcol", [P, P])
        prow2 = sb("prow2", [2, P])
        pcol2 = sb("pcol2", [P, 2])
        squares = sb("squares", [P, TB, DC])
        ss = sb("ss", [P, 6])
        stage = sb("stage", [P, 2, TB, COLS])
        silu, act = stage[:, 0], stage[:, 1]
        UNIT = NT * S * 4
        arena = sb("arena", [P, 11 * UNIT // 4])

        def at(name, shape, where, unit=0, plus=0, dt=F32):
            return nc.alloc_sbuf_tensor_at(name, shape, dt, offset=address[where.name] + unit * UNIT + plus)

        KB = 1024
        xs = at("xs", [P, TB, D], arena)
        fgain = at("fgain", [P, D], xl)
        hh = at("hh", [P, KF, S], arena, dt=F32R)
        hl = at("hl", [P, KF, S], arena, plus=KF * S * 4, dt=F32R)
        ar = at("ar", [P, 2, NT, S], arena, 0)
        kk, r = ar[:, 0, :, :], ar[:, 1, :, :]
        k, v = at("k", [P, NT, S], arena, 2), at("v", [P, NT, S], arena, 3)
        temp = at("temp", [P, 5, S], arena, 7)
        qk = at("qk", [P, 10, S], arena, plus=61 * KB)
        vals = at("vals", [P, TB, S], arena, plus=71 * KB)
        qi = at("qi", [P, 5, S], arena, plus=73 * KB)
        lora = at("lora", [P, 2, S], arena, plus=78 * KB)
        lora_w = at("lora_w", [P, RW], arena, plus=80 * KB)
        lora_g = at("lora_g", [P, RW], arena, plus=84 * KB)
        widx = sb("widx", [P, TB, IDX_HEADS])
        att = (at("att0", [P, AH, P], raw, 1, 4 * KB), at("att1", [P, AH, S], raw, 0))
        turned = at("turned", [P, AH, S], raw, 0)
        relu = (at("relu0", [P, IDX_HEADS, P], stage, 0), at("relu1", [P, IDX_HEADS, S], raw, 0))
        prob_t = at("prob_t", [P, TB, AH, P], xl, 1)
        score = at("score", [P, TB, S], arena, 7)
        top8 = at("top8", [P, 8], arena, 7, 2 * KB)
        top = [at(f"top{i}", [P, 3 * AH], arena, 7, 2 * KB + 64 + 96 * i) for i in range(TB)]
        ksq = at("ksq", [P, NT, S], arena, 3)
        sw = at("sw", [P, NT, S], arena, 4)
        pdec = at("pdec", [P, NT, S], arena, 4)
        lsum = at("lsum", [P, NT, S], arena, 5)
        pinv = at("pinv", [P, NT, S], arena, 5)
        bonus = at("bonus", [P, NT, S], arena, 5)
        iclr = at("iclr", [P, NT, S], arena, 6)
        gate = at("gate", [P, NT, S], xh, 1)
        hstat = at("hstat", [P, 3, S], stage, plus=4 * KB)
        ka1 = sb("ka1", [P, NT])
        pend = sb("pend", [P, NT * NCHUNK, 1])
        a_tok = at("a_tok", [P, TB, RW], arena, 3)
        v_tok = at("v_tok", [P, TB, RW], arena, 4)
        b_tok = at("b_tok", [P, TB, RW], arena, 0)
        k_tok = at("k_tok", [P, TB, RW], arena, 6)
        bx = at("bx", [P, 2 * RH, 2, C], whi)
        kx = at("kx", [P, 2 * RH, 2, C], wlo)
        tt_all = at("tt_all", [P, 2 * RH, C], arena, 2)
        nsys = at("nsys", [P, 1024], arena, 10)
        tinv = at("tinv", [P, 1024], arena, 10, 4 * KB)
        subst = at("subst", [P, 1024], stage, 0, 4 * KB)
        t_plain = at("t_plain", [P, 2 * RH, 32], raw, 1)
        xm = at("xm", [P, 2 * RH, 32], arena, 9, KB)
        akv = at("akv", [P, TB, RW], xl, 1)
        sa0 = at("sa0", [P, TB, RW], stage)
        gt = at("gt", [P, TB, RW], arena, 3)
        state = at("state", [P, NT, C], arena, 10)
        sdec = at("sdec", [P, NT, C], arena, 10, 2 * KB)
        sa = at("sa", [P, RW], arena, 10, 4 * KB)
        y = at("y", [P, NT, S], arena, 2)
        ysq = at("ysq", [P, NT, S], arena, 3)
        n_dram = nc.dram_tensor("n_dram", [4, 2 * RH, 32, 32], F32, kind="Internal").ap()
        t_dram = nc.dram_tensor("t_dram", [2, 4, 2 * RH, 32, 32], F32, kind="Internal").ap()

        psA = pb("psA", [P, TB, COLS])
        psB = pb("psB", [P, TB, COLS])
        psT = pb("psT", [P, 2 * COLS])
        psM = pb("psM", [P, 2 * COLS])
        pA, pB = (ps[:, :, :].rearrange("p b c -> p (b c)") for ps in (psA, psB))
        pT, pM = psT[:, :], psM[:, :]

        PER = 2 * GD
        m0 = FC * PER + DC * GF
        raw_landed = [sem(f"raw_landed{i}") for i in range(SLOTS)]
        hi_ready = sem("hi_ready")
        lo_ready = sem("lo_ready")
        group_used = sem("group_used")
        const_landed = sem("const_landed")
        tables_landed = sem("tables_landed")
        params_turned = sem("params_turned")
        params_ready = sem("params_ready")
        x_landed = [sem(f"x_landed{c}") for c in range(DC)]
        square_ready = sem("square_ready")
        norm_step = sem("norm_step")
        root_ready = sem("root_ready")
        xs_ready = [sem(f"xs_ready{tb}") for tb in range(TB)]
        xs_turned = sem("xs_turned")
        xh_ready = sem("xh_ready")
        xl_ready = sem("xl_ready")
        silu_ready = sem("silu_ready")
        act_ready = sem("act_ready")
        act_turned = sem("act_turned")
        hh_ready = sem("hh_ready")
        hl_ready = sem("hl_ready")
        x_added = sem("x_added")
        gain_landed = sem("gain_landed")
        out_ready = sem("out_ready")
        out_stored = sem("out_stored")
        in_read = sem("in_read")
        a_rest = sem("a_rest")
        lora_landed = sem("lora_landed")
        round_full = sem("round_full")
        round_read = [sem(f"round_read{i}") for i in range(4)]
        sys_stored = sem("sys_stored")
        sys_landed = sem("sys_landed")
        inv_stored = sem("inv_stored")
        inv_landed = sem("inv_landed")
        multiplied = sem("multiplied")
        substituted = sem("substituted")

        def load_group(sp, src, base, n, per, j, ncol=COLS):
            g = base + j
            slot = g % SLOTS
            if not (isinstance(n, int) and g + n * per < SLOTS):
                sp.wait_ge(hi_ready, n * per + g - SLOTS + 1)
                sp.wait_ge(lo_ready, n * per + g - SLOTS + 1)
            sp.dma_start(raw[:, slot, :, 0:ncol], src).then_inc(raw_landed[slot], 16)

        def split_hi(base, n, per, j, ncol=COLS):
            g = base + j
            slot = g % SLOTS
            extra = 48 * min(max(g // SLOTS + 1 - m0 // SLOTS, 0), GD // SLOTS)
            nc.scalar.wait_ge(raw_landed[slot], n * (16 * per // SLOTS) + 16 * (g // SLOTS + 1) + extra)
            if not (isinstance(n, int) and g + n * per < SLOTS):
                nc.scalar.wait_ge(group_used, n * per + g - SLOTS + 1)
            nc.scalar.copy(whi[:, slot, :, 0:ncol], raw[:, slot, :, 0:ncol]).then_inc(hi_ready, 1)

        def split_lo(base, n, per, j, ncol=COLS):
            g = base + j
            slot = g % SLOTS
            nc.vector.wait_ge(hi_ready, n * per + g + 1)
            if not (isinstance(n, int) and g + n * per < SLOTS):
                nc.vector.wait_ge(group_used, n * per + g - SLOTS + 1)
            nc.vector.tensor_tensor(wlo[:, slot, :, 0:ncol], raw[:, slot, :, 0:ncol],
                                    whi[:, slot, :, 0:ncol].bitcast(F32), ALU.subtract).then_inc(lo_ready, 1)

        def wait_group(base, n, per, j):
            nc.tensor.wait_ge(lo_ready, n * per + base + j + 1)

        def project_tokens(ps, h, l, base, n, per, j, k0, first, last, ncol=COLS):
            wait_group(base, n, per, j)
            slot = (base + j) % SLOTS
            for t in range(KT):
                for tb in range(TB):
                    tok = slice(tb * P, tb * P + P)
                    for p, (lhs, rhs) in enumerate(((h, whi), (h, wlo), (l, whi))):
                        mm = nc.tensor.matmul(ps[:, tb, 0:ncol], lhs[:, k0 + t, tok], rhs[:, slot, t, 0:ncol],
                                              start=(first and t == 0 and p == 0),
                                              stop=(last and t == KT - 1 and p == 2))
            mm.then_inc(group_used, 1)

        def rows(w, k0):
            return w[k0 * P:(k0 + KT) * P, :].rearrange("(t p) n -> p t n", p=P)

        def squares_act(f, c):
            if f == 0:
                nc.scalar.wait_ge(x_landed[c], 16)
            else:
                nc.scalar.wait_ge(x_added, DC * (f - 1) + c + 1)
            for tb in range(TB):
                nc.scalar.activation(silu[:, tb, :], x[:, tb, c * COLS:(c + 1) * COLS], ACT.Square,
                                     accum_out=squares[:, tb, c:c + 1]).then_inc(square_ready, 1)
                nc.scalar.wait_ge(square_ready, TB * (DC * f + c) + tb + 1)

        HALF = D // 2

        def norm_act(f):
            for c in range(DC):
                if f == 0 or c == DC - 1:
                    squares_act(f, c)
            nc.scalar.wait_ge(norm_step, 3 * f + 2)
            nc.scalar.activation(ss[:, 2:4], ss[:, 0:2], ACT.Sqrt).then_inc(root_ready, 1)
            if f < 3:
                nc.scalar.wait_ge(norm_step, 3 * f + 3)
                for h in range(2):
                    nc.scalar.activation(xs[:, 0, h * HALF:(h + 1) * HALF], x[:, 0, h * HALF:(h + 1) * HALF],
                                         ACT.Copy, scale=ss[:, 4:5]).then_inc(xs_ready[0], 1)

        def norm_dve(f):
            nc.vector.wait_ge(square_ready, TB * DC * (f + 1))
            nc.vector.tensor_reduce(ss[:, 0:2], squares[:, :, :], AX.X, ALU.add).then_inc(norm_step, 1)
            nc.vector.wait_ge(norm_step, 3 * f + 1)
            nc.vector.tensor_scalar(ss[:, 0:2], ss[:, 0:2], 1.0 / D, NORM_EPS, ALU.mult, ALU.add)\
                .then_inc(norm_step, 1)
            nc.vector.wait_ge(root_ready, f + 1)
            nc.vector.reciprocal(ss[:, 4:6], ss[:, 2:4]).then_inc(norm_step, 1)
            nc.vector.wait_ge(norm_step, 3 * f + 3)
            if f < 3:
                for h in range(2):
                    nc.vector.tensor_scalar(xs[:, 1, h * HALF:(h + 1) * HALF], x[:, 1, h * HALF:(h + 1) * HALF],
                                            ss[:, 5:6], None, ALU.mult).then_inc(xs_ready[1], 1)

        QK = 4

        def turn_norm(f):
            for q in range(KD // QK):
                for tb in range(TB):
                    nc.tensor.wait_ge(xs_ready[tb], 2 * f + q // 2 + 1)
                if q >= 2 or f:
                    nc.tensor.wait_ge(xl_ready, (KD // QK) * f + max(q - 1, 0))
                ps = (psT, psM)[q % 2]
                for t in range(QK):
                    for tb in range(TB):
                        k = q * QK + t
                        mm = nc.tensor.transpose(ps[:, t * S + tb * P:t * S + tb * P + P],
                                                 xs[:, tb, k * P:k * P + P], ident)
                mm.then_inc(xs_turned, 1)

        def norm_hi(f):
            for q in range(KD // QK):
                nc.scalar.wait_ge(xs_turned, (KD // QK) * f + q + 1)
                if q == 0:
                    nc.scalar.wait_ge(params_ready, 1)
                ps = (psT, psM)[q % 2]
                for t in range(QK):
                    k = q * QK + t
                    g = f * KD + k
                    mm = nc.scalar.activation(xh[:, k, :], ps[:, t * S:t * S + S], ACT.Copy, scale=pcol[:, g:g + 1])
                mm.then_inc(xh_ready, 1)

        def norm_lo(f):
            for q in range(KD // QK):
                nc.vector.wait_ge(xh_ready, (KD // QK) * f + q + 1)
                ps = (psT, psM)[q % 2]
                for t in range(QK):
                    k = q * QK + t
                    g = f * KD + k
                    mm = nc.vector.scalar_tensor_tensor(xl[:, k, :], ps[:, t * S:t * S + S], pcol[:, g:g + 1],
                                                        xh[:, k, :].bitcast(F32), ALU.mult, ALU.subtract)
                mm.then_inc(xl_ready, 1)


        def ffn_load(sp, f, base, w_gate, w_up, w_down):
            def chunk(n):
                col = n * COLS
                for j in range(GD):
                    load_group(sp, rows(w_gate, j * KT)[:, :, bass.ds(col, COLS)], base, n, PER, j)
                for j in range(GD):
                    load_group(sp, rows(w_up, j * KT)[:, :, bass.ds(col, COLS)], base, n, PER, GD + j)
            chunk(0)
            with sp.Fori(1, FC) as n:
                chunk(n)
            down = base + FC * PER
            with sp.Fori(0, DC // 2) as m:
                for j in range(2 * GF):
                    col = (2 * m + j // GF) * COLS
                    load_group(sp, rows(w_down, (j % GF) * KT)[:, :, bass.ds(col, COLS)], down, m, 2 * GF, j)

        def ffn_act(f, base):
            def silu_gate(n):
                nc.scalar.wait_ge(group_used, n * PER + (base + GD))
                if not (isinstance(n, int) and n == 0 and f == 0):
                    nc.scalar.wait_ge(act_ready, n + f * FC)
                nc.scalar.activation(silu[:, :, :], psA[:, :, :], ACT.Silu).then_inc(silu_ready, 1)

            def turned_hi(n):
                nc.scalar.wait_ge(act_turned, n + (f * FC + 1))
                nc.scalar.copy(hh[:, bass.ds(n * 4, 4), :], psT[:, :].rearrange("p (t s) -> p t s", t=4))\
                    .then_inc(hh_ready, 1)

            def chunk(n, first):
                for j in range(PER):
                    if not (first and j < SLOTS):
                        split_hi(base, n, PER, j)
                    if j == GD + SLOTS - 1:
                        if not first:
                            turned_hi(n - 1)
                        silu_gate(n)
            chunk(0, True)
            chunk(1, False)
            with nc.scalar.Fori(2, FC) as n:
                chunk(n, False)
            down = base + FC * PER
            for j in range(SLOTS):
                split_hi(down, 0, 2 * GF, j)
            turned_hi(FC - 1)
            for j in range(SLOTS, DC * GF):
                split_hi(down, 0, 0, j)
                if j > GF and j % GF == 2 * SLOTS - 1:
                    squares_act(2 * f + 1, j // GF - 1)

        def ffn_dve(f, base):
            def gate_up(n):
                nc.vector.wait_ge(silu_ready, n + (f * FC + 1))
                nc.vector.wait_ge(group_used, n * PER + (base + PER))
                if not (isinstance(n, int) and n == 0 and f == 0):
                    nc.vector.wait_ge(act_turned, n + f * FC)
                nc.vector.tensor_tensor(act[:, :, :], psB[:, :, :], silu[:, :, :], ALU.mult).then_inc(act_ready, 1)

            def turned_lo(n):
                nc.vector.wait_ge(hh_ready, n + (f * FC + 1))
                nc.vector.tensor_tensor(hl[:, bass.ds(n * 4, 4), :], psT[:, :].rearrange("p (t s) -> p t s", t=4),
                                        hh[:, bass.ds(n * 4, 4), :].bitcast(F32), ALU.subtract)\
                    .then_inc(hl_ready, 1)

            def chunk(n, first):
                for j in range(PER):
                    if not (first and j < SLOTS):
                        split_lo(base, n, PER, j)
                    if j == SLOTS - 1 and not first:
                        gate_up(n - 1)
                    if j == GD + SLOTS - 1 and not first:
                        turned_lo(n - 1)
            chunk(0, True)
            chunk(1, False)
            with nc.vector.Fori(2, FC) as n:
                chunk(n, False)
            down = base + FC * PER
            for j in range(SLOTS):
                split_lo(down, 0, 2 * GF, j)
            gate_up(FC - 1)
            turned_lo(FC - 1)
            for c in range(DC):
                for j in range(GF):
                    if c or j >= SLOTS:
                        split_lo(down, 0, 0, c * GF + j)
                    if c and j == SLOTS - 1:
                        add_down(f, down, c - 1)
            add_down(f, down, DC - 1)

        def add_down(f, down, c):
            nc.vector.wait_ge(group_used, down + (c + 1) * GF)
            ps = (psA, psB)[c % 2]
            nc.vector.scalar_tensor_tensor(x[:, :, c * COLS:(c + 1) * COLS], ps[:, :, :], 0.5,
                                           x[:, :, c * COLS:(c + 1) * COLS], ALU.mult, ALU.add)\
                .then_inc(x_added, 1)

        def ffn_pe(f, base):
            def turn(n):
                nc.tensor.wait_ge(act_ready, n + (f * FC + 1))
                if not (isinstance(n, int) and n == 0 and f == 0):
                    nc.tensor.wait_ge(hl_ready, n + f * FC)
                for t in range(4):
                    for tb in range(TB):
                        mm = nc.tensor.transpose(psT[:, t * S + tb * P:t * S + tb * P + P],
                                                 act[:, tb, t * P:t * P + P], ident)
                mm.then_inc(act_turned, 1)

            def chunk(n, first):
                if not first:
                    nc.tensor.wait_ge(silu_ready, n + f * FC)
                for j in range(GD):
                    if first and j % 2 == 0:
                        nc.tensor.wait_ge(xl_ready, 4 * (2 * f) + j // 2 + 1)
                    project_tokens(psA, xh, xl, base, n, PER, j, j * KT, j == 0, j == GD - 1)
                if not first:
                    turn(n - 1)
                for j in range(GD):
                    project_tokens(psB, xh, xl, base, n, PER, GD + j, j * KT, j == 0, j == GD - 1)
            chunk(0, True)
            chunk(1, False)
            with nc.tensor.Fori(2, FC) as n:
                chunk(n, False)
            down = base + FC * PER
            nc.tensor.wait_ge(silu_ready, (f + 1) * FC)
            nc.tensor.wait_ge(hl_ready, (f + 1) * FC - 1)
            for c in range(DC):
                if c >= 2:
                    nc.tensor.wait_ge(x_added, added_before_down[f] + c - 1)
                for j in range(GF):
                    if c == 0 and j == SLOTS:
                        turn(FC - 1)
                    if c == 0 and j == (KF - 4) // KT:
                        nc.tensor.wait_ge(hl_ready, (f + 1) * FC)
                    project_tokens((psA, psB)[c % 2], hh, hl, down, 0, 0, c * GF + j, j * KT,
                                   j == 0, j == GF - 1)

        FFN_GROUPS = FC * PER + DC * GF
        ki_col, wi_col, rkv_col = 2048, 2112, 2120
        lora_col = rkv_col + 3 * RW
        KI2, LORA, WI = 0, P, P + 192
        SMALL = WI + IDX_HEADS
        NCH = 11
        in_col = [None] + [rkv_col + i * COLS for i in (2, 3, 0, 1, 4, 5)] + [AW, AW + 2 * KVW, 0, COLS]
        m0 = FFN_GROUPS
        w0_out = m0 + NCH * GD

        def in_rows(k0, lo, hi):
            return rows(a["w_in"], k0)[:, :, lo:hi]

        def mix_load(sp):
            sp.dma_start(consts[:, P:], a["consts"][:, P:]).then_inc(tables_landed, 16)
            for j in range(GD):
                g = m0 + j
                slot = g % SLOTS
                sp.wait_ge(hi_ready, g - SLOTS + 1)
                sp.wait_ge(lo_ready, g - SLOTS + 1)
                for at, lo, hi in ((KI2, ki_col, wi_col), (KI2 + 64, ki_col, wi_col),
                                   (LORA, lora_col, lora_col + 192), (WI, wi_col, rkv_col)):
                    sp.dma_start(raw[:, slot, :, at:at + hi - lo], in_rows(j * KT, lo, hi))\
                        .then_inc(raw_landed[slot], 16)
            sp.wait_ge(x_added, DC)
            sp.dma_start(lora_w[0:64, :], a["rwkv_w2"]).then_inc(lora_landed, 16)
            sp.dma_start(lora_w[64:P, :], a["rwkv_a2"]).then_inc(lora_landed, 16)
            sp.dma_start(lora_g[0:64, :], a["rwkv_g2"]).then_inc(lora_landed, 16)
            for c in range(1, NCH):
                for j in range(GD):
                    load_group(sp, in_rows(j * KT, in_col[c], in_col[c] + COLS), m0 + c * GD, 0, 0, j)

        def out_load(sp, g0, g1):
            for g in range(g0, g1):
                c, j = g // GD, g % GD
                load_group(sp, rows(a["w_out"], j * KT)[:, :, c * COLS:(c + 1) * COLS], w0_out, 0, 0, g)

        def project_channels(ps, cts, base, n, per, j, k0, first, last):
            slot = (base + j) % SLOTS
            for i, ct in enumerate(cts):
                for t in range(KT):
                    for p, (w, h) in enumerate(((whi, xh), (wlo, xh), (whi, xl))):
                        mm = nc.tensor.matmul(ps[:, i * S:(i + 1) * S], w[:, slot, t, ct * P:(ct + 1) * P],
                                              h[:, k0 + t, :], start=(first and t == 0 and p == 0 and i % 2 == 0),
                                              stop=(last and t == KT - 1 and p == 2), skip_group_check=True)
            return mm

        def project_small_tokens(ps, at, step, col, width, base, j, k0, first, last):
            slot = (base + j) % SLOTS
            for t in range(KT):
                for tb in range(TB):
                    tok = slice(tb * P, tb * P + P)
                    for p, (h, w) in enumerate(((xh, whi), (xh, wlo), (xl, whi))):
                        mm = nc.tensor.matmul(ps[:, at + tb * step:at + tb * step + width], h[:, k0 + t, tok],
                                              w[:, slot, t, col:col + width],
                                              start=(first and t == 0 and p == 0 and tb == 0),
                                              stop=(last and t == KT - 1 and p == 2), skip_group_check=True)
            return mm

        def win_small():
            for j in range(GD):
                if j % 2 == 0:
                    nc.tensor.wait_ge(xl_ready, 4 + j // 2 + 1)
                wait_group(m0, 0, 0, j)
                project_small_tokens(pA, 2 * S, IDX_HEADS, WI, IDX_HEADS, m0, j, j * KT, j == 0, j == GD - 1)
                slot = (m0 + j) % SLOTS
                for t in range(KT):
                    for p, (w, h) in enumerate(((whi, xh), (wlo, xh), (whi, xl))):
                        nc.tensor.matmul(pA[0:64, 3 * S:4 * S], w[:, slot, t, LORA + P:LORA + 192],
                                         h[:, j * KT + t, :], start=False,
                                         stop=(j == GD - 1 and t == KT - 1 and p == 2), skip_group_check=True)
                project_channels(pA, (0, 1), m0, 0, 0, j, j * KT, j == 0, j == GD - 1).then_inc(group_used, 1)

        def win_groups(g0, g1):
            for g in range(g0, g1):
                c, j = g // GD, g % GD
                base = m0 + c * GD
                if c >= 2 and j == 0:
                    nc.tensor.wait_ge(in_read, c - 1)
                wait_group(base, 0, 0, j)
                if c == 7:
                    project_small_tokens(pB, 2 * S, S, 2 * P, 2 * P, base, j, j * KT, j == 0, j == GD - 1)
                    mm = project_channels(pB, (0, 1), base, 0, 0, j, j * KT, j == 0, j == GD - 1)
                else:
                    mm = project_channels((pA, pB)[c % 2], range(4), base, 0, 0, j, j * KT,
                                          j == 0, j == GD - 1)
                mm.then_inc(group_used, 1)

        def tiles(ps):
            return ps[:, :].rearrange("p (t s) -> p t s", s=S)

        def in_out(c):
            nc.scalar.wait_ge(group_used, m0 + (c + 1) * GD)
            ps = (pA, pB)[c % 2]
            if c == 0:
                nc.scalar.copy(qi[:, 4, :], pA[:, 0:S])
                nc.scalar.copy(lora[:, 0, :], pA[:, S:2 * S])
                nc.scalar.copy(lora[0:64, 1, :], pA[0:64, 3 * S:4 * S])
                last = nc.scalar.activation(widx[:, :, :], pA[:, 2 * S:2 * S + TB * IDX_HEADS]
                                            .rearrange("p (b h) -> p b h", b=TB), ACT.Copy, scale=IDX_SCALE)
            elif c < 7:
                half = 4 * ((c - 1) % 2)
                if c == 5:
                    full(nc.scalar, "bonus", 1)
                last = nc.scalar.copy((k, r, v)[(c - 1) // 2][:, half:half + 4, :], tiles(ps))
            elif c == 7:
                nc.scalar.copy(qk[:, 8:10, :], tiles(pB)[:, 0:2, :])
                last = nc.scalar.copy(vals[:, :, :], tiles(pB)[:, 2:4, :])
            elif c == 8:
                last = nc.scalar.copy(qi[:, 0:4, :], tiles(ps))
            else:
                last = nc.scalar.copy(qk[:, 4 * (c - 9):4 * (c - 8), :], tiles(ps))
            last.then_inc(in_read, 1)

        PAIRS = (pA, pB, pT, pM)
        early = [("z", 0), ("z", 1), ("za", 0), ("za", 1), ("kn", 0), ("kb", 0), ("kb", 1), ("bonus", 0), ("bonus", 1),
                 ("vt", 0), ("vt", 1), ("at", 0), ("at", 1)]
        by_turns = [("bx", i) for i in range(4)] + [("kx", i) for i in range(4)]
        by_turns += [("idx", 0), ("idx", 1), ("g", 0), ("g", 1), ("bt", 0), ("bt", 1), ("kt", 0), ("kt", 1),
                     ("idx", 2), ("idx", 3), ("akv", 0), ("akv", 1), ("m1", 0), ("m1", 1), ("m2", 0), ("m2", 1),
                     ("sa0", 0), ("sa0", 1), ("gt", 0), ("gt", 1)]
        late = [("qk", 0, 0), ("qk", 1, 1), ("ys", 0, 2), ("st", 0, 3), ("qk", 2, 0),
                ("sa", 1, 2), ("ys", 1, 3), ("st", 1, 2), ("pt", 0, 1), ("sa", 2, 3), ("ys", 2, 2), ("st", 2, 3),
                ("pv", 0, 0), ("sa", 3, 2), ("ys", 3, 3), ("pt", 1, 1), ("pt", 2, 0),
                ("mean", 0, 2), ("mean", 1, 3), ("pv", 1, 1), ("var", 0, 2), ("vb", 0, 3), ("vb", 1, 2)]
        number = {name: n for n, name in enumerate(early + by_turns + [(name, i) for name, i, _ in late])}
        pair = {name: 2 + n % 2 for n, name in enumerate(early)}
        pair.update({name: n % 4 for n, name in enumerate(by_turns)})
        pair.update({(name, i): p for name, i, p in late})
        before = {name: sum(pair[other] == pair[name] and number[other] < number[name] for other in number)
                  for name in number}

        def fill(name, i):
            if before[name, i]:
                nc.tensor.wait_ge(round_read[pair[name, i]], before[name, i])
            return PAIRS[pair[name, i]]

        def filled(mm):
            mm.then_inc(round_full, 1)

        def full(eng, name, i):
            eng.wait_ge(round_full, number[name, i] + 1)
            return PAIRS[pair[name, i]]

        def read(ins, name, i):
            ins.then_inc(round_read[pair[name, i]], 1)

        def stored(eng, name, i):
            eng.wait_ge(round_read[pair[name, i]], before[name, i] + 1)

        steps = {name: sem("done_" + name) for name in (
            "qi_roped", "q_roped", "score0_7", "max0", "max1", "exp0", "exp1", "prob0", "prob1",
            "att_hi0", "att_hi1", "lora_wa", "lora_g", "tanh", "gsig", "v1", "kk_sq", "kk_root", "kk_inv",
            "lsum", "p", "pinv", "rk", "b_dec", "r_dec", "k_dec", "b_end", "k_end",
            "t_turned", "tt_zero", "sa_first", "y_intra1", "y_intra2", "y_intra3", "y_sq", "gn_root", "gn_inv",
            "y_gated0", "y_gated1", "mix_hi0", "mix_hi1", "mix_lo0", "mix_lo1")}
        vector_step = sem("vector_step")
        count = {}

        def done(ins, name):
            if name in steps:
                ins.then_inc(steps[name], 1)
            else:
                count[name] = len(count) + 1
                ins.then_inc(vector_step, 1)

        def need(eng, name):
            eng.wait_ge(steps[name], 1)

        def after(name):
            if name in steps:
                nc.vector.wait_ge(steps[name], 1)
            else:
                nc.vector.wait_ge(vector_step, count[name])

        V, A, T = nc.vector, nc.scalar, nc.tensor

        def tt(out, a0, a1, op):
            return V.tensor_tensor(out, a0, a1, op)

        def vdone(ins, name):
            done(ins, name)
            after(name)

        def vread(ins, name, i):
            read(ins, name, i)
            stored(nc.vector, name, i)

        def adone(ins, name):
            done(ins, name)
            nc.scalar.wait_ge(steps[name], 1)

        def aread(ins, name, i):
            read(ins, name, i)
            stored(nc.scalar, name, i)

        def head_rows(h):
            return slice(64 * (h % 2), 64 * (h % 2) + 64)

        def rope(arr, swap_buf, cosv, sinv, rows_, nt, mask, tag):
            vdone(V.stream_shuffle(swap_buf, arr, mask), tag + "_swapped")
            cb = cosv.unsqueeze(1).to_broadcast([rows_, nt, S])
            sb_ = sinv.unsqueeze(1).to_broadcast([rows_, nt, S])
            vdone(tt(swap_buf, swap_buf, sb_, ALU.mult), tag + "_sin")
            vdone(tt(arr, arr, cb, ALU.mult), tag + "_cos")
            vdone(tt(arr, arr, swap_buf, ALU.add), tag + "_roped")

        def scores_dve(tb):
            nk = (tb + 1) * P
            sc = score[:, tb, 0:nk]
            for i in range(2):
                stored(V, "idx", 2 * tb + i)
            for h in range(IDX_HEADS):
                src = relu[tb][:, 4 * (h // 4) + 2 * (h % 2) + (h % 4) // 2, 0:nk]
                if h == 0:
                    step = V.tensor_scalar(sc, src, widx[:, tb, 0:1], None, ALU.mult)
                else:
                    step = V.scalar_tensor_tensor(sc, src, widx[:, tb, h:h + 1], sc, ALU.mult, ALU.add)
                vdone(step, f"score{tb}_{h}")
            vdone(V.memset(score[0:64, tb, nk - 64:nk], HIDDEN), f"hidden{tb}")
            for i in range(TOPK // 8):
                vdone(V.max(top8[:, :], sc), f"top{tb}_{i}")
                vdone(V.match_replace(sc, top8[:, :], sc, TAKEN), f"taken{tb}_{i}")
            vdone(V.tensor_scalar(sc, sc, TAKEN, OFF, ALU.not_equal, ALU.mult), f"bias{tb}")

        def logits_dve(tb):
            nk = (tb + 1) * P
            hs = AH // (1 + tb)
            for i in range(1 + tb):
                ps = full(V, "qk", tb + i)
                vread(V.scalar_tensor_tensor(att[tb][:, i * hs:(i + 1) * hs, 0:nk],
                                             ps[:, 0:hs * nk].rearrange("p (h k) -> p h k", k=nk), ATT_SCALE,
                                             score[:, tb, 0:nk].unsqueeze(1).to_broadcast([P, hs, nk]),
                                             ALU.mult, ALU.add), "qk", tb + i)
            vdone(V.tensor_reduce(top[tb][:, 0:AH], att[tb][:, :, 0:nk], AX.X, ALU.max, negate=True), f"max{tb}")

        def probabilities_dve(tb):
            nk = (tb + 1) * P
            need(V, f"exp{tb}")
            vdone(V.reciprocal(top[tb][:, 2 * AH:3 * AH], top[tb][:, AH:2 * AH]), f"recip{tb}")
            vdone(tt(att[tb][:, :, 0:nk], att[tb][:, :, 0:nk],
                     top[tb][:, 2 * AH:3 * AH].unsqueeze(2).to_broadcast([P, AH, nk]), ALU.mult), f"prob{tb}")

        def attended_lo(tb):
            need(V, f"att_hi{tb}")
            ps = PAIRS[pair["pv", tb]]
            vread(tt(xl[:, 0:AH, tb * P:tb * P + P], ps[:, :].rearrange("p (h q) -> p h q", q=P),
                     xh[:, 0:AH, tb * P:tb * P + P].bitcast(F32), ALU.subtract), "pv", tb)

        def index_act(tb):
            nk = (tb + 1) * P
            for i in range(2):
                ps = full(A, "idx", 2 * tb + i)
                if tb:
                    need(A, "q_roped")
                aread(A.activation(relu[tb][:, 4 * i:4 * i + 4, 0:nk], tiles(ps)[:, :, 0:nk], ACT.Relu),
                      "idx", 2 * tb + i)

        def exponentials_act(tb):
            nk = (tb + 1) * P
            need(A, f"max{tb}")
            for h in range(AH):
                last = A.activation(att[tb][:, h, 0:nk], att[tb][:, h, 0:nk], ACT.Exp, bias=top[tb][:, h:h + 1],
                                    accum_out=top[tb][:, AH + h:AH + h + 1])
            adone(last, f"exp{tb}")

        def turned_probabilities_act(tb):
            for i in range(1 + tb):
                ps = full(A, "pt", tb + i)
                if tb and i == 0:
                    full(A, "pv", 0)
                aread(A.copy(prob_t[:, i, :, :], ps[:, :].rearrange("p (h q) -> p h q", q=P)), "pt", tb + i)

        def attended_hi(tb):
            ps = full(A, "pv", tb)
            adone(A.copy(xh[:, 0:AH, tb * P:tb * P + P], ps[:, :].rearrange("p (h q) -> p h q", q=P)),
                  f"att_hi{tb}")

        def index_pe(tb):
            nk = (tb + 1) * P
            tok = slice(tb * P, tb * P + P)
            for i in range(2):
                ps = fill("idx", 2 * tb + i)
                for m in range(4):
                    h = 4 * i + m
                    at = (2 * (h % 2) + (h % 4) // 2) * S
                    mm = T.matmul(ps[:, at:at + nk], qi[head_rows(h), h // 2, tok], qi[head_rows(h), 4, 0:nk],
                                  start=True, stop=True)
                filled(mm)

        def logits_pe(tb, i):
            nk = (tb + 1) * P
            hs = AH // (1 + tb)
            ps = fill("qk", tb + i)
            for m in range(hs):
                h = i * hs + m
                mm = T.matmul(ps[:, m * nk:(m + 1) * nk], qk[:, h, tb * P:tb * P + P], qk[:, 8 + h // 4, 0:nk],
                              start=True, stop=True)
            filled(mm)

        def turn_probabilities_pe(tb):
            need(T, f"prob{tb}")
            for i in range(1 + tb):
                ps = fill("pt", tb + i)
                for h in range(AH):
                    mm = T.transpose(ps[:, h * P:(h + 1) * P], att[tb][:, h, i * P:(i + 1) * P], ident)
                filled(mm)

        def attend_pe(tb):
            ps = fill("pv", tb)
            for i in range(1 + tb):
                stored(T, "pt", tb + i)
            for gr in range(2):
                for i in range(1 + tb):
                    mm = T.matmul(ps[:, gr * COLS:(gr + 1) * COLS], vals[:, i, gr * P:(gr + 1) * P],
                                  prob_t[:, i, 4 * gr:4 * gr + 4, :].rearrange("p h q -> p (h q)"),
                                  start=(i == 0), stop=(i == tb))
            filled(mm)

        def col(name, t):
            c = 3 * KD + NT * _CHANNELS.index("rwkv_" + name) + t
            return pcol[:, c:c + 1]

        def cols(name):
            c = 3 * KD + NT * _CHANNELS.index("rwkv_" + name)
            return pcol[:, c:c + NT]

        def chunks(arr):
            return arr[:, :, :].rearrange("p t (c s) -> p (t c) s", s=C)

        def lerp(arr, t0, n, tag, mus, rows_=P):
            part = arr[0:rows_, t0:t0 + n, :]
            diff = temp[0:rows_, 0:n, :]
            tt(diff[:, :, 1:S], part[:, :, 0:S - 1], part[:, :, 1:S], ALU.subtract)
            vdone(V.tensor_scalar(diff[:, :, 0:1], part[:, :, 0:1], -1.0, None, ALU.mult), tag + "_d")
            for t in range(n):
                last = V.scalar_tensor_tensor(part[:, t, :], diff[:, t, :], mus(t0 + t), part[:, t, :],
                                              ALU.mult, ALU.add)
            vdone(last, tag)

        def win_dve():
            def splits(g0, g1):
                for g in range(g0, g1):
                    split_lo(m0, 0, 0, g, SMALL if g < GD else COLS)

            splits(SLOTS, 13)
            V.wait_ge(in_read, 1)
            lerp(lora, 0, 1, "lora_wa", lambda t: pcol2[:, 0:1])
            lerp(lora, 1, 1, "lora_g", lambda t: pcol2[0:64, 1:2], 64)
            splits(13, 21)
            V.wait_ge(in_read, 2)
            lerp(k, 0, 4, "k0", lambda t: col("mu_k", t))
            splits(21, 25)
            V.wait_ge(tables_landed, 16)
            for i in range(2):
                stored(V, "z", i)
            for t in range(NT):
                last = V.tensor_tensor_scan(lsum[:, t, :], keep, sw[:, t, :], 0.0, ALU.mult, ALU.add)
            vdone(last, "lsum")
            splits(25, 29)
            V.wait_ge(in_read, 3)
            lerp(k, 4, 4, "k1", lambda t: col("mu_k", t))
            splits(29, 31)
            for t in range(NT):
                last = V.tensor_scalar(kk[:, t, :], k[:, t, :], col("k_k", t), None, ALU.mult)
            vdone(last, "kk_raw")
            splits(31, 32)
            vdone(tt(ksq[:, :, :], kk[:, :, :], kk[:, :, :], ALU.mult), "kk_sq")
            splits(32, 37)
            V.wait_ge(in_read, 4)
            lerp(r, 0, 4, "r0", lambda t: col("mu_r", t))
            splits(37, 39)
            ps = full(V, "kn", 0)
            vread(V.tensor_scalar(hstat[0:RH, 0, :], ps[0:RH, 0:S], 1e-24, None, ALU.max), "kn", 0)
            splits(39, 40)
            vdone(V.tensor_scalar(ka1[:, :], cols("k_a"), -1.0, 1.0, ALU.mult, ALU.add), "ka1")
            for i in range(2):
                stored(V, "za", i)
            for t in range(NT):
                last = V.tensor_scalar(ksq[:, t, :], iclr[:, t, :], col("k_a", t), ka1[:, t:t + 1],
                                       ALU.mult, ALU.add)
            vdone(last, "kmul")
            splits(40, 42)
            need(V, "kk_root")
            vdone(V.reciprocal(hstat[0:RH, 2, :], hstat[0:RH, 1, :]), "kk_inv")
            vdone(tt(k[:, :, :], k[:, :, :], ksq[:, :, :], ALU.mult), "k_mod")
            splits(42, 45)
            V.wait_ge(in_read, 5)
            lerp(r, 4, 4, "r1", lambda t: col("mu_r", t))
            splits(45, 47)
            for t in range(NT):
                last = V.scalar_tensor_tensor(ksq[:, t, :], r[:, t, :], col("r_k", t), k[:, t, :],
                                              ALU.mult, ALU.mult)
            vdone(last, "rk")
            splits(47, 49)
            for i in range(2):
                ps = full(V, "kb", i)
                vread(tt(kk[:, 4 * i:4 * i + 4, :], kk[:, 4 * i:4 * i + 4, :], tiles(ps), ALU.mult), "kb", i)
            splits(49, 50)
            vdone(tt(iclr[:, :, :], iclr[:, :, :], kk[:, :, :], ALU.mult), "b")
            splits(50, 51)
            need(V, "p")
            a_dec, r_dec = chunks(kk), chunks(r)
            tt(a_dec[:, :, 1:C], a_dec[:, :, 1:C], chunks(pdec)[:, :, 0:C - 1], ALU.mult).then_inc(a_rest, 1)
            V.wait_ge(a_rest, 1)
            vdone(V.tensor_scalar(kk[:, :, :], kk[:, :, :], -1.0, None, ALU.mult), "a_dec")
            splits(51, 53)
            V.wait_ge(in_read, 6)
            lerp(v, 0, 4, "v0", lambda t: col("mu_v", t))
            splits(53, 55)
            vdone(tt(r_dec, r_dec, chunks(pdec), ALU.mult), "r_dec")
            splits(55, 57)
            vdone(V.tensor_copy(pend[:, :, :], chunks(pdec)[:, :, C - 1:C]), "pend")
            need(V, "pinv")
            vdone(tt(iclr[:, :, :], iclr[:, :, :], pinv[:, :, :], ALU.mult), "b_dec")
            splits(57, 59)
            vdone(tt(k[:, :, :], k[:, :, :], pinv[:, :, :], ALU.mult), "k_dec")
            splits(59, 61)
            V.wait_ge(in_read, 7)
            lerp(v, 4, 4, "v1", lambda t: col("mu_v", t))
            splits(61, 64)
            for i in range(2):
                ps = full(V, "bonus", i)
                vread(tt(bonus[:, 4 * i:4 * i + 4, :], v[:, 4 * i:4 * i + 4, :], tiles(ps), ALU.mult), "bonus", i)
            splits(64, 69)
            V.wait_ge(in_read, 8)
            rope_heads(qk[0:32, 8:10, :], temp[0:32, 0:2, :], "k")
            splits(69, 77)
            V.wait_ge(in_read, 9)
            rope(qi[:, :, :], temp[:, 0:5, :], cos_i, sin_i, P, 5, [8 + i for i in range(8)] + list(range(8))
                 + list(range(16, 32)), "qi")
            splits(77, NCH * GD)

        def rope_heads(arr, swap_buf, tag):
            rope(arr, swap_buf, cos_q, sin_q, 32, arr.shape[1], [16 + i for i in range(16)] + list(range(16)), tag)

        def win_act():
            def splits(g0, g1):
                for g in range(g0, g1):
                    split_hi(m0, 0, 0, g, SMALL if g < GD else COLS)
                    if g > GD and g % GD == SLOTS - 1:
                        in_out(g // GD - 1)

            def sigmoids(name, dst, bias, i):
                ps = full(A, name, i)
                for t in range(4):
                    last = A.activation(dst[:, 4 * i + t, :], tiles(ps)[:, t, :], ACT.Sigmoid,
                                        bias=col(bias, 4 * i + t))
                aread(last, name, i)

            splits(SLOTS, 15)
            need(A, "lora_wa")
            adone(A.activation(lora[0:64, 0, :], lora[0:64, 0, :], ACT.Tanh), "tanh")
            need(A, "lora_g")
            adone(A.activation(lora[0:64, 1, :], lora[0:64, 1, :], ACT.Sigmoid), "gsig")
            splits(15, 22)
            sigmoids("z", sw, "w0", 0)
            splits(22, 23)
            sigmoids("z", sw, "w0", 1)
            splits(23, 30)
            sigmoids("za", iclr, "a0", 0)
            splits(30, 31)
            sigmoids("za", iclr, "a0", 1)
            splits(31, 33)
            need(A, "lsum")
            adone(A.activation(pdec[:, :, :], lsum[:, :, :], ACT.Exp, scale=-DECAY), "p")
            splits(33, 35)
            adone(A.activation(pinv[:, :, :], lsum[:, :, :], ACT.Exp, scale=DECAY), "pinv")
            splits(35, 40)
            stored(A, "kn", 0)
            adone(A.activation(hstat[0:RH, 1, :], hstat[0:RH, 0, :], ACT.Sqrt), "kk_root")
            splits(40, 70)
            for i in range(2):
                copy_tokens("vt", v_tok, i)
            splits(70, 78)
            for i in range(2):
                copy_tokens("at", a_tok, i)
            splits(78, NCH * GD)
            in_out(NCH - 1)

        def copy_tokens(name, dst, i):
            ps = full(A, name, i)
            aread(A.copy(dst[:, i, :], ps[:, :]), name, i)

        def rwkv_systems():
            for name, dst in (("bx", bx), ("kx", kx)):
                for i in range(4):
                    ps = full(V, name, i)
                    vread(tt(dst[:, 8 * i:8 * i + 8, :, :].rearrange("p j a t -> p j (a t)"),
                            ps[:, :].rearrange("p (j a) -> p j a", j=8),
                            mask2.unsqueeze(1).to_broadcast([P, 8, 2 * C]), ALU.mult), name, i)
            pe_ = pend[:, :, :].to_broadcast([P, NT * NCHUNK, C])
            vdone(tt(chunks(iclr), chunks(iclr), pe_, ALU.mult), "b_end")
            vdone(tt(chunks(k), chunks(k), pe_, ALU.mult), "k_end")
            rope_heads(qk[0:32, 0:8, :], turned[0:32, :, :], "q")

        def rwkv_dve():
            stored(V, "g", 1)
            vdone(V.memset(tinv[:, :], 0.0), "t_zero")
            vdone(V.memset(tinv[:, 0:1024:33], 1.0), "t_one")
            V.wait_ge(sys_landed, 16)
            tv = tinv[:, :].rearrange("p (t s) -> p t s", s=32)
            nv = nsys[:, :].rearrange("p (s t) -> p s t", t=32)
            for q in range(31):
                if q:
                    V.wait_ge(substituted, q)
                shape = [P, 31 - q, q + 1]
                tmp = subst[:, 0:(31 - q) * (q + 1)].rearrange("p (t s) -> p t s", s=q + 1)
                tt(tmp, nv[:, q, q + 1:32].unsqueeze(2).to_broadcast(shape),
                   tv[:, q, 0:q + 1].unsqueeze(1).to_broadcast(shape), ALU.mult).then_inc(multiplied, 1)
                V.wait_ge(multiplied, q + 1)
                tt(tv[:, q + 1:32, 0:q + 1], tv[:, q + 1:32, 0:q + 1], tmp, ALU.add).then_inc(substituted, 1)
            V.wait_ge(substituted, 31)
            stored(V, "kt", 1)
            vdone(V.memset(tt_all[:, :, :], 0.0), "tt_zero")
            vdone(V.tensor_copy(subst[:, :].rearrange("p (s t) -> p s t", t=32),
                               tv.rearrange("p t s -> p s t")), "t_turned")
            scores_dve(0)
            scores_dve(1)
            for i in range(2):
                stored(V, "sa0", i)
            for c in range(NCHUNK):
                half, blk = c % 2, c // 2
                hp = slice(64 * half, 64 * half + 64)
                if c:
                    ps = full(V, "sa", c)
                    vread(tt(sa[hp, :], sa0[hp, blk, :], ps[hp, :], ALU.add), "sa", c)
                else:
                    vdone(V.tensor_copy(sa[hp, :], sa0[hp, 0, :]), "sa_first")
                    logits_dve(0)
                if c < NCHUNK - 1:
                    if c:
                        stored(V, "st", c - 1)
                        vdone(tt(sdec[:, :, :], state[:, :, :], pend[:, c:32:4, :].to_broadcast([P, NT, C]),
                                ALU.mult), f"sdec{c}")
                    ps = full(V, "st", c)
                    s3 = ps[:, 0:COLS].rearrange("p (t v) -> p t v", v=C)
                    if c:
                        step = tt(state[:, :, :], sdec[:, :, :], s3, ALU.add)
                    else:
                        step = V.tensor_copy(state[:, :, :], s3)
                    vread(step, "st", c)
                if c:
                    need(V, f"y_intra{c}")
                    ps = PAIRS[pair["ys", c]]
                    yc = y[:, :, c * C:(c + 1) * C]
                    vread(tt(yc, yc, ps[:, 0:COLS].rearrange("p (t s) -> p t s", s=C), ALU.add), "ys", c)
                if c == 0:
                    logits_dve(1)
                elif c == 1:
                    probabilities_dve(0)
                elif c == 2:
                    probabilities_dve(1)
                else:
                    attended_lo(0)
            for i in range(2):
                ps = full(V, "mean", i)
                yi = y[:, 4 * i:4 * i + 4, :]
                vread(V.scalar_tensor_tensor(yi, tiles(ps), -1.0 / C, yi, ALU.mult, ALU.add), "mean", i)
            for i in range(2):
                stored(V, "mean", i)
            vdone(tt(ysq[:, :, :], y[:, :, :], y[:, :, :], ALU.mult), "y_sq")
            attended_lo(1)
            for g in range(2):
                split_lo(w0_out, 0, 0, g)
            ps = full(V, "var", 0)
            vread(V.tensor_scalar(hstat[0:RH, 0, :], ps[0:RH, 0:S], 1.0 / C, GN_EPS, ALU.mult, ALU.add), "var", 0)
            need(V, "gn_root")
            vdone(V.reciprocal(hstat[0:RH, 2, :], hstat[0:RH, 1, :]), "gn_inv")
            split_lo(w0_out, 0, 0, 2)
            for i in range(2):
                stored(V, "bonus", i)
                stored(V, "g", i)
            for i in range(2):
                half = slice(4 * i, 4 * i + 4)
                ps = full(V, "vb", i)
                vread(tt(y[:, half, :], y[:, half, :], tiles(ps), ALU.mult), "vb", i)
                for t in range(4 * i, 4 * i + 4):
                    last = V.tensor_scalar(y[:, t, :], y[:, t, :], col("gn_gain", t), col("gn_bias", t),
                                           ALU.mult, ALU.add)
                vdone(last, f"y_affine{i}")
                vdone(tt(y[:, half, :], y[:, half, :], bonus[:, half, :], ALU.add), f"y_bonus{i}")
                vdone(tt(y[:, half, :], y[:, half, :], gate[:, half, :], ALU.mult), f"y_gated{i}")
                if i == 0:
                    split_lo(w0_out, 0, 0, 3)
            for i in range(2):
                half = slice(4 * i, 4 * i + 4)
                need(V, f"mix_hi{i}")
                vdone(tt(xl[:, NT + 4 * i:NT + 4 * i + 4, :], y[:, half, :],
                         xh[:, NT + 4 * i:NT + 4 * i + 4, :].bitcast(F32), ALU.subtract), f"mix_lo{i}")

        def systems_act():
            index_act(0)
            for i in range(2):
                ps = full(A, "g", i)
                aread(A.copy(gate[:, 4 * i:4 * i + 4, :], tiles(ps)), "g", i)
            for name, dst in (("bt", b_tok), ("kt", k_tok)):
                for i in range(2):
                    copy_tokens(name, dst, i)
            index_act(1)
            for i in range(2):
                copy_tokens("akv", akv, i)

        def rwkv_act():
            for i in range(2):
                ps = full(A, "m1", i)
                rows_ = slice(64 * i + 32, 64 * i + 64)
                aread(A.copy(xm[rows_, :, :], ps[rows_, :].rearrange("p (j s) -> p j s", s=32)), "m1", i)
            for i in range(2):
                ps = full(A, "m2", i)
                rows_ = slice(64 * i, 64 * i + 32)
                aread(A.copy(tt_all[rows_, :, 32:64], ps[rows_, :].rearrange("p (j s) -> p j s", s=32)), "m2", i)
            need(A, "score0_7")
            for name, dst in (("sa0", sa0), ("gt", gt)):
                for i in range(2):
                    copy_tokens(name, dst, i)
            for c in range(NCHUNK):
                ps = full(A, "ys", c)
                step = A.copy(y[:, :, c * C:(c + 1) * C],
                              ps[:, COLS:2 * COLS].rearrange("p (t s) -> p t s", s=C))
                if c:
                    adone(step, f"y_intra{c}")
                else:
                    aread(step, "ys", 0)
                if c == 0:
                    exponentials_act(0)
                elif c == 1:
                    turned_probabilities_act(0)
                elif c == 2:
                    exponentials_act(1)
                    attended_hi(0)
                else:
                    turned_probabilities_act(1)
                    attended_hi(1)
            for g in range(2):
                split_hi(w0_out, 0, 0, g)
            stored(A, "var", 0)
            adone(A.activation(hstat[0:RH, 1, :], hstat[0:RH, 0, :], ACT.Sqrt), "gn_root")
            for g in range(2, SLOTS):
                split_hi(w0_out, 0, 0, g)
            for i in range(2):
                need(A, f"y_gated{i}")
                adone(A.copy(xh[:, NT + 4 * i:NT + 4 * i + 4, :], y[:, 4 * i:4 * i + 4, :]), f"mix_hi{i}")

        def channel_rounds(name, lhs, rhs, width=S):
            for i in range(2):
                ps = fill(name, i)
                for t in range(4):
                    mm = T.matmul(ps[:, t * S:(t + 1) * S], lhs(4 * i + t), rhs, start=True, stop=True)
                filled(mm)

        def spread(name):
            for i in range(2):
                ps = fill(name, i)
                for t in range(4):
                    mm = T.matmul(ps[:, t * S:(t + 1) * S], to_channels[0:RH, 4 * i + t, :], hstat[0:RH, 2, :],
                                  start=True, stop=True)
                filled(mm)

        def head_sums(name, src):
            ps = fill(name, 0)
            for t in range(NT):
                mm = T.matmul(ps[0:RH, 0:S], to_heads[:, t, :], src[:, t, :], start=(t == 0), stop=(t == NT - 1))
            filled(mm)

        def within_heads(name, src):
            for i in range(2):
                ps = fill(name, i)
                for b in range(2):
                    t = 4 * i + 2 * b
                    mm = T.matmul(ps[:, b * COLS:(b + 1) * COLS], same_head,
                                  src[:, t:t + 2, :].rearrange("p t s -> p (t s)"), start=True, stop=True)
                filled(mm)

        def turn_tokens(name, tile_of):
            for i in range(TB):
                ps = fill(name, i)
                for t in range(NT):
                    mm = T.transpose(ps[:, t * P:(t + 1) * P], tile_of(t, i), ident)
                filled(mm)

        def win_pe():
            win_small()
            win_groups(GD, 17)
            T.wait_ge(lora_landed, 48)
            need(T, "tanh")
            channel_rounds("z", lambda t: lora_w[0:64, t * P:(t + 1) * P], lora[0:64, 0, :])
            win_groups(17, 25)
            channel_rounds("za", lambda t: lora_w[64:P, t * P:(t + 1) * P], lora[64:P, 0, :])
            win_groups(25, 33)
            T.wait_ge(tables_landed, 16)
            need(T, "kk_sq")
            head_sums("kn", ksq)
            win_groups(33, 43)
            need(T, "kk_inv")
            spread("kb")
            win_groups(43, 49)
            need(T, "rk")
            within_heads("bonus", ksq)
            win_groups(49, 65)
            need(T, "v1")
            turn_tokens("vt", lambda t, i: v[:, t, i * P:(i + 1) * P])
            win_groups(65, 73)
            turn_tokens("at", lambda t, i: kk[:, t, i * P:(i + 1) * P])
            win_groups(73, NCH * GD)

        def systems_pe():
            T.wait_ge(in_read, NCH)
            for name, arr in (("bx", iclr), ("kx", k)):
                for i in range(4):
                    blk, par = i // 2, i % 2
                    hs = slice(64 * par, 64 * par + 64)
                    ps = fill(name, i)
                    for t in range(NT):
                        for half in range(2):
                            c = 2 * blk + half
                            mm = T.matmul(ps[64 * half:64 * half + 64, t * 2 * C:(t + 1) * 2 * C].rearrange(
                                              "p (a s) -> p a s", a=2),
                                          arr[hs, t, c * C:(c + 1) * C],
                                          ar[hs, :, t, c * C:(c + 1) * C],
                                          start=True, stop=True)
                    filled(mm)
            index_pe(0)
            channel_rounds("g", lambda t: lora_g[0:64, t * P:(t + 1) * P], lora[0:64, 1, :])
            need(T, "b_end")
            turn_tokens("bt", lambda t, i: iclr[:, t, i * P:(i + 1) * P])
            need(T, "k_end")
            turn_tokens("kt", lambda t, i: k[:, t, i * P:(i + 1) * P])
            index_pe(1)

        def rwkv_pe():
            for i in range(2):
                stored(T, "vt", i)
            for i in range(4):
                stored(T, "kx", i)

            def by_chunk(name, lhs, rhs, extra=None):
                for blk in range(2):
                    ps = fill(name, blk)
                    for jj in range(RH):
                        for half in range(2):
                            hs = slice(64 * half, 64 * half + 64)
                            mm = T.matmul(ps[hs, jj * C:(jj + 1) * C], lhs(hs, blk, jj), rhs(hs, blk, jj),
                                          start=True, stop=True)
                    filled(mm)

            def hcol(jj):
                h = 2 * (jj % NT) + jj // NT
                return slice(h * C, h * C + C)
            by_chunk("akv", lambda hs, b, jj: kx[hs, b * RH + jj, 0, :], lambda hs, b, jj: v_tok[hs, b, hcol(jj)])
            T.wait_ge(inv_landed, 16 * 6)
            for i in range(2):
                ps = fill("m1", i)
                lo, hi = slice(64 * i, 64 * i + 32), slice(64 * i + 32, 64 * i + 64)
                for j in range(2 * RH):
                    mm = T.matmul(ps[hi, j * 32:(j + 1) * 32], bx[lo, j, 0, 32:64], t_plain[lo, j, :],
                                  start=True, stop=True)
                filled(mm)
            for i in range(2):
                stored(T, "m1", i)
                ps = fill("m2", i)
                lo, hi = slice(64 * i, 64 * i + 32), slice(64 * i + 32, 64 * i + 64)
                for j in range(2 * RH):
                    mm = T.matmul(ps[lo, j * 32:(j + 1) * 32], xm[hi, j, :], tt_all[hi, j, 32:64],
                                  start=True, stop=True)
                filled(mm)
            for i in range(2):
                stored(T, "m2", i)
                stored(T, "akv", i)
                stored(T, "at", i)
            by_chunk("sa0", lambda hs, b, jj: tt_all[hs, b * RH + jj, :], lambda hs, b, jj: akv[hs, b, jj * C:(jj + 1) * C])
            for blk in range(2):
                ps = fill("gt", blk)
                for half in range(2):
                    hs = slice(64 * half, 64 * half + 64)
                    for jj in range(RH):
                        par, t = jj // NT, jj % NT
                        mm = T.matmul(ps[64 * par:64 * par + 64, half * COLS + t * C:half * COLS + (t + 1) * C],
                                      a_tok[hs, blk, hcol(jj)], tt_all[hs, blk * RH + jj, :], start=True, stop=True)
                filled(mm)
            for i in range(2):
                stored(T, "gt", i)
                stored(T, "bt", i)
                stored(T, "kt", i)
                stored(T, "sa0", i)
            need(T, "q_roped")
            logits_pe(0, 0)
            logits_pe(1, 0)
            for c in range(NCHUNK):
                half, blk = c % 2, c // 2
                hs = slice(64 * half, 64 * half + 64)
                if c:
                    stored(T, "st", c - 1)
                    ps = fill("sa", c)
                    for jj in range(RH):
                        par, t = jj // NT, jj % NT
                        ch = slice(64 * par, 64 * par + 64)
                        mm = T.matmul(ps[hs, jj * C:(jj + 1) * C],
                                      gt[ch, blk, half * COLS + t * C:half * COLS + (t + 1) * C], state[ch, t, :],
                                      start=True, stop=True)
                    filled(mm)
                ps = fill("ys", c)
                if c:
                    for jj in range(RH):
                        par, t = jj // NT, jj % NT
                        ch = slice(64 * par, 64 * par + 64)
                        T.matmul(ps[ch, t * C:(t + 1) * C], state[ch, t, :], ar[ch, 1, t, c * C:(c + 1) * C],
                                 start=True, stop=True)
                    stored(T, "sa", c)
                else:
                    need(T, "sa_first")
                for jj in range(RH):
                    par, t = jj // NT, jj % NT
                    ch = slice(64 * par, 64 * par + 64)
                    out_ = ps[ch, COLS + t * C:COLS + (t + 1) * C]
                    j = blk * RH + jj
                    T.matmul(out_, sa[hs, jj * C:(jj + 1) * C], bx[hs, j, 1, :], start=True, stop=False)
                    mm = T.matmul(out_, v_tok[hs, blk, hcol(jj)], kx[hs, j, 1, :], start=False, stop=True)
                filled(mm)
                if c < NCHUNK - 1:
                    ps = fill("st", c)
                    for jj in range(RH):
                        par, t = jj // NT, jj % NT
                        ch = slice(64 * par, 64 * par + 64)
                        out_ = ps[ch, t * C:(t + 1) * C]
                        T.matmul(out_, b_tok[hs, blk, hcol(jj)], sa[hs, jj * C:(jj + 1) * C], start=True, stop=False)
                        mm = T.matmul(out_, k_tok[hs, blk, hcol(jj)], v_tok[hs, blk, hcol(jj)], start=False, stop=True)
                    filled(mm)
                if c == 0:
                    logits_pe(1, 1)
                elif c == 1:
                    turn_probabilities_pe(0)
                elif c == 2:
                    attend_pe(0)
                else:
                    turn_probabilities_pe(1)
            for c in range(NCHUNK):
                stored(T, "ys", c)
            within_heads("mean", y)
            attend_pe(1)
            need(T, "y_sq")
            head_sums("var", ysq)
            need(T, "gn_inv")
            spread("vb")

        def mix_sp_dmas(eng):
            for i in range(4):
                stored(eng, "bx", i)
            for q in range(4):
                half = q % 2
                eng.dma_start(n_dram[q].rearrange("j s t -> s j t"),
                              bx[32 * q:32 * q + 32, :, 0, 32 * half:32 * half + 32]).then_inc(sys_stored, 16)
            eng.wait_ge(sys_stored, 64)
            eng.dma_start(nsys[:, :], n_dram.rearrange("q j s t -> (q j) (s t)")).then_inc(sys_landed, 16)
            need(eng, "t_turned")
            need(eng, "tt_zero")
            eng.dma_start(t_dram[0].rearrange("q j s t -> (q j) (s t)"), subst[:, :]).then_inc(inv_stored, 16)
            eng.dma_start(t_dram[1].rearrange("q j s t -> (q j) (s t)"), tinv[:, :]).then_inc(inv_stored, 16)
            eng.wait_ge(inv_stored, 32)
            for q in range(4):
                half = q % 2
                eng.dma_start(tt_all[32 * q:32 * q + 32, :, 32 * half:32 * half + 32],
                              t_dram[0, q].rearrange("j s t -> s j t")).then_inc(inv_landed, 16)
                if half == 0:
                    eng.dma_start(t_plain[32 * q:32 * q + 32, :, :],
                                  t_dram[1, q].rearrange("j t s -> t j s")).then_inc(inv_landed, 16)

        def out_pe():
            stored(T, "pt", 2)
            for i in range(TB):
                stored(T, "pv", i)
            for c in range(DC):
                if c >= 2:
                    T.wait_ge(x_added, DC + c - 1)
                for j in range(GD):
                    if c == 0 and j in (4, 6):
                        need(T, f"mix_lo{(j - 4) // 2}")
                    project_tokens((psA, psB)[c % 2], xh, xl, w0_out, 0, 0, c * GD + j, j * KT,
                                   j == 0, j == GD - 1)

        def out_act():
            for g in range(SLOTS, DC * GD):
                split_hi(w0_out, 0, 0, g)
                if g > GD and g % GD == 2 * SLOTS - 1:
                    squares_act(2, g // GD - 1)

        def out_dve():
            def add(c):
                V.wait_ge(group_used, w0_out + (c + 1) * GD)
                xc = x[:, :, c * COLS:(c + 1) * COLS]
                tt(xc, (psA, psB)[c % 2][:, :, :], xc, ALU.add).then_inc(x_added, 1)
            for g in range(SLOTS, DC * GD):
                split_lo(w0_out, 0, 0, g)
                if g > GD and g % GD == SLOTS - 1:
                    add(g // GD - 1)
            add(DC - 1)

        def mix_load_all(sp):
            mix_load(sp)
            mix_sp_dmas(sp)
            full(sp, "pt", 2)
            out_load(sp, 0, DC * GD)

        def mix_act():
            for j in range(SLOTS):
                split_hi(m0, 0, 0, j, SMALL)
            norm_act(1)
            norm_hi(1)
            win_act()
            systems_act()
            rwkv_act()
            out_act()

        def mix_dve():
            for j in range(SLOTS):
                split_lo(m0, 0, 0, j, SMALL)
            norm_dve(1)
            norm_lo(1)
            win_dve()
            rwkv_systems()
            rwkv_dve()
            out_dve()

        def mix_pe():
            turn_norm(1)
            win_pe()
            systems_pe()
            rwkv_pe()
            out_pe()

        added_before_down = [0, 2 * DC]

        ffn1, ffn2 = a["ffn1"], a["ffn2"]
        base2 = FFN_GROUPS + MIX_GROUPS

        block = ctx.enter_context(nc.Block())

        @block.sync
        def _(sp):
            xv = a["x"].rearrange("(b p) d -> p b d", p=P)
            for c in range(DC):
                sp.dma_start(x[:, :, c * COLS:(c + 1) * COLS], xv[:, :, c * COLS:(c + 1) * COLS])\
                    .then_inc(x_landed[c], 16)
            ffn_load(sp, 0, 0, *ffn1)
            mix_load_all(sp)
            ffn_load(sp, 1, base2, *ffn2)
            sp.wait_ge(group_used, base2 + FC * PER)
            sp.dma_start(fgain[:, :], a["final_norm"].rearrange("(o d) -> o d", o=1).to_broadcast([P, D]))\
                .then_inc(gain_landed, 16)
            ov = out.rearrange("(b p) d -> p b d", p=P)
            for n in range(2 * TB):
                tb, cols_ = n // 2, slice((n % 2) * HALF, (n % 2 + 1) * HALF)
                sp.wait_ge(out_ready, n + 1)
                sp.dma_start(ov[:, tb, cols_], xs[:, tb, cols_]).then_inc(out_stored, 16)
            sp.wait_ge(out_stored, 16 * 2 * TB)

        @block.scalar
        def _(act):
            act.dma_start(consts[:, 0:P], a["consts"][:, 0:P]).then_inc(const_landed, 16)
            n = 0
            for name in ("ffn1_norm", "mix_norm", "ffn2_norm"):
                act.dma_start(prow[n:n + KD, :], a[name].rearrange("(k p) -> k p", p=P)).then_inc(const_landed, 16)
                n += KD
            for name in _CHANNELS:
                act.dma_start(prow[n:n + NT, :], a[name].rearrange("(k p) -> k p", p=P)).then_inc(const_landed, 16)
                n += NT
            for row, col_, name in ((0, 0, "rwkv_mu_w"), (0, 64, "rwkv_mu_a"), (1, 0, "rwkv_mu_g"), (1, 64, "rwkv_mu_g")):
                act.dma_start(prow2[row:row + 1, col_:col_ + 64], a[name].rearrange("(o n) -> o n", o=1))\
                    .then_inc(const_landed, 16)
            norm_act(0)
            for j in range(2):
                split_hi(0, 0, PER, j)
            norm_hi(0)
            for j in range(2, SLOTS):
                split_hi(0, 0, PER, j)
            ffn_act(0, 0)
            mix_act()
            for j in range(SLOTS):
                split_hi(base2, 0, PER, j)
            norm_act(2)
            norm_hi(2)
            ffn_act(1, base2)
            norm_act(3)

        @block.vector
        def _(dve):
            dve.wait_ge(params_turned, 1)
            nc.vector.tensor_copy(pcol2[:, :], psM[:, P:P + 2])
            nc.vector.tensor_copy(pcol[:, :], psM[:, 0:P]).then_inc(params_ready, 1)
            norm_dve(0)
            for j in range(2):
                split_lo(0, 0, PER, j)
            norm_lo(0)
            for j in range(2, SLOTS):
                split_lo(0, 0, PER, j)
            ffn_dve(0, 0)
            mix_dve()
            for j in range(SLOTS):
                split_lo(base2, 0, PER, j)
            norm_dve(2)
            norm_lo(2)
            ffn_dve(1, base2)
            norm_dve(3)
            dve.wait_ge(gain_landed, 16)
            for n in range(2 * TB):
                tb, cols_ = n // 2, slice((n % 2) * HALF, (n % 2 + 1) * HALF)
                nc.vector.scalar_tensor_tensor(xs[:, tb, cols_], x[:, tb, cols_], ss[:, 4 + tb:5 + tb],
                                               fgain[:, cols_], ALU.mult, ALU.mult).then_inc(out_ready, 1)

        @block.tensor
        def _(pe):
            pe.wait_ge(const_landed, 16 * (8 + len(_CHANNELS)))
            nc.tensor.transpose(psM[:, 0:P], prow[:, :], ident)
            nc.tensor.transpose(psM[:, P:P + 2], prow2[:, :], ident[0:2, 0:2]).then_inc(params_turned, 1)
            turn_norm(0)
            ffn_pe(0, 0)
            mix_pe()
            turn_norm(2)
            ffn_pe(1, base2)


_CHANNELS = ["rwkv_mu_r", "rwkv_mu_k", "rwkv_mu_v", "rwkv_w0", "rwkv_a0", "rwkv_k_k", "rwkv_k_a", "rwkv_r_k",
             "rwkv_gn_gain", "rwkv_gn_bias"]


def launch(nc, args, out):
    a = {}
    for name, v in args.items():
        a[name] = v if name == "final_norm" else v[0]
    a["rwkv_r_k"] = a["rwkv_r_k"].rearrange("h n -> (h n)")
    for f in ("ffn1", "ffn2"):
        a[f] = (a[f + "_w_gate"], a[f + "_w_up"], a[f + "_w_down"])
    a["consts"] = nc.inline_tensor(constants(), "constants").ap()
    build(nc, a, out[0])


def kernel(**inputs):
    import numpy as _np
    import concourse.bacc as _bacc
    from concourse import mybir as _mybir
    from concourse.bass_utils import run_bass_kernel_spmd as _run

    nc = _bacc.Bacc("TRN2", target_bir_lowering=False, num_devices=1)
    arrays, args = {}, {}
    for name, v in inputs.items():
        v = _np.ascontiguousarray(v)
        arrays[f"in_{name}"] = v
        args[name] = nc.dram_tensor(f"in_{name}", v.shape, _mybir.dt.from_np(v.dtype), kind="ExternalInput").ap()
    out = nc.dram_tensor("out", (1, S, D), F32, kind="ExternalOutput").ap()
    launch(nc, args, out)
    r = _run(nc, [arrays], core_ids=[0])
    return r.results[0]["out"]
```
